# Optimizing a Trainium2 kernel written in Bass

```python
import jax
import jax.numpy as jnp
from jax import lax
import numpy as np

D_MODEL = 2048
BATCH = 1
SEQ = 256
DEPTH = 1

HEAD_DIM = 128
HEADS = 4
GROUP_W = HEADS * HEAD_DIM
D_MIX = 4 * GROUP_W
N_SOFTMAX_HEADS = 2 * HEADS

MLSTM_CHUNK = 64
MLSTM_CONV = 4
MOBA_BLOCK = 256
MOBA_TOPK = 3
MOBA_QC = 16
RET_CHUNK = 128
NSA_CMP_LEN = 32
NSA_CMP_STRIDE = 16
NSA_SEL_BLOCK = 64
NSA_SEL_TOPN = 4
NSA_WINDOW = 512
NSA_QC = 32
WIN_QBLOCK = 128
N_GROUPS = 4
EXPERTS_PER_GROUP = 8
N_EXPERTS = N_GROUPS * EXPERTS_PER_GROUP
TOP_K_IN_GROUP = 2
D_EXPERT = 512
MOE_BLOCK = 128

NORM_EPS = 1e-6
NEG = -1e30
BIG = 1e9

IN_LAYOUT = (
    ('m_q', GROUP_W), ('m_k', GROUP_W), ('m_v', GROUP_W), ('m_o', GROUP_W), ('m_i', HEADS), ('m_f', HEADS),
    ('b_q', GROUP_W), ('b_k', GROUP_W), ('b_v', GROUP_W),
    ('r_q', GROUP_W), ('r_k', GROUP_W), ('r_v', GROUP_W), ('r_g', GROUP_W),
    ('n_q', GROUP_W), ('n_kc', GROUP_W), ('n_vc', GROUP_W), ('n_ks', GROUP_W), ('n_vs', GROUP_W),
    ('n_kw', GROUP_W), ('n_vw', GROUP_W), ('n_g', 3 * HEADS),
)
D_IN = sum(w for _, w in IN_LAYOUT)

kernel_name = 'hybrid_mlstm_moba_retnet_nsa_hmoe'

def _rms(z, g):
    zf = z.astype(jnp.float32)
    zf = zf * lax.rsqrt(jnp.mean(zf * zf, axis=-1, keepdims=True) + NORM_EPS)
    return zf * g.astype(jnp.float32)

def to_heads(z):
    b, t, _ = z.shape
    return z.reshape(b, t, -1, HEAD_DIM).transpose(0, 2, 1, 3)

def from_heads(z):
    b, h, t, d = z.shape
    return z.transpose(0, 2, 1, 3).reshape(b, t, h * d)

def alibi_slopes():
    n = N_SOFTMAX_HEADS
    return jnp.exp2(-8.0 * jnp.arange(1, n + 1, dtype=jnp.float32) / n)

def causal_dwconv(x, w):
    k = w.shape[0]
    return lax.conv_general_dilated(
        x, w.astype(x.dtype)[:, None, :], window_strides=(1,), padding=((k - 1, 0),),
        dimension_numbers=('NWC', 'WIO', 'NWC'), feature_group_count=x.shape[-1])

def mlstm_mixer(q, k, v, o, ig, fg, conv_w, gate_b, out_g):
    f32 = jnp.float32
    qk = jax.nn.silu(causal_dwconv(jnp.concatenate([q, k], axis=-1), conv_w))
    q, k = jnp.split(qk, 2, axis=-1)
    q = to_heads(q).astype(f32) * HEAD_DIM ** -0.5
    k = to_heads(k).astype(f32)
    v = to_heads(v).astype(f32)
    i_pre = jnp.swapaxes((ig + gate_b[0]).astype(f32), 1, 2)
    log_f = jax.nn.log_sigmoid(jnp.swapaxes((fg + gate_b[1]).astype(f32), 1, 2))
    b, h, t, d = q.shape
    nc = t // MLSTM_CHUNK
    causal = jnp.tril(jnp.ones((MLSTM_CHUNK, MLSTM_CHUNK), dtype=bool))

    def chunked(z):
        return jnp.moveaxis(z.reshape(b, h, nc, MLSTM_CHUNK, *z.shape[3:]), 2, 0)

    def step(carry, inp):
        c_st, n_st, m_st = carry
        qc, kc, vc, ic, fc = inp
        a = jnp.cumsum(fc, axis=-1)
        log_d = jnp.where(causal, a[..., :, None] - a[..., None, :] + ic[..., None, :], NEG)
        m_inter = a + m_st[..., None]
        m_row = jnp.maximum(m_inter, jnp.max(log_d, axis=-1))
        s = jnp.einsum('bhjd,bhsd->bhjs', qc, kc) * jnp.exp(log_d - m_row[..., None])
        w_inter = jnp.exp(m_inter - m_row)
        num = (jnp.einsum('bhjs,bhse->bhje', s, vc)
               + w_inter[..., None] * jnp.einsum('bhjd,bhde->bhje', qc, c_st))
        den = jnp.sum(s, axis=-1) + w_inter * jnp.einsum('bhjd,bhd->bhj', qc, n_st)
        h_out = num / jnp.maximum(jnp.abs(den), jnp.exp(-m_row))[..., None]
        a_last = a[..., -1]
        w_log = a_last[..., None] - a + ic
        m_new = jnp.maximum(a_last + m_st, jnp.max(w_log, axis=-1))
        w = jnp.exp(w_log - m_new[..., None])
        decay = jnp.exp(a_last + m_st - m_new)
        c_st = decay[..., None, None] * c_st + jnp.einsum('bhs,bhsd,bhse->bhde', w, kc, vc)
        n_st = decay[..., None] * n_st + jnp.einsum('bhs,bhsd->bhd', w, kc)
        return (c_st, n_st, m_new), h_out

    carry0 = (jnp.zeros((b, h, d, d), f32), jnp.zeros((b, h, d), f32), jnp.zeros((b, h), f32))
    _, hs = lax.scan(step, carry0, (chunked(q), chunked(k), chunked(v), chunked(i_pre), chunked(log_f)))
    hs = jnp.moveaxis(hs, 0, 2).reshape(b, h, t, d)
    return from_heads(_rms(hs, out_g)) * jax.nn.sigmoid(o.astype(f32))

def moba_mixer(q, k, v, qk_g, slopes):
    f32 = jnp.float32
    q = _rms(to_heads(q), qk_g[0])
    k = _rms(to_heads(k), qk_g[1])
    v = to_heads(v).astype(f32)
    b, h, t, d = q.shape
    scale = d ** -0.5
    nb = -(-t // MOBA_BLOCK)
    tp = nb * MOBA_BLOCK
    padw = ((0, 0), (0, 0), (0, tp - t), (0, 0))
    q, k, v = jnp.pad(q, padw), jnp.pad(k, padw), jnp.pad(v, padw)
    kb = k.reshape(b, h, nb, MOBA_BLOCK, d)
    vb = v.reshape(b, h, nb, MOBA_BLOCK, d)
    qblk = jnp.arange(tp, dtype=jnp.int32) // MOBA_BLOCK
    blk = jnp.arange(nb, dtype=jnp.int32)
    gate = jnp.einsum('bhtd,bhnd->bhtn', q, jnp.mean(kb, axis=3))
    gate = jnp.where(blk[None, :] < qblk[:, None], gate, NEG)
    n_sel = min(MOBA_TOPK, nb)
    _, sel = lax.top_k(gate, n_sel)
    nq = tp // MOBA_QC
    q_ch = jnp.moveaxis(q.reshape(b, h, nq, MOBA_QC, d), 2, 0)
    sel_ch = jnp.moveaxis(sel.reshape(b, h, nq, MOBA_QC, n_sel), 2, 0)
    starts = jnp.arange(nq, dtype=jnp.int32) * MOBA_QC
    bi = jnp.arange(b)[:, None, None, None]
    hi = jnp.arange(h)[None, :, None, None]
    slope = slopes[None, :, None, None]
    offs = jnp.arange(MOBA_BLOCK, dtype=jnp.int32)

    def chunk_attn(args):
        qc, sc, start = args
        tq = start + jnp.arange(MOBA_QC, dtype=jnp.int32)
        own = start // MOBA_BLOCK
        k_own = lax.dynamic_index_in_dim(kb, own, axis=2, keepdims=False)
        v_own = lax.dynamic_index_in_dim(vb, own, axis=2, keepdims=False)
        dist_own = (tq[:, None] - (own * MOBA_BLOCK + offs)[None, :]).astype(f32)
        s_own = jnp.einsum('bhqd,bhkd->bhqk', qc, k_own) * scale - slope * dist_own
        s_own = jnp.where(dist_own >= 0, s_own, NEG)
        k_sel = kb[bi, hi, sc]
        v_sel = vb[bi, hi, sc]
        dist_sel = (tq[None, None, :, None, None] - (sc[..., None] * MOBA_BLOCK + offs)).astype(f32)
        s_sel = jnp.einsum('bhqd,bhqnkd->bhqnk', qc, k_sel) * scale - slope[..., None] * dist_sel
        s_sel = jnp.where((sc < own)[..., None], s_sel, NEG)
        s_all = jnp.concatenate([s_own, s_sel.reshape(b, h, MOBA_QC, n_sel * MOBA_BLOCK)], axis=-1)
        p = jax.nn.softmax(s_all, axis=-1)
        p_own = p[..., :MOBA_BLOCK]
        p_sel = p[..., MOBA_BLOCK:].reshape(b, h, MOBA_QC, n_sel, MOBA_BLOCK)
        return (jnp.einsum('bhqk,bhkd->bhqd', p_own, v_own)
                + jnp.einsum('bhqnk,bhqnkd->bhqd', p_sel, v_sel))

    out = lax.map(chunk_attn, (q_ch, sel_ch, starts))
    out = jnp.moveaxis(out, 0, 2).reshape(b, h, tp, d)[:, :, :t]
    return from_heads(out)

def retention_mixer(q, k, v, g, out_g):
    f32 = jnp.float32
    q = to_heads(q).astype(f32)
    k = to_heads(k).astype(f32) * HEAD_DIM ** -0.5
    v = to_heads(v).astype(f32)
    b, h, t, d = q.shape
    lg = jnp.log(1.0 - jnp.exp2(-5.0 - jnp.arange(h, dtype=f32)))
    cl = RET_CHUNK
    nc = t // cl
    qc = q.reshape(b, h, nc, cl, d)
    kc = k.reshape(b, h, nc, cl, d)
    vc = v.reshape(b, h, nc, cl, d)
    j = jnp.arange(cl, dtype=f32)
    diff = j[:, None] - j[None, :]
    decay_in = jnp.where(diff >= 0, jnp.exp(lg[:, None, None] * jnp.maximum(diff, 0.0)), 0.0)
    scores = jnp.einsum('bhcid,bhcjd->bhcij', qc, kc) * decay_in[None, :, None]
    o_intra = jnp.einsum('bhcij,bhcjd->bhcid', scores, vc)
    zeta = jnp.exp(lg[:, None] * (cl - 1 - j)[None, :])
    kv = jnp.einsum('bhcjd,hj,bhcje->bhcde', kc, zeta, vc)
    g_chunk = jnp.exp(lg * cl)[None, :, None, None]

    def step(r, kv_c):
        return g_chunk * r + kv_c, r

    _, r_prev = lax.scan(step, jnp.zeros((b, h, d, d), f32), jnp.moveaxis(kv, 2, 0))
    r_prev = jnp.moveaxis(r_prev, 0, 2)
    xi = jnp.exp(lg[:, None] * (j + 1.0)[None, :])
    o_cross = jnp.einsum('bhcid,bhcde->bhcie', qc, r_prev) * xi[None, :, None, :, None]
    o = (o_intra + o_cross).reshape(b, h, t, d)
    return from_heads(_rms(o, out_g)) * jax.nn.silu(g.astype(f32))

def nsa_mixer(q, kc, vc, ks, vs, kw, vw, gates, q_g, k_g, cmp_pos, cmp_w1, cmp_w2, slopes):
    f32 = jnp.float32
    q = _rms(to_heads(q), q_g)
    b, h, t, d = q.shape
    scale = d ** -0.5
    slope = slopes[None, :, None, None]
    pos = jnp.arange(t, dtype=jnp.int32)

    def compress(z, pe, w1, w2):
        nsub = t // NSA_CMP_STRIDE
        zs = z.reshape(b, h, nsub, NSA_CMP_STRIDE, d)
        blocks = jnp.concatenate([zs[:, :, :-1], zs[:, :, 1:]], axis=3) + pe
        hid = jax.nn.gelu(jnp.einsum('bhnf,fe->bhne', blocks.reshape(b, h, nsub - 1, NSA_CMP_LEN * d), w1))
        return jnp.einsum('bhne,ed->bhnd', hid, w2)

    k_cmp = _rms(compress(to_heads(kc).astype(f32), cmp_pos[0], cmp_w1[0], cmp_w2[0]), k_g[0])
    v_cmp = compress(to_heads(vc).astype(f32), cmp_pos[1], cmp_w1[1], cmp_w2[1])
    n_cmp = k_cmp.shape[2]
    cmp_end = jnp.arange(n_cmp, dtype=jnp.int32) * NSA_CMP_STRIDE + NSA_CMP_LEN - 1
    dist_c = (pos[:, None] - cmp_end[None, :]).astype(f32)
    ok_c = dist_c >= 0
    s_c = jnp.where(ok_c, jnp.einsum('bhtd,bhnd->bhtn', q, k_cmp) * scale - slope * dist_c, NEG)
    m_c = jnp.max(s_c, axis=-1, keepdims=True)
    e_c = jnp.where(ok_c, jnp.exp(s_c - m_c), 0.0)
    p_c = e_c / jnp.maximum(jnp.sum(e_c, axis=-1, keepdims=True), 1e-30)
    o_cmp = jnp.einsum('bhtn,bhnd->bhtd', p_c, v_cmp)

    n_sel = t // NSA_SEL_BLOCK
    ci = jnp.arange(n_cmp, dtype=jnp.int32)[:, None]
    sj = jnp.arange(n_sel, dtype=jnp.int32)[None, :]
    overlap = ((ci * NSA_CMP_STRIDE <= sj * NSA_SEL_BLOCK + NSA_SEL_BLOCK - 1)
               & (ci * NSA_CMP_STRIDE + NSA_CMP_LEN - 1 >= sj * NSA_SEL_BLOCK)).astype(f32)
    imp = jnp.einsum('bhtn,ns->bhts', p_c, overlap)
    cur = (pos // NSA_SEL_BLOCK)[:, None]
    imp = jnp.where(sj == cur, BIG, jnp.where(sj < cur, imp, NEG))
    n_top = min(NSA_SEL_TOPN, n_sel)
    _, sidx = lax.top_k(imp, n_top)
    ks_b = _rms(to_heads(ks), k_g[1]).reshape(b, h, n_sel, NSA_SEL_BLOCK, d)
    vs_b = to_heads(vs).astype(f32).reshape(b, h, n_sel, NSA_SEL_BLOCK, d)
    nq = t // NSA_QC
    q_ch = jnp.moveaxis(q.reshape(b, h, nq, NSA_QC, d), 2, 0)
    s_ch = jnp.moveaxis(sidx.reshape(b, h, nq, NSA_QC, n_top), 2, 0)
    starts = jnp.arange(nq, dtype=jnp.int32) * NSA_QC
    bi = jnp.arange(b)[:, None, None, None]
    hi = jnp.arange(h)[None, :, None, None]
    offs = jnp.arange(NSA_SEL_BLOCK, dtype=jnp.int32)

    def chunk_attn(args):
        qc, sc, start = args
        tq = start + jnp.arange(NSA_QC, dtype=jnp.int32)
        k_gth = ks_b[bi, hi, sc]
        v_gth = vs_b[bi, hi, sc]
        dist = (tq[None, None, :, None, None] - (sc[..., None] * NSA_SEL_BLOCK + offs)).astype(f32)
        s = jnp.einsum('bhqd,bhqnkd->bhqnk', qc, k_gth) * scale - slope[..., None] * dist
        s = jnp.where(dist >= 0, s, NEG).reshape(b, h, NSA_QC, n_top * NSA_SEL_BLOCK)
        p = jax.nn.softmax(s, axis=-1).reshape(b, h, NSA_QC, n_top, NSA_SEL_BLOCK)
        return jnp.einsum('bhqnk,bhqnkd->bhqd', p, v_gth)

    o_slc = lax.map(chunk_attn, (q_ch, s_ch, starts))
    o_slc = jnp.moveaxis(o_slc, 0, 2).reshape(b, h, t, d)

    qb = WIN_QBLOCK
    nqb = t // qb
    nprev = NSA_WINDOW // qb

    def band(z):
        zp = jnp.pad(z, ((0, 0), (0, 0), (nprev * qb, 0), (0, 0))).reshape(b, h, nqb + nprev, qb, d)
        return jnp.concatenate([zp[:, :, i:i + nqb] for i in range(nprev + 1)], axis=3)

    k_band = band(_rms(to_heads(kw), k_g[2]))
    v_band = band(to_heads(vw).astype(f32))
    blk_i = jnp.arange(nqb, dtype=jnp.int32)[:, None]
    qpos = blk_i * qb + jnp.arange(qb, dtype=jnp.int32)[None, :]
    kpos = blk_i * qb - nprev * qb + jnp.arange((nprev + 1) * qb, dtype=jnp.int32)[None, :]
    dist_w = qpos[:, :, None] - kpos[:, None, :]
    ok_w = (dist_w >= 0) & (dist_w < NSA_WINDOW) & (kpos[:, None, :] >= 0)
    s_w = (jnp.einsum('bhnqd,bhnkd->bhnqk', q.reshape(b, h, nqb, qb, d), k_band) * scale
           - slopes[None, :, None, None, None] * dist_w.astype(f32))
    p_w = jax.nn.softmax(jnp.where(ok_w, s_w, NEG), axis=-1)
    o_win = jnp.einsum('bhnqk,bhnkd->bhnqd', p_w, v_band).reshape(b, h, t, d)

    g = jax.nn.sigmoid(gates.astype(f32)).reshape(b, t, 3, h)
    g = jnp.transpose(g, (2, 0, 3, 1))[..., None]
    return from_heads(g[0] * o_cmp + g[1] * o_slc + g[2] * o_win)

def grouped_experts(xf, eid, gate, w1, w3, w2):
    n, dm = xf.shape
    na = eid.shape[0]
    tok = jnp.arange(na, dtype=jnp.int32) // TOP_K_IN_GROUP
    order = jnp.argsort(eid)
    se = eid[order]
    counts = jnp.bincount(eid, length=N_EXPERTS)
    pcounts = (counts + MOE_BLOCK - 1) // MOE_BLOCK * MOE_BLOCK
    starts = jnp.cumsum(counts) - counts
    pends = jnp.cumsum(pcounts)
    pstarts = pends - pcounts
    dest = pstarts[se] + (jnp.arange(na, dtype=jnp.int32) - starts[se])
    cap = (-(-na // MOE_BLOCK) + N_EXPERTS) * MOE_BLOCK
    nblk = cap // MOE_BLOCK
    buf_tok = jnp.full((cap,), n, dtype=jnp.int32).at[dest].set(tok[order])
    buf_gate = jnp.zeros((cap,), jnp.float32).at[dest].set(gate[order])
    blk_e = jnp.minimum(jnp.searchsorted(pends, jnp.arange(nblk, dtype=jnp.int32) * MOE_BLOCK, side='right'),
                        N_EXPERTS - 1)
    xpad = jnp.concatenate([xf, jnp.zeros((1, dm), xf.dtype)], axis=0)
    xb = xpad[buf_tok].reshape(nblk, MOE_BLOCK, dm)

    def expert_block(args):
        xblk, e = args
        return (jax.nn.silu(xblk @ w1[e]) * (xblk @ w3[e])) @ w2[e]

    yb = lax.map(expert_block, (xb, blk_e)).reshape(cap, dm)
    yb = yb * buf_gate[:, None].astype(yb.dtype)
    return jnp.zeros((n + 1, dm), yb.dtype).at[buf_tok].add(yb)[:n]

def hier_moe(h, wg, bg, we, be, w1, w3, w2):
    f32 = jnp.float32
    b, t, dm = h.shape
    n = b * t
    xf = h.reshape(n, dm)
    lg = (xf @ wg + bg).astype(f32)
    pg = jax.nn.softmax(lg, axis=-1)
    _, grp = lax.top_k(lg, 1)
    grp_1h = jax.nn.one_hot(grp[:, 0], N_GROUPS, dtype=f32)
    p_grp = jnp.sum(pg * grp_1h, axis=-1, keepdims=True)
    le = (xf @ we + be).astype(f32).reshape(n, N_GROUPS, EXPERTS_PER_GROUP)
    le_g = jnp.einsum('ng,nge->ne', grp_1h, le)
    top_p, top_i = lax.top_k(jax.nn.softmax(le_g, axis=-1), TOP_K_IN_GROUP)
    top_p = top_p / jnp.sum(top_p, axis=-1, keepdims=True)
    gate = p_grp * top_p
    eid = grp * EXPERTS_PER_GROUP + top_i
    y = grouped_experts(xf, eid.reshape(-1), gate.reshape(-1), w1, w3, w2)
    return y.reshape(b, t, dm)

def hybrid_layer(x, c, norm1_g, norm2_g, ada_w, ada_b, w_in, mlstm_gate_b, mlstm_conv_w, mlstm_out_g,
                 moba_qk_g, ret_out_g, nsa_q_g, nsa_k_g, nsa_cmp_pos, nsa_cmp_w1, nsa_cmp_w2, w_out,
                 router_g_w, router_g_b, router_e_w, router_e_b, exp_w1, exp_w3, exp_w2):
    dtype = x.dtype
    mod = jax.nn.silu(c) @ ada_w + ada_b
    sh1, sc1, g1, sh2, sc2, g2 = jnp.split(mod[:, None, :], 6, axis=-1)
    h = (_rms(x, norm1_g) * (1.0 + sc1) + sh1).astype(dtype)
    z = h @ w_in
    p = {}
    off = 0
    for name, width in IN_LAYOUT:
        p[name] = z[..., off:off + width]
        off += width
    slopes = alibi_slopes()
    y_m = mlstm_mixer(p['m_q'], p['m_k'], p['m_v'], p['m_o'], p['m_i'], p['m_f'],
                      mlstm_conv_w, mlstm_gate_b, mlstm_out_g)
    y_b = moba_mixer(p['b_q'], p['b_k'], p['b_v'], moba_qk_g, slopes[0::2])
    y_r = retention_mixer(p['r_q'], p['r_k'], p['r_v'], p['r_g'], ret_out_g)
    y_n = nsa_mixer(p['n_q'], p['n_kc'], p['n_vc'], p['n_ks'], p['n_vs'], p['n_kw'], p['n_vw'], p['n_g'],
                    nsa_q_g, nsa_k_g, nsa_cmp_pos, nsa_cmp_w1, nsa_cmp_w2, slopes[1::2])
    y = jnp.concatenate([y_m, y_b, y_r, y_n], axis=-1).astype(dtype) @ w_out
    x = x + g1 * y
    h2 = (_rms(x, norm2_g) * (1.0 + sc2) + sh2).astype(dtype)
    return x + g2 * hier_moe(h2, router_g_w, router_g_b, router_e_w, router_e_b, exp_w1, exp_w3, exp_w2)

def setup_inputs(seed: int = 0) -> dict:
    key = jax.random.key(seed)
    keys = iter(jax.random.split(key, 40))

    def nrm(shape, scale):
        return jax.random.normal(next(keys), shape, jnp.float32) * scale

    L, D, H, DH = DEPTH, D_MODEL, HEADS, HEAD_DIM
    f_bias = jnp.linspace(3.0, 6.0, H, dtype=jnp.float32)[None, :] + nrm((L, H), 0.1)
    return {
        'x': nrm((BATCH, SEQ, D), 1.0),
        'c': nrm((BATCH, D), 1.0),
        'norm1_g': 1.0 + nrm((L, D), 0.02),
        'norm2_g': 1.0 + nrm((L, D), 0.02),
        'ada_w': nrm((L, D, 6 * D), 0.5 * D ** -0.5),
        'ada_b': nrm((L, 6 * D), 0.01),
        'w_in': nrm((L, D, D_IN), D ** -0.5),
        'mlstm_gate_b': jnp.stack([nrm((L, H), 0.1), f_bias], axis=1),
        'mlstm_conv_w': nrm((L, MLSTM_CONV, 2 * GROUP_W), MLSTM_CONV ** -0.5),
        'mlstm_out_g': 1.0 + nrm((L, DH), 0.02),
        'moba_qk_g': 1.0 + nrm((L, 2, DH), 0.02),
        'ret_out_g': 1.0 + nrm((L, DH), 0.02),
        'nsa_q_g': 1.0 + nrm((L, DH), 0.02),
        'nsa_k_g': 1.0 + nrm((L, 3, DH), 0.02),
        'nsa_cmp_pos': nrm((L, 2, NSA_CMP_LEN, DH), 0.02),
        'nsa_cmp_w1': nrm((L, 2, NSA_CMP_LEN * DH, DH), (NSA_CMP_LEN * DH) ** -0.5),
        'nsa_cmp_w2': nrm((L, 2, DH, DH), DH ** -0.5),
        'w_out': nrm((L, D_MIX, D), D_MIX ** -0.5),
        'router_g_w': nrm((L, D, N_GROUPS), D ** -0.5),
        'router_g_b': nrm((L, N_GROUPS), 0.01),
        'router_e_w': nrm((L, D, N_EXPERTS), D ** -0.5),
        'router_e_b': nrm((L, N_EXPERTS), 0.01),
        'exp_w1': nrm((L, N_EXPERTS, D, D_EXPERT), D ** -0.5),
        'exp_w3': nrm((L, N_EXPERTS, D, D_EXPERT), D ** -0.5),
        'exp_w2': nrm((L, N_EXPERTS, D_EXPERT, D), D_EXPERT ** -0.5),
    }

def reference(x, c, norm1_g, norm2_g, ada_w, ada_b, w_in, mlstm_gate_b, mlstm_conv_w, mlstm_out_g,
              moba_qk_g, ret_out_g, nsa_q_g, nsa_k_g, nsa_cmp_pos, nsa_cmp_w1, nsa_cmp_w2, w_out,
              router_g_w, router_g_b, router_e_w, router_e_b, exp_w1, exp_w3, exp_w2):
    for l in range(DEPTH):
        x = hybrid_layer(x, c, norm1_g[l], norm2_g[l], ada_w[l], ada_b[l], w_in[l], mlstm_gate_b[l],
                         mlstm_conv_w[l], mlstm_out_g[l], moba_qk_g[l], ret_out_g[l], nsa_q_g[l], nsa_k_g[l],
                         nsa_cmp_pos[l], nsa_cmp_w1[l], nsa_cmp_w2[l], w_out[l], router_g_w[l], router_g_b[l],
                         router_e_w[l], router_e_b[l], exp_w1[l], exp_w3[l], exp_w2[l])
    return x


_drawn_inputs = setup_inputs


def setup_inputs(seed=0):
    import zlib

    import numpy as np

    out = dict(_drawn_inputs(seed))
    spreads = {}
    factors = {'norm1_g': 7.024,
     'norm2_g': 5.386,
     'ada_b': 5.35,
     'mlstm_out_g': 8.0,
     'moba_qk_g': 8.0,
     'ret_out_g': 8.0,
     'nsa_q_g': 8.0,
     'nsa_k_g': 8.0,
     'nsa_cmp_pos': 8.0,
     'router_g_b': 8.0,
     'router_e_b': 8.0}
    for name, (base, spread) in spreads.items():
        noise = np.random.default_rng([zlib.crc32(name.encode()), seed]).standard_normal(out[name].shape)
        drawn = base * np.exp(spread * noise) if base else spread * noise
        out[name] = jnp.asarray(drawn.astype(out[name].dtype))
    for name, factor in factors.items():
        out[name] = (out[name] * factor).astype(out[name].dtype)
    return out
```

```python
from contextlib import ExitStack

import numpy as np

import concourse.bass as bass
from concourse import mybir

F32 = mybir.dt.float32
I32 = mybir.dt.int32
ALU = mybir.AluOpType
ACT = mybir.ActivationFunctionType
AX = mybir.AxisListType.X

P = 128
D = 2048
T = 256
TT = T // P
KT = D // P
H = 4
DH = 128
GW = H * DH
NE = 32
NG = 4
EPG = NE // NG
DE = 512
N_CMP = T // 16 - 1
CMP_LEN = 32
EPS = 1e-6
NEG = -1e30
QSCALE = float(DH) ** -0.5

LAYOUT = (('m_q', GW), ('m_k', GW), ('m_v', GW), ('m_o', GW), ('m_i', H), ('m_f', H),
          ('b_q', GW), ('b_k', GW), ('b_v', GW), ('r_q', GW), ('r_k', GW), ('r_v', GW), ('r_g', GW),
          ('n_q', GW), ('n_kc', GW), ('n_vc', GW), ('n_ks', GW), ('n_vs', GW), ('n_kw', GW), ('n_vw', GW),
          ('n_g', 3 * H))
COL = {}
_o = 0
for _n, _w in LAYOUT:
    COL[_n] = _o
    _o += _w
NX = 2 * H + 3 * H

CONST = {}
_o = 0
for _n, _w in (('ident', P), ('tri', P), ('ones', P), ('sel4', P), ('iota', 32), ('alibi', 8 * T),
               ('cmp_bias', TT * H * N_CMP), ('cmp_ok', TT * H * N_CMP),
               ('decay', H * T), ('negmask', T)):
    CONST[_n] = (_o, _w)
    _o += _w
NCONST = _o
N_EARLY = CONST['decay'][0]

ADA_FIRST = [4, 0, 5, 1, 6, 2, 7, 3]
ADA_LATER = [16, 12, 17, 13, 18, 14, 19, 15, 8, 9, 10, 11, 20, 21, 22, 23]
ADA = ADA_FIRST + ADA_LATER
ORDER = [('chunk', 'n_kc'), ('extras', 0), ('ada', 8), ('chunk', 'n_vc'), ('gates', 0), ('ada', 9),
         ('cmp_hid', 0), ('chunk', 'n_q'), ('ada', 10), ('cmp_out', 0),
         ('chunk', 'n_ks'), ('norm', 'n_q'), ('turn', 'n_q'), ('ada', 11), ('cmp_kT', 0),
         ('chunk', 'n_vs'), ('norm', 'n_ks'), ('cmp_scores', 0), ('ada', 12), ('turn', 'n_ks'),
         ('chunk', 'n_kw'), ('cmp_pT', 0), ('ada', 13), ('cmp_pv', 0),
         ('chunk', 'n_vw'), ('norm', 'n_kw'), ('scores', 'slc'), ('ada', 14), ('turn', 'n_kw'),
         ('chunk', 'm_q'), ('turn_p', 'slc'), ('ada', 15), ('conv', 'm_q'),
         ('chunk', 'm_k'), ('pv', 'slc'), ('scores', 'win'), ('ada', 16), ('conv', 'm_k'),
         ('chunk', 'm_v'), ('turn_p', 'win'), ('ada', 17), ('pv', 'win'), ('m_decay', 0),
         ('chunk', 'm_o'), ('turn_y', 'n'), ('ada', 18), ('m_scores', 0),
         ('chunk', 'b_q'), ('m_pv', 0), ('norm', 'b_q'), ('ada', 19), ('turn', 'b_q'),
         ('chunk', 'b_k'), ('turn_y', 'm'), ('norm', 'b_k'), ('ada', 20), ('turn', 'b_k'),
         ('chunk', 'b_v'), ('scores', 'moba'), ('ada', 21),
         ('chunk', 'r_q'), ('turn_p', 'moba'), ('ada', 22),
         ('chunk', 'r_k'), ('pv', 'moba'), ('ada', 23),
         ('chunk', 'r_v'), ('r_scores', 0), ('turn_y', 'b'),
         ('chunk', 'r_g'), ('r_pv', 0), ('turn_y', 'r')]


def place_sums(order):
    placed, waiting = [], []
    for step, arg in order:
        placed.append((step, arg))
        if step == 'ada':
            waiting.append(arg)
        elif step == 'chunk':
            placed += [('ada_sum', n) for n in waiting]
            waiting = []
    assert not waiting
    return placed


ORDER = place_sums(ORDER)
CHUNKS = [a for s, a in ORDER if s == 'chunk']
MIX_Y = {'m': 0, 'b': 1, 'r': 2, 'n': 3}
STREAM = ([('ada', n) for n in range(len(ADA_FIRST))]
          + [(s if s != 'cmp_hid' else 'cmp', a) for s, a in ORDER if s in ('chunk', 'ada', 'cmp_hid')]
          + [('wout', n) for n in range(D // 512)])
RING = 4
HALF = 8 * 512
PER_GROUP = 24
EXPERT_BASE = 2 * len(STREAM)


SEMAPHORES = (
    "slot_full0", "slot_full1", "slot_full2", "slot_full3", "half_used", "rounds_ready", "out_ready", "stored",
    "exponent_ready", "x_ms", "x_rstd", "kc_ms", "kc_rstd", "norm_n_q_ms", "norm_n_ks_ms", "norm_n_kw_ms",
    "norm_b_q_ms", "norm_b_k_ms", "norm_n_q_rstd", "norm_n_ks_rstd", "norm_n_kw_rstd", "norm_b_q_rstd",
    "norm_b_k_rstd", "y_m_ms", "y_r_ms", "y_m_rstd", "y_r_rstd", "scores_done", "negmask_loaded",
    "decay_loaded", "r_scores_done", "router_loaded", "x_again", "x1_ms", "x1_rstd", "consts_loaded",
    "rows_loaded", "cols_turned", "xhat_ready1", "xhat_ready2", "xT_copied1", "xT_copied2", "xT_turned1",
    "xT_turned2", "csil_ready", "ada_combined", "ada_partial", "ada_summed", "chunk_copied", "h_ready",
    "misc_loaded", "cols_ready", "extras_done", "zx_ready", "gates_turned", "gates_read", "blocks_ready",
    "hid_ready", "cmp_projected", "kc_normed", "turned_ready", "kc_turned", "kct_ready", "cmp_scores_done",
    "cmp_exp", "cmp_p_turned", "cmp_pT_ready", "cmp_pv_done", "normed", "kc_read", "vc_ready",
    "cmp_scores_read", "scores_read", "m_o_read", "yT_ready_m", "turned", "cmp_y", "o_read", "exp_done",
    "p_turned", "pT_ready", "o_done", "gate_rows_ready", "hsel_ready", "m_cols_turned", "conv_done",
    "yT_ready_n", "y_ready_b", "m_scores_done", "m_p_ready", "r_p_ready", "yT_ready_b", "m_pv_done",
    "r_pv_done", "y_ready_n", "y_ready_m", "y_ready_r", "m_cols_read", "m_args_ready", "y_turned_n",
    "y_turned_m", "y_turned_b", "y_turned_r", "yT_ready_r", "x1_ready", "router_done", "mask_ready",
    "places_done", "g_ready", "y_added", "gathered", "g_turned", "xt_act", "xt_dve", "gt_ready", "round_shifted", "hh_ready",
    "hh_turned", "hT_ready", "y_copied", "scattered", "x_loaded", "c_tanh", "x_squared", "gains_ready",
    "gate_tanh_m", "gate_tanh_r", "n_gate_tanh", "f_abs", "f_exp", "f_one", "f_ln", "gelu_arg", "gelu_tanh",
    "cmp_arg", "cmp_e", "nmax_ready", "conv_sum", "conv_tanh", "enm_ready", "m_decay_ready", "x1_squared",
    "group_arg", "group_exp", "pair_arg", "pair_exp", "e_ready", "dve_step", "hid_read", "r_o_read",
    "dve_loop_step",
)


def constants():
    c = np.zeros((P, NCONST), np.float32)

    def put(name, a):
        o, w = CONST[name]
        c[:, o:o + w] = np.asarray(a, np.float32).reshape(P, w)
    p = np.arange(P)
    put('ident', np.eye(P))
    put('tri', p[:, None] <= p[None, :])
    put('ones', np.ones((P, P)))
    put('sel4', np.repeat((p % 32 == 0)[:, None], P, 1))
    put('iota', np.tile(np.arange(32), (P, 1)))
    slopes = 2.0 ** (-np.arange(1, 2 * H + 1, dtype=np.float64))
    dist = (P + p)[:, None] - np.arange(T)[None, :]
    put('alibi', np.stack([np.where(dist >= 0, -slopes[2 * h + st] * dist, NEG)
                           for st in range(2) for h in range(H)], 1))
    gam = np.log1p(-2.0 ** (-5.0 - np.arange(H)))
    fwd = np.arange(T)[None, :] - p[:, None]
    put('decay', np.stack([np.where(fwd >= 0, np.exp(gam[h] * np.maximum(fwd, 0)), 0.0) * QSCALE
                           for h in range(H)], 1))
    t = (np.arange(TT) * P)[None, :, None] + p[:, None, None]
    dc = t - (np.arange(N_CMP) * 16 + CMP_LEN - 1)[None, None, :]
    put('cmp_bias', np.stack([np.where(dc >= 0, -slopes[2 * h + 1] * dc, NEG) for h in range(H)], 2))
    put('cmp_ok', np.stack([dc >= 0] * H, 2))
    put('negmask', np.where(fwd >= 0, 0.0, NEG))
    return c


def build_program(nc, a, out):
    with ExitStack() as ctx:
        def sb(name, cols, dt=F32):
            return ctx.enter_context(nc.sbuf_tensor(name, [P, cols], dt))

        def psum(name, cols):
            return ctx.enter_context(nc.psum_tensor(name, [P, cols], F32))

        ring = [sb(f"ring{s}", HALF) for s in range(RING)]
        consts = sb("consts", N_EARLY)
        buf_h = sb("buf_h", TT * D)
        buf_x = sb("buf_x", TT * D)
        g1b = sb("g1b", D)
        g2b = sb("g2b", D)
        Z = sb("Z", 10 * 1024)
        pad = sb("pad", 2 * H * (T + 3))
        tmp = sb("tmp", 2048)
        yb = sb("yb", 1024)
        PA = sb("PA", 1536)
        PB = sb("PB", 1536)
        ada_s = sb("ada_s", 512)
        rows = PB[:, 0:3 * P]
        w2c = PB[:, 384:640]
        wx = PA[:, 1024:1024 + KT * NX]
        cols_a = sb("cols_a", 88)
        cols_b = sb("cols_b", 96)
        cols_c = sb("cols_c", 64)
        csil = sb("csil", KT * 32)
        small = sb("small", 512)
        rb = sb("rb", 36)
        modc = sb("modc", 4 * KT)
        gsc = sb("gsc", 2 * KT)
        hsel = PB[:, 0:H * P]
        hid = sb("hid", 120)
        kct = sb("kct", 60)
        vc = Z[:, 9216:9216 + GW]
        wr = Z[:, 8192:8192 + KT * 36]
        zx = sb("zx", TT * NX)
        sgn = sb("sgn", TT * 3 * H)
        gat = sb("gat", 3 * T)
        gb = sb("gb", 2)
        cnt_i = sb("cnt_i", 1, I32)

        W = psum("W", 2048)
        M = psum("M", 1536)
        A = psum("A", 512)

        hT = buf_h[:].rearrange("p (k t) -> p k t", k=KT)
        x1 = buf_h[:].rearrange("p (a d) -> p a d", a=TT)
        xs = buf_x[:].rearrange("p (a d) -> p a d", a=TT)
        YT = buf_x[:].rearrange("p (k t) -> p k t", k=KT)

        negmask = Z[:, 5120:5376]

        def const(name):
            o, w = CONST[name]
            return consts[:, o:o + w]
        ident, tri, ones, sel4 = const('ident'), const('tri'), const('ones'), const('sel4')
        alibi = const('alibi').rearrange("p (s h t) -> p s h t", s=2, h=H)
        decay = Z[:, 3072:4096].rearrange("p (h t) -> p h t", h=H)

        def slot(i):
            return Z[:, i * 1024:(i + 1) * 1024]
        zslot = {'n_kc': slot(0), 'n_vc': slot(1), 'n_q': slot(2), 'n_ks': slot(4), 'n_vs': slot(6),
                 'n_kw': slot(7), 'n_vw': slot(9), 'm_v': slot(2), 'm_o': slot(4), 'b_q': slot(0),
                 'b_k': slot(1), 'b_v': slot(6), 'r_q': slot(8), 'r_k': slot(2), 'r_v': slot(9), 'r_g': slot(4)}
        tslot = {'n_q': slot(3), 'n_ks': slot(5), 'n_kw': slot(8), 'b_q': slot(7), 'b_k': slot(0),
                 'm_q': slot(0), 'm_k': slot(1), 'r_q': slot(8), 'r_k': slot(2)}
        padv = pad[:].rearrange("p (w h t) -> p w h t", w=2, h=H)
        blk = [pad[:, 0:CMP_LEN * 60], tmp[:, 0:CMP_LEN * 60]]

        def heads(ap):
            return ap.rearrange("p (h t) -> p h t", h=H)

        def tth(ap):
            return ap.rearrange("p (a d) -> p a d", d=DH)

        CA_C, CA_N1, CA_N2, CA_CONV, CA_G = 0, 16, 32, 48, 80
        GAIN = {'m': CA_G, 'b_q': CA_G + 1, 'b_k': CA_G + 2, 'r': CA_G + 3, 'n_q': CA_G + 4,
                'cmp': CA_G + 5, 'n_ks': CA_G + 6, 'n_kw': CA_G + 7}

        used = [0]

        def sm(n):
            o = used[0]
            used[0] += n
            assert used[0] <= 512
            return small[:, o:o + n]
        minus_half = sm(8)
        ss, rst = sm(8), sm(8)
        ssx, rsx = sm(2), sm(2)
        mx, nmx, lsum, fac = sm(8), sm(8), sm(8), sm(8)
        ssy, rsy = sm(8), sm(8)
        bcol_enm, den = sm(16), sm(8)
        bcol, enm = bcol_enm[:, 0:8], bcol_enm[:, 8:16]
        ssc, rsc = sm(1), sm(1)
        cmx, csum, cf = sm(8), sm(8), sm(8)
        cs = sm(48)
        exc = sm(24)
        lg = sm(TT * 36)
        pos = sm(TT * (NE + 4))
        gate = sm(TT * (NE + 4))
        rt = sm(40)

        sem = {name: ctx.enter_context(nc.semaphore(name)) for name in SEMAPHORES}
        slot_full = [sem[f"slot_full{s}"] for s in range(RING)]
        half_used = sem["half_used"]

        def chunk_no(name):
            return CHUNKS.index(name) + 1

        def item_done(eng, kind, arg):
            eng.wait_ge(half_used, 2 * (STREAM.index((kind, arg)) + 1))

        def kview(ap):
            return ap.rearrange("(k p) n -> p k n", p=P)
        ada_w, w_in, w_out = kview(a['ada_w'][0]), kview(a['w_in'][0]), kview(a['w_out'][0])
        cmp1 = a['nsa_cmp_w1'][0]

        h2T = Z[:, 0:4096].rearrange("p (k t) -> p k t", k=KT)
        yacc = Z[:, 0:4096].rearrange("p (a d) -> p a d", a=TT)
        XT = Z[:, 4096:6144].rearrange("p (k j) -> p k j", k=KT)
        ysb = Z[:, 6144:8192]
        Gm = tmp[:, 0:256].rearrange("p (a q j) -> p a q j", a=TT, q=4)
        Gg = tmp[:, 256:512].rearrange("p (a q j) -> p a q j", a=TT, q=4)
        GT = tmp[:, 512:768]
        hh, ee, aa = (tmp[:, 768 + 128 * i:896 + 128 * i] for i in range(3))
        hTs = tmp[:, 1408:1536]
        ohg, le_g, oh1, oh2, le2, tie = (PA[:, 64 * i:64 * i + 64] for i in range(6))
        expd = PA[:, 384:512]
        mask = PA[:, 512:576]
        mprod = PA[:, 576:640]
        jdesc = PA[:, 640:672]
        w12 = PA[:, 672:688]

        def load_rounds(eng):
            eng.wait_ge(sem["rounds_ready"], 1)
            return eng.value_load(cnt_i[0:1, 0:1], min_val=1, max_val=T // 32)

        block = ctx.enter_context(nc.Block())

        @block.sync
        def _(sp):
            for i in range(EXPERT_BASE):
                kind, arg = STREAM[i // 2]
                hf = i % 2
                if i >= RING:
                    sp.wait_ge(half_used, i - RING + 1)
                dst = ring[i % RING][:].rearrange("p (k n) -> p k n", k=8)
                ks = slice(8 * hf, 8 * hf + 8)
                if kind == 'ada':
                    src = ada_w[:, ks, 512 * ADA[arg]:512 * ADA[arg] + 512]
                elif kind == 'chunk':
                    src = w_in[:, ks, COL[arg]:COL[arg] + GW]
                elif kind == 'cmp':
                    src = cmp1[hf].rearrange("(l p) e -> p l e", p=P)
                    dst = ring[i % RING][:].rearrange("p (l e) -> p l e", l=CMP_LEN)
                else:
                    src = w_out[:, ks, 512 * arg:512 * arg + 512]
                sp.dma_start(dst, src).then_inc(slot_full[i % RING], 16)

            def four_experts(it, g):
                for j in range(PER_GROUP):
                    q, part, hf = j // 6, j % 6 // 2, j % 2
                    i = EXPERT_BASE + j
                    sp.wait_ge(half_used, PER_GROUP * it + (i - RING + 1))
                    if part < 2:
                        w = a['exp_w1' if part == 0 else 'exp_w3'][0]
                        sp.dma_start(ring[i % RING][:].rearrange("p (k n) -> p k n", k=8),
                                     w[4 * g + q].rearrange("(k p) n -> p k n", p=P)[:, 8 * hf:8 * hf + 8, :]
                                     ).then_inc(slot_full[i % RING], 16)
                    else:
                        w = a['exp_w2'][0]
                        sp.dma_start(ring[i % RING][:].rearrange("p (c n) -> p c n", c=2),
                                     w[4 * g + q].rearrange("(c p) n -> p c n", p=P)[:, 2 * hf:2 * hf + 2, :]
                                     ).then_inc(slot_full[i % RING], 16)

            four_experts(0, 0)
            rounds = load_rounds(sp)
            with sp.Fori(1, rounds * (NE // 4)) as it:
                four_experts(it, it % (NE // 4))
            sp.wait_ge(sem["out_ready"], 2)
            sp.dma_start(out[0].rearrange("(a p) d -> p a d", p=P), yacc).then_inc(sem["stored"], 16)
            sp.wait_ge(sem["stored"], 16)

        @block.gpsimd
        def _(pool):
            pool.memset(minus_half, -0.5).then_inc(sem["exponent_ready"], 1)
            pool.wait_ge(sem["exponent_ready"], 1)

            def rsqrt(v):
                return pool.tensor_tensor(v, v, minus_half[0:v.shape[0], 0:v.shape[1]], ALU.pow)

            pool.wait_ge(sem["x_ms"], 1)
            rsqrt(rsx).then_inc(sem["x_rstd"], 1)
            n_att = 0
            for step, arg in ORDER:
                if step == 'cmp_out':
                    pool.wait_ge(sem["kc_ms"], 1)
                    rsqrt(rsc[0:60, :]).then_inc(sem["kc_rstd"], 1)
                elif step == 'norm':
                    pool.wait_ge(sem[f"norm_{arg}_ms"], 1)
                    rsqrt(rst).then_inc(sem[f"norm_{arg}_rstd"], 1)
                elif step in ('m_pv', 'r_pv'):
                    pool.wait_ge(sem[f"y_{step[0]}_ms"], 1)
                    rsqrt(rsy).then_inc(sem[f"y_{step[0]}_rstd"], 1)
                elif step == 'scores':
                    n_att += 1
                    if arg == 'slc':
                        pool.wait_ge(sem["scores_done"], n_att)
                        o, w = CONST['negmask']
                        pool.dma_start(negmask, a['consts'][:, o:o + w]).then_inc(sem["negmask_loaded"], 16)
                    elif arg == 'win':
                        pool.wait_ge(sem["scores_done"], n_att)
                        o, w = CONST['decay']
                        pool.dma_start(Z[:, 3072:4096], a['consts'][:, o:o + w]).then_inc(sem["decay_loaded"], 16)
                elif step == 'r_scores':
                    pool.wait_ge(sem["r_scores_done"], 1)
                    wrv = wr.rearrange("p (k n) -> p k n", k=KT)
                    pool.dma_start(wrv[:, :, 0:NG], kview(a['router_g_w'][0])).then_inc(sem["router_loaded"], 16)
                    pool.dma_start(wrv[:, :, NG:36], kview(a['router_e_w'][0])).then_inc(sem["router_loaded"], 16)
                    pool.dma_start(rb[:, 0:NG], a['router_g_b'].to_broadcast([P,
                            NG])).then_inc(sem["router_loaded"], 16)
                    pool.dma_start(rb[:, NG:36], a['router_e_b'].to_broadcast([P,
                            NE])).then_inc(sem["router_loaded"], 16)
                elif (step, arg) == ('chunk', CHUNKS[-1]):
                    item_done(pool, 'chunk', arg)
                    pool.dma_start(x1, a['x'][0].rearrange("(a p) d -> p a d", p=P)).then_inc(sem["x_again"], 16)
            pool.wait_ge(sem["x1_ms"], 1)
            rsqrt(rsx).then_inc(sem["x1_rstd"], 1)
            pool.memset(GT, 0.0).then_inc(sem["gt_ready"], 1)
            pool.wait_ge(sem["gt_ready"], 1)
            for q in range(4):
                pool.memset(ysb[32 * q:32 * q + 32, :], 0.0).then_inc(sem["y_copied"], 1)
                pool.wait_ge(sem["y_copied"], q + 1)
            pool.wait_ge(sem["router_done"], 1)
            pool.memset(Z[:, 0:4096], 0.0).then_inc(sem["y_added"], 1)

        @block.tensor
        def _(pe):
            half = [0]

            def half_arrives():
                i = half[0]
                pe.wait_ge(slot_full[i % RING], 16 * (i // RING + 1))
                return ring[i % RING]

            def half_done(ins):
                ins.then_inc(half_used, 1)
                half[0] += 1

            pe.wait_ge(sem["consts_loaded"], 16)
            pe.wait_ge(sem["rows_loaded"], 16 * 11)
            r3 = rows.rearrange("p (i d) -> p i d", i=3)
            pe.transpose(M[:, 0:88], r3[0:88, 0, :], ident[0:88, 0:88])
            pe.transpose(M[:, 512:608], r3[0:96, 1, :], ident[0:96, 0:96])
            pe.transpose(M[:, 1024:1088], r3[0:64, 2, :], ident[0:64, 0:64]).then_inc(sem["cols_turned"], 1)

            def turn_x(first):
                for b in range(4):
                    if b == 0:
                        pe.wait_ge(sem[f"xhat_ready{first}"], 1)
                    if b >= 2:
                        pe.wait_ge(sem[f"xT_copied{first}"], b - 1)
                    for k in range(4):
                        for tt in range(TT):
                            o = (b % 2) * 1024 + k * T + tt * P
                            ins = pe.transpose(W[:, o:o + P], xs[:, tt, (4 * b + k) * P:(4 * b + k + 1) * P], ident)
                    ins.then_inc(sem[f"xT_turned{first}"], 1)
            turn_x(1)

            def ada_products(n):
                if n == 0:
                    pe.wait_ge(sem["csil_ready"], 1)
                else:
                    pe.wait_ge(sem["ada_combined"], n)
                for hf in range(2):
                    w = half_arrives()
                    for k in range(8):
                        kk = 8 * hf + k
                        j = kk % 4
                        ins = pe.matmul(A[32 * j:32 * j + 32, :], csil[:, 32 * kk:32 * kk + 32],
                                        w[:, 512 * k:512 * k + 512], start=(kk < 4), stop=(kk >= 12))
                    half_done(ins)

            def ada_combine(n):
                pe.wait_ge(sem["ada_partial"], n + 1)
                if ADA[n] // 4 in (2, 5):
                    pe.matmul(A[:], sel4, ada_s[:], start=True, stop=True).then_inc(sem["ada_summed"], 1)
                else:
                    for b in range(4):
                        ins = pe.matmul(A[:, b:b + 1], ada_s[:, b * P:(b + 1) * P], sel4[:, 0:1], start=True, stop=True)
                    ins.then_inc(sem["ada_summed"], 1)

            def chunk(name, n):
                o = (n % 2) * 1024
                if n >= 2:
                    pe.wait_ge(sem["chunk_copied"], n - 1)
                elif n == 0:
                    pe.wait_ge(sem["h_ready"], 4)
                    pe.wait_ge(sem["xT_copied1"], 4)
                lo, hi = half_arrives(), ring[(half[0] + 1) % RING]
                if name in ('m_q', 'm_k', 'r_q', 'r_k', 'n_kc', 'n_vc'):
                    for hf, w in ((0, lo), (1, hi)):
                        if hf == 1:
                            half_arrives()
                        for h in range(H):
                            for k in range(8):
                                kk = 8 * hf + k
                                ins = pe.matmul(W[:, o + h * T:o + h * T + T],
                                                w[:, 512 * k + h * P:512 * k + h * P + P], hT[:, kk, :],
                                                start=(kk == 0 and h % 2 == 0), stop=(kk == KT - 1),
                                                skip_group_check=True)
                        if hf == 0:
                            half_done(ins)
                else:
                    for hf, w in ((0, lo), (1, hi)):
                        if hf == 1:
                            half_arrives()
                        for k in range(8):
                            for tt in range(TT):
                                kk = 8 * hf + k
                                ins = pe.matmul(W[:, o + tt * 512:o + tt * 512 + 512], hT[:, kk, tt * P:tt * P + P],
                                                w[:, 512 * k:512 * k + 512], start=(kk == 0), stop=(kk == KT - 1))
                        if hf == 0:
                            half_done(ins)
                half_done(ins)

            def turn8(src):
                for h in range(H):
                    for tt in range(TT):
                        ins = pe.transpose(M[:, h * T + tt * P:h * T + tt * P + P],
                                           src[:, tt * 512 + h * DH:tt * 512 + h * DH + DH], ident)
                return ins

            n_chunk = n_turn = n_att = 0
            for n in range(len(ADA_FIRST)):
                ada_products(n)
                ada_combine(n)
            for step, arg in ORDER:
                if step == 'ada':
                    ada_products(arg)
                elif step == 'ada_sum':
                    ada_combine(arg)
                elif step == 'chunk':
                    chunk(arg, n_chunk)
                    n_chunk += 1
                elif step == 'extras':
                    pe.wait_ge(sem["misc_loaded"], 16 * 7)
                    pe.wait_ge(sem["cols_ready"], 1)
                    for tt in range(TT):
                        for k in range(KT):
                            ins = pe.matmul(M[:, tt * 512:tt * 512 + NX], hT[:, k, tt * P:tt * P + P],
                                            wx[:, k * NX:k * NX + NX], start=(k == 0), stop=(k == KT - 1))
                    ins.then_inc(sem["extras_done"], 1)
                elif step == 'gates':
                    pe.wait_ge(sem["zx_ready"], 1)
                    for f in range(2):
                        for tt in range(TT):
                            ins = pe.transpose(M[0:H, f * T + tt * P:f * T + tt * P + P],
                                               zx[:, tt * NX + H * f:tt * NX + H * f + H], ident)
                    ins.then_inc(sem["gates_turned"], 1)
                elif step == 'cmp_hid':
                    pe.wait_ge(sem["gates_read"], 1)
                    for w in range(2):
                        wt = half_arrives()
                        pe.wait_ge(sem["blocks_ready"], w + 1)
                        for l in range(CMP_LEN):
                            ins = pe.matmul(M[:, 512 * w:512 * w + 60], wt[:, l * P:l * P + P],
                                            blk[w][:, l * 60:l * 60 + 60], start=(l == 0), stop=(l == CMP_LEN - 1))
                        half_done(ins)
                elif step == 'cmp_out':
                    pe.wait_ge(sem["hid_ready"], 1)
                    pe.matmul(M[0:60, 0:DH], hid[:, 0:60], w2c[:, 0:DH], start=True, stop=True)
                    for h in range(H):
                        ins = pe.matmul(M[0:N_CMP, 512 + h * DH:512 + h * DH + DH], hid[:, 60 + 15 * h:75 + 15 * h],
                                        w2c[:, DH:2 * DH], start=True, stop=True)
                    ins.then_inc(sem["cmp_projected"], 1)
                elif step == 'cmp_kT':
                    pe.wait_ge(sem["kc_normed"], 1)
                    pe.wait_ge(sem["turned_ready"], 1)
                    pe.transpose(M[:, 0:60], tmp[0:60, 1024:1152], ident[0:60, 0:60]).then_inc(sem["kc_turned"], 1)
                elif step == 'cmp_scores':
                    pe.wait_ge(sem["kct_ready"], 1)
                    pe.wait_ge(sem["turned_ready"], 1)
                    for tt in range(TT):
                        for h in range(H):
                            o = (tt * H + h) * N_CMP
                            ins = pe.matmul(M[:, o:o + N_CMP], heads(tslot['n_q'])[:, h, tt * P:tt * P + P],
                                            kct[:, 15 * h:15 * h + 15], start=True, stop=True)
                    ins.then_inc(sem["cmp_scores_done"], 1)
                elif step == 'cmp_pT':
                    pe.wait_ge(sem["cmp_exp"], 1)
                    pe.wait_ge(sem["turned_ready"], 2)
                    for i in range(TT * H):
                        ins = pe.transpose(M[0:N_CMP, i * P:i * P + P], PA[:, i * N_CMP:(i + 1) * N_CMP], ident)
                    ins.then_inc(sem["cmp_p_turned"], 1)
                elif step == 'cmp_pv':
                    pe.wait_ge(sem["cmp_pT_ready"], 1)
                    for tt in range(TT):
                        for h in range(H):
                            ins = pe.matmul(M[:, tt * 512 + h * DH:tt * 512 + h * DH + DH],
                                            PB[0:N_CMP, (tt * H + h) * P:(tt * H + h + 1) * P],
                                            vc[0:N_CMP, h * DH:h * DH + DH], start=True, stop=True)
                    ins.then_inc(sem["cmp_pv_done"], 1)
                elif step == 'turn':
                    n_turn += 1
                    pe.wait_ge(sem["normed"], n_turn)
                    if arg == 'n_q':
                        pe.wait_ge(sem["kc_read"], 1)
                        pe.wait_ge(sem["vc_ready"], 1)
                    elif arg == 'n_ks':
                        pe.wait_ge(sem["cmp_scores_read"], 1)
                    elif arg == 'n_kw':
                        pe.wait_ge(sem["scores_read"], 1)
                    elif arg == 'b_q':
                        pe.wait_ge(sem["m_o_read"], 1)
                    else:
                        pe.wait_ge(sem["yT_ready_m"], 1)
                    turn8(zslot[arg]).then_inc(sem["turned"], 1)
                elif step == 'scores':
                    n_att += 1
                    qn, kn = {'slc': ('n_q', 'n_ks'), 'win': ('n_q', 'n_kw'), 'moba': ('b_q', 'b_k')}[arg]
                    pe.wait_ge(sem["turned_ready"], {'slc': 2, 'win': 3, 'moba': 5}[arg])
                    if arg == 'slc':
                        pe.wait_ge(sem["cmp_y"], 1)
                    elif arg == 'win':
                        pe.wait_ge(sem["o_read"], 1)
                    qT, kT = heads(tslot[qn]), heads(tslot[kn])
                    for h in range(H):
                        pe.matmul(M[:, h * T:h * T + T], qT[:, h, P:T], kT[:, h, :], start=True, stop=True)
                        ins = pe.matmul(M[:, 1024 + h * P:1024 + h * P + P], qT[:, h, 0:P], kT[:, h, 0:P],
                                        start=True, stop=True)
                    ins.then_inc(sem["scores_done"], 1)
                elif step == 'turn_p':
                    pe.wait_ge(sem["exp_done"], n_att)
                    if arg == 'slc':
                        pe.wait_ge(sem["turned_ready"], 3)
                    for h in range(H):
                        for i, o in enumerate((1024 + h * P, h * T, h * T + P)):
                            ins = pe.transpose(M[:, h * 384 + i * P:h * 384 + i * P + P], PA[:, o:o + P], ident)
                    ins.then_inc(sem["p_turned"], 1)
                elif step == 'pv':
                    v = zslot[{'slc': 'n_vs', 'win': 'n_vw', 'moba': 'b_v'}[arg]]
                    pe.wait_ge(sem["chunk_copied"], chunk_no({'slc': 'n_vs', 'win': 'n_vw', 'moba': 'b_v'}[arg]))
                    pe.wait_ge(sem["pT_ready"], n_att)
                    for h in range(H):
                        pt = PB[:, h * 384:h * 384 + 384]
                        d = slice(h * DH, h * DH + DH)
                        pe.matmul(M[:, d], pt[:, 0:P], v[:, d], start=True, stop=True)
                        o1 = M[:, 512 + h * DH:512 + h * DH + DH]
                        pe.matmul(o1, pt[:, P:2 * P], v[:, d], start=True, stop=False)
                        ins = pe.matmul(o1, pt[:, 2 * P:3 * P], v[:, 512 + h * DH:512 + h * DH + DH],
                                        start=False, stop=True)
                    ins.then_inc(sem["o_done"], 1)
                elif step == 'm_decay':
                    pe.wait_ge(sem["gate_rows_ready"], 1)
                    pe.wait_ge(sem["hsel_ready"], 1)
                    pe.wait_ge(sem["o_read"], 2)
                    for i in range(2):
                        for tt in range(TT):
                            pe.transpose(M[:, 8 * i + 4 * tt:8 * i + 4 * tt + 4],
                                         gat[0:H, i * T + tt * P:i * T + tt * P + P], ident[0:H, 0:H])
                    for h in range(H):
                        ins = pe.matmul(M[:, 512 + h * T:512 + h * T + T], hsel[0:H, h * P:h * P + P],
                                        gat[0:H, 2 * T:3 * T], start=True, stop=True)
                    ins.then_inc(sem["m_cols_turned"], 1)
                elif step in ('m_scores', 'r_scores'):
                    who = step[0]
                    if who == 'm':
                        pe.wait_ge(sem["conv_done"], 2)
                    else:
                        pe.wait_ge(sem["chunk_copied"], chunk_no('r_k'))
                    if who == 'm':
                        pe.wait_ge(sem["yT_ready_n"], 1)
                    else:
                        pe.wait_ge(sem["y_ready_b"], 1)
                    qT, kT = heads(tslot[who + '_q']), heads(tslot[who + '_k'])
                    for h in range(H):
                        pe.matmul(M[:, h * T:h * T + T], kT[:, h, 0:P], qT[:, h, :], start=True, stop=True)
                        ins = pe.matmul(M[:, 1024 + h * P:1024 + h * P + P], kT[:, h, P:T], qT[:, h, P:T],
                                        start=True, stop=True)
                    ins.then_inc(sem[f"{who}_scores_done"], 1)
                elif step in ('m_pv', 'r_pv'):
                    who = step[0]
                    v = zslot[who + '_v']
                    pe.wait_ge(sem[f"{who}_p_ready"], 1)
                    pe.wait_ge(sem["chunk_copied"], chunk_no(who + '_v'))
                    if who == 'r':
                        pe.wait_ge(sem["yT_ready_b"], 1)
                    for h in range(H):
                        d = slice(h * DH, h * DH + DH)
                        o1 = M[:, 512 + h * DH:512 + h * DH + DH]
                        p0, p01, p11 = (PB[:, h * T:h * T + P], PB[:, h * T + P:h * T + T],
                                        PB[:, 1024 + h * P:1024 + h * P + P])
                        v0, v1 = v[:, d], v[:, 512 + h * DH:512 + h * DH + DH]
                        pe.matmul(M[:, d], p0, v0, start=True, stop=True)
                        pe.matmul(o1, p01, v0, start=True, stop=False)
                        ins = pe.matmul(o1, p11, v1, start=False, stop=True)
                        if who == 'm':
                            pe.matmul(M[:, 1024 + h:1025 + h], p0, ones[:, 0:1], start=True, stop=True)
                            pe.matmul(M[:, 1028 + h:1029 + h], p01, ones[:, 0:1], start=True, stop=False)
                            ins = pe.matmul(M[:, 1028 + h:1029 + h], p11, ones[:, 0:1], start=False, stop=True)
                    ins.then_inc(sem[f"{who}_pv_done"], 1)
                elif step == 'turn_y':
                    pe.wait_ge(sem[f"y_ready_{arg}"], 1)
                    if arg == 'n':
                        pe.wait_ge(sem["m_cols_read"], 1)
                        pe.wait_ge(sem["m_args_ready"], 1)
                    elif arg == 'm':
                        pe.wait_ge(sem["turned_ready"], 4)
                    elif arg == 'b':
                        pe.wait_ge(sem["r_p_ready"], 1)
                    turn8(yb[:]).then_inc(sem[f"y_turned_{arg}"], 1)

            for m in 'nmbr':
                pe.wait_ge(sem[f"yT_ready_{m}"], 1)
            for n in range(D // 512):
                o = (n % 2) * 1024
                if n < 2:
                    pe.wait_ge(sem["chunk_copied"], len(CHUNKS) - 1 + n)
                else:
                    pe.wait_ge(sem["x1_ready"], n - 1)
                for hf in range(2):
                    w = half_arrives()
                    for k in range(8):
                        for tt in range(TT):
                            kk = 8 * hf + k
                            ins = pe.matmul(W[:, o + tt * 512:o + tt * 512 + 512], YT[:, kk, tt * P:tt * P + P],
                                            w[:, 512 * k:512 * k + 512], start=(kk == 0), stop=(kk == KT - 1))
                    half_done(ins)
            assert half[0] == EXPERT_BASE

            pe.wait_ge(sem["x1_ready"], 4)
            turn_x(2)
            pe.wait_ge(sem["router_loaded"], 64)
            pe.wait_ge(sem["xT_copied2"], 4)
            for tt in range(TT):
                for k in range(KT):
                    ins = pe.matmul(M[:, tt * 512:tt * 512 + 36], h2T[:, k, tt * P:tt * P + P], wr[:, 36 * k:36 * k + 36],
                                    start=(k == 0), stop=(k == KT - 1))
            ins.then_inc(sem["router_done"], 1)
            pe.wait_ge(sem["mask_ready"], 1)
            pe.matmul(M[:, 0:NE], tri, mask[:, 0:NE], start=True, stop=True)
            pe.matmul(M[:, 512:512 + NE], ones, mask[:, 0:NE], start=True, stop=False)
            pe.matmul(M[:, 512:512 + NE], tri, mask[:, NE:2 * NE], start=False, stop=True)
            pe.matmul(M[:, 1024:1024 + NE], ones, mask[:, 0:NE], start=True, stop=False)
            pe.matmul(M[:, 1024:1024 + NE], ones, mask[:, NE:2 * NE], start=False,
                    stop=True).then_inc(sem["places_done"], 1)

            def gather():
                for b in range(2):
                    for k in range(8 * b, 8 * b + 8):
                        for tt in range(TT):
                            ins = pe.matmul(W[:, k * P:k * P + P], xs[:, tt, k * P:k * P + P],
                                            tmp[:, 128 * tt:128 * tt + 128], start=(tt == 0), stop=(tt == 1))
                    ins.then_inc(sem["gathered"], 1)

            def scatter(n):
                pe.wait_ge(sem["gt_ready"], n + 1)
                pe.wait_ge(sem["y_copied"], 4 * n + 4)
                for tt in range(TT):
                    pe.wait_ge(sem["y_added"], 2 * n + tt + 1)
                    for b in range(4):
                        ins = pe.matmul(W[:, 512 * b:512 * b + 512], GT[:, tt * P:tt * P + P],
                                        ysb[:, 512 * b:512 * b + 512], start=True, stop=True)
                    ins.then_inc(sem["scattered"], 1)

            pe.wait_ge(sem["g_ready"], 1)
            gather()
            rounds = load_rounds(pe)
            with pe.Fori(0, rounds) as r:
                with pe.Fori(0, NE // 4) as g:
                    it = 8 * r + g
                    for q in range(4):
                        if q == 0:
                            pe.wait_ge(sem["xt_act"], it + 1)
                            pe.wait_ge(sem["xt_dve"], it + 1)
                        elif q == 3:
                            pe.wait_ge(sem["g_ready"], it + 2)
                            pe.wait_ge(sem["y_added"], 2 * it + 3)
                            gather()
                        for w13 in range(2):
                            for hf in range(2):
                                j = 6 * q + 2 * w13 + hf
                                i = EXPERT_BASE + j
                                pe.wait_ge(slot_full[i % RING], 96 * it + 16 * (i // RING + 1))
                                w = ring[i % RING]
                                for k in range(8):
                                    kk = 8 * hf + k
                                    for c in range(4):
                                        ins = pe.matmul(M[32 * c:32 * c + 32, 512 * w13:512 * w13 + 128],
                                                        XT[:, kk, 32 * q:32 * q + 32],
                                                        w[:, 512 * k + 128 * c:512 * k + 128 * c + 128],
                                                        start=(kk == 0), stop=(kk == KT - 1))
                                ins.then_inc(half_used, 1)
                        if q == 0:
                            scatter(it)
                            for tt in range(TT):
                                ins = pe.transpose(M[:, 1024 + tt * P:1024 + tt * P + P],
                                                   tmp[:, 256 + 128 * tt:384 + 128 * tt], ident)
                            ins.then_inc(sem["g_turned"], 1)
                            pe.wait_ge(sem["gt_ready"], it + 2)
                        pe.wait_ge(sem["hh_ready"], 4 * it + q + 1)
                        pe.transpose(M[:, 1024:1152], hh, ident).then_inc(sem["hh_turned"], 1)
                        pe.wait_ge(sem["hT_ready"], 4 * it + q + 1)
                        pe.wait_ge(sem["y_copied"], 4 * it + q + 4)
                        for hf in range(2):
                            i = EXPERT_BASE + 6 * q + 4 + hf
                            pe.wait_ge(slot_full[i % RING], 96 * it + 16 * (i // RING + 1))
                            w = ring[i % RING]
                            for c2 in range(2):
                                c = 2 * hf + c2
                                for m in range(4):
                                    ins = pe.matmul(A[32 * m:32 * m + 32, :], hTs[:, 32 * c:32 * c + 32],
                                                    w[:, 2048 * c2 + 512 * m:2048 * c2 + 512 * m + 512],
                                                    start=(c == 0), stop=(c == 3))
                            ins.then_inc(half_used, 1)
            pe.wait_ge(sem["xt_act"], 8 * rounds + 1)
            pe.wait_ge(sem["xt_dve"], 8 * rounds + 1)
            scatter(8 * rounds)

        @block.scalar
        def _(act):
            x0 = a['x'][0].rearrange("(a p) d -> p a d", p=P)
            act.dma_start(consts[:], a['consts'][:, 0:N_EARLY]).then_inc(sem["consts_loaded"], 16)
            r3 = rows.rearrange("p (i d) -> p i d", i=3)
            act.dma_start(r3[0:16, 0, :], a['c'].rearrange("o (k p) -> (o k) p",
                    p=P)).then_inc(sem["rows_loaded"], 16)
            act.dma_start(r3[16:32, 0, :], a['norm1_g'].rearrange("o (k p) -> (o k) p",
                    p=P)).then_inc(sem["rows_loaded"], 16)
            act.dma_start(r3[32:48, 0, :], a['norm2_g'].rearrange("o (k p) -> (o k) p",
                    p=P)).then_inc(sem["rows_loaded"], 16)
            act.dma_start(r3[48:80, 0, :], a['mlstm_conv_w'][0].rearrange("j (b p) -> (j b) p",
                    p=P)).then_inc(sem["rows_loaded"], 16)
            act.dma_start(r3[80:81, 0, :], a['mlstm_out_g']).then_inc(sem["rows_loaded"], 16)
            act.dma_start(r3[81:83, 0, :], a['moba_qk_g'][0]).then_inc(sem["rows_loaded"], 16)
            act.dma_start(r3[83:84, 0, :], a['ret_out_g']).then_inc(sem["rows_loaded"], 16)
            act.dma_start(r3[84:85, 0, :], a['nsa_q_g']).then_inc(sem["rows_loaded"], 16)
            act.dma_start(r3[85:88, 0, :], a['nsa_k_g'][0]).then_inc(sem["rows_loaded"], 16)
            act.dma_start(r3[0:96, 1, :], a['ada_b'].rearrange("o (k p) -> (o k) p",
                    p=P)).then_inc(sem["rows_loaded"], 16)
            act.dma_start(r3[0:64, 2, :],
                    a['nsa_cmp_pos'][0].rearrange("w l d -> (w l) d")).then_inc(sem["rows_loaded"], 16)
            act.dma_start(xs, x0).then_inc(sem["x_loaded"], 16)
            wxv = wx.rearrange("p (k n) -> p k n", k=KT)
            act.dma_start(wxv[:, :, 0:2 * H], w_in[:, :,
                    COL['m_i']:COL['m_i'] + 2 * H]).then_inc(sem["misc_loaded"], 16)
            act.dma_start(wxv[:, :, 2 * H:NX], w_in[:, :,
                    COL['n_g']:COL['n_g'] + 3 * H]).then_inc(sem["misc_loaded"], 16)
            for f in range(2):
                act.dma_start(gb[0:H, f:f + 1], a['mlstm_gate_b'][0, f, :].unsqueeze(1),
                              allow_slow_non_contiguous=True).then_inc(sem["misc_loaded"], 16)
            act.dma_start(w2c.rearrange("p (w d) -> p w d", w=2),
                           a['nsa_cmp_w2'][0].rearrange("w e d -> e w d")).then_inc(sem["misc_loaded"], 16)
            act.dma_start(g1b[:], a['ada_b'][0:1, 2 * D:3 * D].to_broadcast([P, D])).then_inc(sem["misc_loaded"], 16)
            act.dma_start(g2b[:], a['ada_b'][0:1, 5 * D:6 * D].to_broadcast([P, D])).then_inc(sem["misc_loaded"], 16)
            act.wait_ge(sem["cols_turned"], 1)
            act.activation(cols_a[:], M[:, 0:88], ACT.Copy)
            act.activation(cols_b[:], M[:, 512:608], ACT.Copy)
            act.activation(cols_c[:], M[:, 1024:1088], ACT.Copy).then_inc(sem["cols_ready"], 1)
            act.wait_ge(sem["cols_ready"], 1)
            act.activation(cs[:, 0:16], cols_a[:, CA_C:CA_C + 16], ACT.Tanh, scale=0.5).then_inc(sem["c_tanh"], 1)
            act.wait_ge(sem["x_loaded"], 16)
            act.activation(Z[:, 0:2048], xs[:, 0, :], ACT.Square, accum_out=ssx[:, 0:1])
            act.activation(Z[:, 2048:4096], xs[:, 1, :], ACT.Square, accum_out=ssx[:,
                    1:2]).then_inc(sem["x_squared"], 1)
            for b in range(4):
                act.wait_ge(sem["xT_turned1"], b + 1)
                act.activation(buf_h[:, b * 1024:(b + 1) * 1024], W[:, (b % 2) * 1024:(b % 2) * 1024 + 1024],
                               ACT.Copy).then_inc(sem["xT_copied1"], 1)

            def ada_evacuate(n):
                item_done(act, 'ada', n)
                act.activation(ada_s[:], A[:], ACT.Copy).then_inc(sem["ada_partial"], 1)

            for n in range(len(ADA_FIRST)):
                ada_evacuate(n)
            act.wait_ge(sem["gains_ready"], 1)
            n_turn = n_att = n_chunk = 0
            for step, arg in ORDER:
                if step == 'ada':
                    ada_evacuate(arg)
                elif step == 'chunk':
                    item_done(act, 'chunk', arg)
                    if arg == 'm_v':
                        act.wait_ge(sem["turned"], 1)
                    elif arg == 'm_o':
                        act.wait_ge(sem["turned"], 2)
                    elif arg in ('b_q', 'b_k'):
                        act.wait_ge(sem["m_scores_done"], 1)
                    elif arg == 'b_v':
                        act.wait_ge(sem["o_done"], 1)
                    elif arg == 'r_q':
                        act.wait_ge(sem["scores_done"], 2)
                    elif arg == 'r_k':
                        act.wait_ge(sem["m_pv_done"], 1)
                    elif arg == 'r_v':
                        act.wait_ge(sem["o_done"], 2)
                    elif arg == 'r_g':
                        act.wait_ge(sem["y_ready_m"], 1)
                    o = (n_chunk % 2) * 1024
                    if arg in ('m_q', 'm_k'):
                        dst, src = padv[:, int(arg == 'm_k'), :, 3:T + 3], heads(W[:, o:o + 1024])
                    else:
                        dst, src = zslot[arg], W[:, o:o + 1024]
                    act.activation(dst, src, ACT.Copy).then_inc(sem["chunk_copied"], 1)
                    n_chunk += 1
                    if arg in ('m_o', 'r_g'):
                        act.wait_ge(sem["chunk_copied"], n_chunk)
                        if arg == 'm_o':
                            act.activation(zslot[arg], zslot[arg], ACT.Tanh,
                                    scale=0.5).then_inc(sem["gate_tanh_m"], 1)
                        else:
                            act.wait_ge(sem["p_turned"], 3)
                            act.activation(PA[:, 0:1024], zslot[arg], ACT.Tanh,
                                    scale=0.5).then_inc(sem["gate_tanh_r"], 1)
                elif step == 'gates':
                    act.wait_ge(sem["zx_ready"], 1)
                    act.activation(exc.rearrange("p (a n) -> p a n", a=TT),
                                   zx[:].rearrange("p (a n) -> p a n", a=TT)[:, :, 2 * H:NX],
                                   ACT.Tanh, scale=0.5).then_inc(sem["n_gate_tanh"], 1)
                    fa = PA[0:H, 2 * T:3 * T]
                    act.wait_ge(sem["f_abs"], 1)
                    act.activation(fa, fa, ACT.Exp).then_inc(sem["f_exp"], 1)
                    act.wait_ge(sem["f_one"], 1)
                    act.activation(fa, fa, ACT.Ln).then_inc(sem["f_ln"], 1)
                elif step == 'cmp_hid':
                    act.wait_ge(sem["gelu_arg"], 1)
                    act.activation(tmp[:, 0:120], tmp[:, 0:120], ACT.Tanh,
                            scale=0.7978845608028654).then_inc(sem["gelu_tanh"], 1)
                elif step == 'cmp_out':
                    act.wait_ge(sem["cmp_projected"], 1)
                    act.activation(vc[0:N_CMP], M[0:N_CMP, 512:1024], ACT.Copy).then_inc(sem["vc_ready"], 1)
                elif step == 'cmp_kT':
                    act.wait_ge(sem["kc_turned"], 1)
                    act.activation(kct[:], M[:, 0:60], ACT.Copy, scale=cols_a[:,
                            GAIN['cmp']:GAIN['cmp'] + 1]).then_inc(sem["kct_ready"], 1)
                elif step == 'cmp_scores':
                    act.wait_ge(sem["cmp_arg"], 1)
                    act.activation(PA[:, 0:120], PA[:, 0:120], ACT.Exp).then_inc(sem["cmp_e"], 1)
                elif step == 'cmp_pT':
                    act.wait_ge(sem["cmp_p_turned"], 1)
                    act.activation(PB[0:N_CMP, 0:1024], M[0:N_CMP, 0:1024], ACT.Copy).then_inc(sem["cmp_pT_ready"], 1)
                elif step == 'turn':
                    n_turn += 1
                    act.wait_ge(sem["turned"], n_turn)
                    act.activation(tslot[arg], M[:, 0:1024], ACT.Copy,
                                   scale=cols_a[:, GAIN[arg]:GAIN[arg] + 1]).then_inc(sem["turned_ready"], 1)
                elif step == 'scores':
                    n_att += 1
                    act.wait_ge(sem["nmax_ready"], n_att)
                    for h in range(H):
                        act.activation(PA[:, h * T:h * T + T], PA[:, h * T:h * T + T], ACT.Exp,
                                       bias=nmx[:, 4 + h:5 + h], accum_out=lsum[:, 4 + h:5 + h])
                        o = 1024 + h * P
                        ins = act.activation(PA[:, o:o + P], PA[:, o:o + P], ACT.Exp,
                                             bias=nmx[:, h:h + 1], accum_out=lsum[:, h:h + 1])
                    ins.then_inc(sem["exp_done"], 1)
                elif step == 'turn_p':
                    act.wait_ge(sem["p_turned"], n_att)
                    act.activation(PB[:], M[:], ACT.Copy).then_inc(sem["pT_ready"], 1)
                elif step == 'conv':
                    w = int(arg == 'm_k')
                    act.wait_ge(sem["conv_sum"], w + 1)
                    act.activation(tmp[:, 1024:2048], tslot[arg], ACT.Tanh, scale=0.5).then_inc(sem["conv_tanh"], 1)
                elif step == 'm_decay':
                    act.wait_ge(sem["m_cols_read"], 1)
                    act.activation(enm, enm, ACT.Exp).then_inc(sem["enm_ready"], 1)
                    act.wait_ge(sem["m_args_ready"], 1)
                    act.activation(PA[:], PA[:], ACT.Exp).then_inc(sem["m_decay_ready"], 1)
                elif step == 'turn_y':
                    act.wait_ge(sem[f"y_turned_{arg}"], 1)
                    g = MIX_Y[arg]
                    kw = dict(scale=cols_a[:, GAIN[arg]:GAIN[arg] + 1]) if arg in 'mr' else {}
                    act.activation(buf_x[:, g * 1024:(g + 1) * 1024], M[:, 0:1024], ACT.Copy,
                            **kw).then_inc(sem[f"yT_ready_{arg}"], 1)

            act.wait_ge(sem["x1_ready"], 4)
            act.activation(Z[:, 4096:6144], x1[:, 0, :], ACT.Square, accum_out=ssx[:, 0:1])
            act.activation(Z[:, 6144:8192], x1[:, 1, :], ACT.Square, accum_out=ssx[:,
                    1:2]).then_inc(sem["x1_squared"], 1)
            for b in range(4):
                act.wait_ge(sem["xT_turned2"], b + 1)
                for k in range(4):
                    kk = 4 * b + k
                    ins = act.activation(h2T[:, kk, :], W[:, (b % 2) * 1024 + k * T:(b % 2) * 1024 + k * T + T],
                                         ACT.Identity, scale=gsc[:, KT + kk:KT + kk + 1],
                                         bias=modc[:, 3 * KT + kk:3 * KT + kk + 1])
                ins.then_inc(sem["xT_copied2"], 1)
            act.wait_ge(sem["group_arg"], 1)
            act.activation(rt[:, 8:16], rt[:, 8:16], ACT.Exp).then_inc(sem["group_exp"], 1)
            act.wait_ge(sem["pair_arg"], 1)
            act.activation(rt[:, 24:26], rt[:, 24:26], ACT.Exp).then_inc(sem["pair_exp"], 1)

            def dress_tokens():
                for k in range(8):
                    ins = act.activation(XT[:, k, :], W[:, k * P:k * P + P], ACT.Identity,
                                         scale=gsc[:, KT + k:KT + k + 1],
                                         bias=modc[:, 3 * KT + k:3 * KT + k + 1])
                ins.then_inc(sem["xt_act"], 1)

            act.wait_ge(sem["gathered"], 1)
            dress_tokens()
            rounds = load_rounds(act)
            with act.Fori(0, rounds) as r:
                with act.Fori(0, NE // 4) as g:
                    it = 8 * r + g
                    for q in range(4):
                        act.wait_ge(half_used, PER_GROUP * it + (EXPERT_BASE + 6 * q + 4))
                        act.activation(ee, M[:, 0:128], ACT.Tanh, scale=0.5).then_inc(sem["e_ready"], 1)
                        if q == 0:
                            act.wait_ge(sem["g_turned"], it + 1)
                            act.activation(GT, M[:, 1024:1280], ACT.Copy).then_inc(sem["gt_ready"], 1)
                        act.wait_ge(sem["hh_turned"], 4 * it + q + 1)
                        act.activation(hTs, M[:, 1024:1152], ACT.Copy).then_inc(sem["hT_ready"], 1)
                        if q == 3:
                            act.wait_ge(sem["gathered"], 2 * it + 3)
                            dress_tokens()
                        act.wait_ge(half_used, PER_GROUP * it + (EXPERT_BASE + 6 * q + 6))
                        for m in range(4):
                            ins = act.activation(ysb[32 * q:32 * q + 32, 512 * m:512 * m + 512],
                                                 A[32 * m:32 * m + 32, :], ACT.Copy)
                        ins.then_inc(sem["y_copied"], 1)

        @block.vector
        def _(dve):
            chain = [0]

            def step_no():
                chain[0] += 1
                return chain[0]

            def tt_op(o, x, y, op):
                return dve.tensor_tensor(o, x, y, op)

            def mean_eps(dst, src, n):
                return dve.tensor_scalar(dst, src, 1.0 / n, EPS, ALU.mult, ALU.add)

            def half_one_plus(v):
                dve.tensor_scalar(v, v, 0.5, 0.5, ALU.mult, ALU.add).then_inc(sem["dve_step"], 1)
                dve.wait_ge(sem["dve_step"], step_no())

            def bc(v, n):
                return v.unsqueeze(2).to_broadcast([v.shape[0], v.shape[1], n])

            dve.wait_ge(sem["c_tanh"], 1)
            dve.wait_ge(sem["cols_ready"], 1)
            half_one_plus(cs[:, 0:16])
            tt_op(cs[:, 16:32], cs[:, 0:16], cols_a[:, CA_C:CA_C + 16], ALU.mult).then_inc(sem["dve_step"], 1)
            dve.wait_ge(sem["dve_step"], step_no())
            dve.tensor_copy(csil[:].rearrange("p (k j) -> p k j", j=32), bc(cs[:, 16:32],
                    32)).then_inc(sem["csil_ready"], 1)
            for q in ('b_q', 'n_q'):
                g = cols_a[:, GAIN[q]:GAIN[q] + 1]
                ins = dve.tensor_scalar(g, g, QSCALE, None, ALU.mult)
            ins.then_inc(sem["gains_ready"], 1)
            dve.wait_ge(sem["x_squared"], 1)
            mean_eps(rsx, ssx, D).then_inc(sem["x_ms"], 1)
            dve.wait_ge(sem["x_rstd"], 1)
            dve.tensor_scalar(xs[:, 0, :], xs[:, 0, :], rsx[:, 0:1], None, ALU.mult)
            dve.tensor_scalar(xs[:, 1, :], xs[:, 1, :], rsx[:, 1:2], None, ALU.mult).then_inc(sem["xhat_ready1"], 1)

            def ada_finish(n):
                part, c = ADA[n] // 4, ADA[n] % 4
                dve.wait_ge(sem["ada_summed"], n + 1)
                if part in (2, 5):
                    gv = (g1b if part == 2 else g2b)[:, 512 * c:512 * c + 512]
                    dve.wait_ge(sem["misc_loaded"], 16 * 7)
                    tt_op(gv, A[:], gv, ALU.add).then_inc(sem["ada_combined"], 1)
                    return
                o = {1: 0, 0: KT, 4: 2 * KT, 3: 3 * KT}[part] + 4 * c
                tt_op(modc[:, o:o + 4], A[:, 0:4], cols_b[:,
                        16 * part + 4 * c:16 * part + 4 * c + 4], ALU.add).then_inc(sem["ada_combined"], 1)
                if part in (0, 3):
                    sub = int(part == 3)
                    dve.wait_ge(sem["ada_combined"], n + 1)
                    dve.scalar_tensor_tensor(gsc[:, KT * sub + 4 * c:KT * sub + 4 * c + 4],
                                             modc[:, 2 * KT * sub + 4 * c:2 * KT * sub + 4 * c + 4], 1.0,
                                             cols_a[:, CA_N1 + 16 * sub + 4 * c:CA_N1 + 16 * sub + 4 * c + 4],
                                             ALU.add, ALU.mult).then_inc(sem["dve_step"], 1)
                    dve.wait_ge(sem["dve_step"], step_no())
                if part == 0:
                    dve.wait_ge(sem["xT_copied1"], c + 1)
                    for k in range(4 * c, 4 * c + 4):
                        ins = dve.tensor_scalar(hT[:, k, :], hT[:, k, :], gsc[:, k:k + 1],
                                                modc[:, KT + k:KT + k + 1], ALU.mult, ALU.add)
                    ins.then_inc(sem["h_ready"], 1)

            for n in range(len(ADA_FIRST)):
                ada_finish(n)

            def out_norm(who, hs):
                tt_op(tmp[:, 0:1024], hs, hs, ALU.mult).then_inc(sem["dve_step"], 1)
                dve.wait_ge(sem["dve_step"], step_no())
                dve.tensor_reduce(ssy, tth(tmp[:, 0:1024]), AX, ALU.add).then_inc(sem["dve_step"], 1)
                dve.wait_ge(sem["dve_step"], step_no())
                mean_eps(rsy, ssy, DH).then_inc(sem[f"y_{who}_ms"], 1)
                dve.wait_ge(sem[f"gate_tanh_{who}"], 1)
                gv = zslot['m_o'] if who == 'm' else PA[:, 0:1024]
                half_one_plus(gv)
                if who == 'r':
                    tt_op(gv, gv, zslot['r_g'], ALU.mult).then_inc(sem["dve_step"], 1)
                    dve.wait_ge(sem["dve_step"], step_no())
                dve.wait_ge(sem[f"y_{who}_rstd"], 1)
                tt_op(tth(hs), tth(hs), bc(rsy, DH), ALU.mult).then_inc(sem["dve_step"], 1)
                dve.wait_ge(sem["dve_step"], step_no())
                tt_op(yb[:], hs, gv, ALU.mult).then_inc(sem[f"y_ready_{who}"], 1)

            sgv = sgn[:].rearrange("p (a n) -> p a n", a=TT)
            n_att = 0
            for step, arg in ORDER:
                if step == 'ada_sum':
                    ada_finish(arg)
                elif step == 'extras':
                    dve.wait_ge(sem["extras_done"], 1)
                    dve.tensor_copy(zx[:].rearrange("p (a n) -> p a n", a=TT),
                                    M[:, 0:1024].rearrange("p (a n) -> p a n", a=TT)[:, :,
                                            0:NX]).then_inc(sem["zx_ready"], 1)
                elif step == 'gates':
                    dve.wait_ge(sem["gates_turned"], 1)
                    dve.wait_ge(sem["misc_loaded"], 16 * 7)
                    ip, fp, fa, zeros = (PA[0:H, i * T:(i + 1) * T] for i in range(4))
                    dve.memset(zeros, 0.0).then_inc(sem["dve_step"], 1)
                    dve.wait_ge(sem["dve_step"], step_no())
                    dve.tensor_scalar(ip, M[0:H, 0:T], gb[0:H, 0:1], None, ALU.add)
                    dve.tensor_scalar(fp, M[0:H, T:2 * T], gb[0:H, 1:2], None, ALU.add).then_inc(sem["gates_read"], 1)
                    dve.wait_ge(sem["gates_read"], 1)
                    dve.scalar_tensor_tensor(fa, fp, -1.0, fp, ALU.mult, ALU.min).then_inc(sem["f_abs"], 1)
                    dve.wait_ge(sem["n_gate_tanh"], 1)
                    dve.tensor_scalar(sgn[:], exc, 0.5, 0.5, ALU.mult, ALU.add).then_inc(sem["dve_step"], 1)
                    dve.wait_ge(sem["dve_step"], step_no())
                    dve.wait_ge(sem["f_exp"], 1)
                    dve.tensor_scalar(fa, fa, 1.0, None, ALU.add).then_inc(sem["f_one"], 1)
                    dve.wait_ge(sem["f_ln"], 1)
                    dve.scalar_tensor_tensor(fa, fp, 0.0, fa, ALU.min, ALU.subtract).then_inc(sem["dve_step"], 1)
                    dve.wait_ge(sem["dve_step"], step_no())
                    dve.tensor_tensor_scan(fp, fa, zeros, 0.0, ALU.add, ALU.add).then_inc(sem["dve_step"], 1)
                    dve.wait_ge(sem["dve_step"], step_no())
                    b_row = gat[0:H, 0:T]
                    tt_op(b_row, ip, fp, ALU.subtract).then_inc(sem["dve_step"], 1)
                    dve.wait_ge(sem["dve_step"], step_no())
                    dve.tensor_tensor_scan(fa, b_row, b_row, 0.0, ALU.max, ALU.max).then_inc(sem["dve_step"], 1)
                    dve.wait_ge(sem["dve_step"], step_no())
                    dve.scalar_tensor_tensor(gat[0:H, T:2 * T], fa, -1.0, fp, ALU.mult,
                            ALU.subtract).then_inc(sem["dve_step"], 1)
                    dve.wait_ge(sem["dve_step"], step_no())
                    dve.tensor_scalar(gat[0:H, T:2 * T], gat[0:H, T:2 * T], 87.0, None, ALU.min)
                    dve.tensor_scalar(gat[0:H, 2 * T:3 * T], fa, -1.0, None,
                            ALU.mult).then_inc(sem["gate_rows_ready"], 1)
                elif step == 'cmp_hid':
                    for w in range(2):
                        dve.wait_ge(sem["chunk_copied"], chunk_no(('n_kc', 'n_vc')[w]))
                        src = zslot[('n_kc', 'n_vc')[w]].rearrange("p (h n l) -> p l h n", h=H, l=16)
                        dst = blk[w].rearrange("p (l h n) -> p l h n", l=CMP_LEN, h=H)
                        for lh in range(2):
                            pe_c = cols_c[:, 32 * w + 16 * lh:32 * w + 16 * lh + 16].unsqueeze(2).unsqueeze(3)
                            ins = tt_op(dst[:, 16 * lh:16 * lh + 16], src[:, :, :, lh:lh + N_CMP],
                                        pe_c.to_broadcast([P, 16, H, N_CMP]), ALU.add)
                        ins.then_inc(sem["blocks_ready"], 1)
                    item_done(dve, 'cmp', 0)
                    dve.tensor_copy(hid[:].rearrange("p (w n) -> p w n", w=2),
                                    M[:, 0:1024].rearrange("p (w n) -> p w n", w=2)[:, :,
                                            0:60]).then_inc(sem["hid_read"], 1)
                    dve.wait_ge(sem["hid_read"], 1)
                    u, v = tmp[:, 0:120], tmp[:, 128:248]
                    tt_op(v, hid[:], hid[:], ALU.mult).then_inc(sem["dve_step"], 1)
                    dve.wait_ge(sem["dve_step"], step_no())
                    dve.tensor_scalar(v, v, 0.044715, 1.0, ALU.mult, ALU.add).then_inc(sem["dve_step"], 1)
                    dve.wait_ge(sem["dve_step"], step_no())
                    tt_op(u, v, hid[:], ALU.mult).then_inc(sem["gelu_arg"], 1)
                    dve.wait_ge(sem["gelu_tanh"], 1)
                    half_one_plus(u)
                    tt_op(hid[:], hid[:], u, ALU.mult).then_inc(sem["hid_ready"], 1)
                elif step == 'cmp_out':
                    kc, sq = tmp[0:60, 1024:1152], tmp[0:60, 1152:1280]
                    dve.wait_ge(sem["cmp_projected"], 1)
                    dve.tensor_copy(kc, M[0:60, 0:DH]).then_inc(sem["kc_read"], 1)
                    dve.wait_ge(sem["kc_read"], 1)
                    tt_op(sq, kc, kc, ALU.mult).then_inc(sem["dve_step"], 1)
                    dve.wait_ge(sem["dve_step"], step_no())
                    dve.tensor_reduce(ssc[0:60, :], sq, AX, ALU.add).then_inc(sem["dve_step"], 1)
                    dve.wait_ge(sem["dve_step"], step_no())
                    mean_eps(rsc[0:60, :], ssc[0:60, :], DH).then_inc(sem["kc_ms"], 1)
                    dve.wait_ge(sem["kc_rstd"], 1)
                    dve.tensor_scalar(kc, kc, rsc[0:60, :], None, ALU.mult).then_inc(sem["kc_normed"], 1)
                elif step == 'cmp_scores':
                    s = PA[:, 0:120]
                    s3 = s.rearrange("p (a n) -> p a n", n=N_CMP)
                    dve.wait_ge(sem["cmp_scores_done"], 1)
                    tt_op(s, M[:, 0:120], const('cmp_bias'), ALU.add).then_inc(sem["cmp_scores_read"], 1)
                    dve.wait_ge(sem["cmp_scores_read"], 1)
                    dve.tensor_reduce(cmx, s3, AX, ALU.max).then_inc(sem["dve_step"], 1)
                    dve.wait_ge(sem["dve_step"], step_no())
                    tt_op(s3, s3, bc(cmx, N_CMP), ALU.subtract).then_inc(sem["cmp_arg"], 1)
                    dve.wait_ge(sem["cmp_e"], 1)
                    tt_op(s, s, const('cmp_ok'), ALU.mult).then_inc(sem["cmp_exp"], 1)
                    dve.wait_ge(sem["cmp_exp"], 1)
                    dve.tensor_reduce(csum, s3, AX, ALU.add).then_inc(sem["dve_step"], 1)
                    dve.wait_ge(sem["dve_step"], step_no())
                    dve.tensor_scalar(csum, csum, 1e-30, None, ALU.max).then_inc(sem["dve_step"], 1)
                    dve.wait_ge(sem["dve_step"], step_no())
                    dve.reciprocal(cf, csum).then_inc(sem["dve_step"], 1)
                    dve.wait_ge(sem["dve_step"], step_no())
                    cf2 = cf.rearrange("p (a h) -> p a h", a=TT)
                    tt_op(cf2, cf2, sgv[:, :, 0:H], ALU.mult).then_inc(sem["dve_step"], 1)
                    dve.wait_ge(sem["dve_step"], step_no())
                elif step == 'cmp_pv':
                    dve.wait_ge(sem["cmp_pv_done"], 1)
                    tt_op(tth(yb[:]), tth(M[:, 0:1024]), bc(cf, DH), ALU.mult).then_inc(sem["cmp_y"], 1)
                elif step == 'norm':
                    z = zslot[arg]
                    dve.wait_ge(sem["chunk_copied"], chunk_no(arg))
                    tt_op(tmp[:, 0:1024], z, z, ALU.mult).then_inc(sem["dve_step"], 1)
                    dve.wait_ge(sem["dve_step"], step_no())
                    dve.tensor_reduce(ss, tth(tmp[:, 0:1024]), AX, ALU.add).then_inc(sem["dve_step"], 1)
                    dve.wait_ge(sem["dve_step"], step_no())
                    mean_eps(rst, ss, DH).then_inc(sem[f"norm_{arg}_ms"], 1)
                    dve.wait_ge(sem[f"norm_{arg}_rstd"], 1)
                    tt_op(tth(z), tth(z), bc(rst, DH), ALU.mult).then_inc(sem["normed"], 1)
                elif step == 'scores':
                    n_att += 1
                    al = alibi[:, int(arg != 'moba')]
                    dve.wait_ge(sem["scores_done"], n_att)
                    tt_op(heads(PA[:, 0:1024]), heads(M[:, 0:1024]), al, ALU.add).then_inc(sem["dve_step"], 1)
                    dve.wait_ge(sem["dve_step"], step_no())
                    tt_op(heads(PA[:, 1024:1536]), heads(M[:, 1024:1536]), al[:, :, P:T],
                            ALU.add).then_inc(sem["scores_read"], 1)
                    dve.tensor_reduce(mx[:, 4:8], heads(PA[:, 0:1024]), AX, ALU.max).then_inc(sem["dve_step"], 1)
                    dve.wait_ge(sem["dve_step"], step_no())
                    dve.wait_ge(sem["scores_read"], n_att)
                    dve.tensor_reduce(mx[:, 0:4], heads(PA[:, 1024:1536]), AX, ALU.max).then_inc(sem["dve_step"], 1)
                    dve.wait_ge(sem["dve_step"], step_no())
                    dve.tensor_scalar(nmx, mx, -1.0, None, ALU.mult).then_inc(sem["nmax_ready"], 1)
                elif step == 'pv':
                    dve.wait_ge(sem["exp_done"], n_att)
                    dve.reciprocal(fac, lsum).then_inc(sem["dve_step"], 1)
                    dve.wait_ge(sem["dve_step"], step_no())
                    if arg != 'moba':
                        br = {'slc': 1, 'win': 2}[arg]
                        f2 = fac.rearrange("p (a h) -> p a h", a=TT)
                        tt_op(f2, f2, sgv[:, :, br * H:br * H + H], ALU.mult).then_inc(sem["dve_step"], 1)
                        dve.wait_ge(sem["dve_step"], step_no())
                    dve.wait_ge(sem["o_done"], n_att)
                    if arg == 'moba':
                        tt_op(tth(yb[:]), tth(M[:, 0:1024]), bc(fac, DH), ALU.mult).then_inc(sem["y_ready_b"], 1)
                    else:
                        tt_op(tth(tmp[:, 0:1024]), tth(M[:, 0:1024]), bc(fac, DH),
                                ALU.mult).then_inc(sem["o_read"], 1)
                        dve.wait_ge(sem["o_read"], n_att)
                        ins = tt_op(yb[:], yb[:], tmp[:, 0:1024], ALU.add)
                        if arg == 'win':
                            ins.then_inc(sem["y_ready_n"], 1)
                            dve.tensor_copy(hsel[0:H, :].rearrange("p (h t) -> p h t", h=H),
                                            bc(ident[0:H, 0:H], P)).then_inc(sem["hsel_ready"], 1)
                        else:
                            ins.then_inc(sem["dve_step"], 1)
                            dve.wait_ge(sem["dve_step"], step_no())
                elif step == 'conv':
                    w = int(arg == 'm_k')
                    acc, pd = heads(tslot[arg]), padv[:, w]
                    if w == 0:
                        item_done(dve, 'cmp', 0)
                        dve.memset(padv[:, :, :, 0:3].rearrange("p w h t -> p (w h) t"),
                                0.0).then_inc(sem["dve_step"], 1)
                        dve.wait_ge(sem["dve_step"], step_no())
                    dve.wait_ge(sem["chunk_copied"], chunk_no(arg))
                    for j in (3, 2, 1, 0):
                        for h in range(H):
                            o = CA_CONV + 8 * j + 4 * w + h
                            cw = cols_a[:, o:o + 1]
                            if j == 3:
                                ins = dve.tensor_scalar(acc[:, h], pd[:, h, 3:3 + T], cw, None, ALU.mult)
                            else:
                                ins = dve.scalar_tensor_tensor(acc[:, h], pd[:, h, j:j + T], cw, acc[:, h],
                                                               ALU.mult, ALU.add)
                            if (j, h) != (0, H - 1) and h == H - 1:
                                ins.then_inc(sem["dve_step"], 1)
                                dve.wait_ge(sem["dve_step"], step_no())
                    ins.then_inc(sem["conv_sum"], 1)
                    dve.wait_ge(sem["conv_tanh"], w + 1)
                    e = tmp[:, 1024:2048]
                    half_one_plus(e)
                    dve.scalar_tensor_tensor(tslot[arg], tslot[arg], 1.0 if w else QSCALE, e,
                                             ALU.mult, ALU.mult).then_inc(sem["conv_done"], 1)
                elif step == 'm_decay':
                    dve.wait_ge(sem["m_cols_turned"], 1)
                    dve.tensor_copy(bcol_enm, M[:, 0:16]).then_inc(sem["m_cols_read"], 1)
                    dve.wait_ge(sem["m_cols_read"], 1)
                    dve.wait_ge(sem["negmask_loaded"], 16)
                    nm = negmask
                    for h in range(H):
                        o = 512 + h * T
                        dve.scalar_tensor_tensor(PA[:, h * T:h * T + T], M[:, o:o + T], bcol[:, h:h + 1], nm,
                                                 ALU.add, ALU.add)
                        ins = dve.scalar_tensor_tensor(PA[:, 1024 + h * P:1024 + h * P + P], M[:, o + P:o + T],
                                                       bcol[:, 4 + h:5 + h], nm[:, 0:P], ALU.add, ALU.add)
                    ins.then_inc(sem["m_args_ready"], 1)
                elif step == 'm_scores':
                    dve.wait_ge(sem["m_decay_ready"], 1)
                    dve.wait_ge(sem["m_scores_done"], 1)
                    tt_op(PB[:], M[:], PA[:], ALU.mult).then_inc(sem["m_p_ready"], 1)
                elif step == 'm_pv':
                    dve.wait_ge(sem["enm_ready"], 1)
                    dve.wait_ge(sem["m_pv_done"], 1)
                    dve.tensor_copy(den, M[:, 1024:1032]).then_inc(sem["dve_step"], 1)
                    dve.wait_ge(sem["dve_step"], step_no())
                    dve.scalar_tensor_tensor(den, den, -1.0, den, ALU.mult, ALU.max).then_inc(sem["dve_step"], 1)
                    dve.wait_ge(sem["dve_step"], step_no())
                    tt_op(den, den, enm, ALU.max).then_inc(sem["dve_step"], 1)
                    dve.wait_ge(sem["dve_step"], step_no())
                    dve.reciprocal(den, den).then_inc(sem["dve_step"], 1)
                    dve.wait_ge(sem["dve_step"], step_no())
                    hs = tmp[:, 1024:2048]
                    tt_op(tth(hs), tth(M[:, 0:1024]), bc(den, DH), ALU.mult).then_inc(sem["m_o_read"], 1)
                    dve.wait_ge(sem["m_o_read"], 1)
                    out_norm('m', hs)
                elif step == 'r_scores':
                    dve.wait_ge(sem["decay_loaded"], 16)
                    dve.wait_ge(sem["r_scores_done"], 1)
                    dve.tensor_tensor(heads(PB[:, 0:1024]), heads(M[:, 0:1024]), decay, ALU.mult)
                    tt_op(heads(PB[:, 1024:1536]), heads(M[:, 1024:1536]), decay[:, :, 0:P],
                            ALU.mult).then_inc(sem["r_p_ready"], 1)
                elif step == 'r_pv':
                    dve.wait_ge(sem["r_pv_done"], 1)
                    hs = tmp[:, 1024:2048]
                    dve.tensor_copy(hs, M[:, 0:1024]).then_inc(sem["r_o_read"], 1)
                    dve.wait_ge(sem["r_o_read"], 1)
                    out_norm('r', hs)

            dve.wait_ge(sem["x_again"], 16)
            for n in range(D // 512):
                item_done(dve, 'wout', n)
                if n > 0:
                    dve.wait_ge(sem["x1_ready"], n)
                o = (n % 2) * 1024
                t3 = tmp[:, 0:1024].rearrange("p (a d) -> p a d", a=TT)
                tt_op(t3, W[:, o:o + 1024].rearrange("p (a d) -> p a d", a=TT),
                      g1b[:, 512 * n:512 * n + 512].unsqueeze(1).to_broadcast([P, TT, 512]),
                              ALU.mult).then_inc(sem["dve_step"], 1)
                dve.wait_ge(sem["dve_step"], step_no())
                xo = x1[:, :, 512 * n:512 * n + 512]
                tt_op(xo, xo, t3, ALU.add).then_inc(sem["x1_ready"], 1)
            dve.wait_ge(sem["x1_squared"], 1)
            mean_eps(rsx, ssx, D).then_inc(sem["x1_ms"], 1)
            dve.wait_ge(sem["x1_rstd"], 1)
            dve.tensor_scalar(xs[:, 0, :], x1[:, 0, :], rsx[:, 0:1], None, ALU.mult)
            dve.tensor_scalar(xs[:, 1, :], x1[:, 1, :], rsx[:, 1:2], None, ALU.mult).then_inc(sem["xhat_ready2"], 1)

            L = lg.rearrange("p (a n) -> p a n", a=TT)
            Lg, Le = L[:, :, 0:NG], L[:, :, NG:36].rearrange("p a (g j) -> p a g j", g=NG)
            dve.tensor_scalar(jdesc, const('iota'), -1.0, 32.0, ALU.mult, ALU.add)
            dve.wait_ge(sem["router_loaded"], 64)
            dve.wait_ge(sem["router_done"], 1)
            tt_op(L, M[:, 0:1024].rearrange("p (a n) -> p a n", a=TT)[:, :, 0:36],
                  rb[:].unsqueeze(1).to_broadcast([P, TT, 36]), ALU.add).then_inc(sem["dve_step"], 1)
            dve.wait_ge(sem["dve_step"], step_no())

            def first_maximum(dst, vals, top, n):
                t = tie[:, 0:TT * n].rearrange("p (a n) -> p a n", a=TT)
                dve.tensor_reduce(top, vals, AX, ALU.max).then_inc(sem["dve_step"], 1)
                dve.wait_ge(sem["dve_step"], step_no())
                tt_op(dst, vals, bc(top, n), ALU.is_equal).then_inc(sem["dve_step"], 1)
                dve.wait_ge(sem["dve_step"], step_no())
                tt_op(t, dst, jdesc[:, 0:n].unsqueeze(1).to_broadcast([P, TT, n]),
                        ALU.mult).then_inc(sem["dve_step"], 1)
                dve.wait_ge(sem["dve_step"], step_no())
                dve.tensor_reduce(rt[:, 38:40], t, AX, ALU.max).then_inc(sem["dve_step"], 1)
                dve.wait_ge(sem["dve_step"], step_no())
                tt_op(dst, t, bc(rt[:, 38:40], n), ALU.is_equal).then_inc(sem["dve_step"], 1)
                dve.wait_ge(sem["dve_step"], step_no())

            og = ohg[:, 0:TT * NG].rearrange("p (a n) -> p a n", a=TT)
            first_maximum(og, Lg, rt[:, 0:2], NG)
            eg = rt[:, 8:16].rearrange("p (a n) -> p a n", a=TT)
            tt_op(eg, Lg, bc(rt[:, 0:2], NG), ALU.subtract).then_inc(sem["group_arg"], 1)
            mp = mprod.rearrange("p (a g j) -> p a g j", a=TT, g=NG)
            ogb = og.unsqueeze(3).to_broadcast([P, TT, NG, EPG])
            tt_op(mp, Le, ogb, ALU.mult).then_inc(sem["dve_step"], 1)
            dve.wait_ge(sem["dve_step"], step_no())
            lev = le_g[:, 0:16].rearrange("p (a j) -> p a j", a=TT)
            dve.tensor_reduce(lev, mp.rearrange("p a g j -> p a j g"), AX, ALU.add).then_inc(sem["dve_step"], 1)
            dve.wait_ge(sem["dve_step"], step_no())
            o1, o2, l2 = (v[:, 0:16].rearrange("p (a j) -> p a j", a=TT) for v in (oh1, oh2, le2))
            first_maximum(o1, lev, rt[:, 2:4], EPG)
            dve.scalar_tensor_tensor(l2, o1, NEG, lev, ALU.mult, ALU.add).then_inc(sem["dve_step"], 1)
            dve.wait_ge(sem["dve_step"], step_no())
            first_maximum(o2, l2, rt[:, 4:6], EPG)
            tt_op(rt[:, 24:26], rt[:, 4:6], rt[:, 2:4], ALU.subtract).then_inc(sem["pair_arg"], 1)
            dve.wait_ge(sem["group_exp"], 1)
            dve.tensor_reduce(rt[:, 16:18], eg, AX, ALU.add).then_inc(sem["dve_step"], 1)
            dve.wait_ge(sem["dve_step"], step_no())
            dve.reciprocal(rt[:, 18:20], rt[:, 16:18]).then_inc(sem["dve_step"], 1)
            dve.wait_ge(sem["dve_step"], step_no())
            dve.wait_ge(sem["pair_exp"], 1)
            dve.tensor_scalar(rt[:, 26:28], rt[:, 24:26], 1.0, None, ALU.add).then_inc(sem["dve_step"], 1)
            dve.wait_ge(sem["dve_step"], step_no())
            dve.reciprocal(rt[:, 28:30], rt[:, 26:28]).then_inc(sem["dve_step"], 1)
            dve.wait_ge(sem["dve_step"], step_no())
            tt_op(rt[:, 30:32], rt[:, 28:30], rt[:, 18:20], ALU.mult).then_inc(sem["dve_step"], 1)
            dve.wait_ge(sem["dve_step"], step_no())
            tt_op(rt[:, 32:34], rt[:, 30:32], rt[:, 24:26], ALU.mult).then_inc(sem["dve_step"], 1)
            dve.wait_ge(sem["dve_step"], step_no())
            both = w12.rearrange("p (a j) -> p a j", a=TT)
            tt_op(lev, o1, bc(rt[:, 30:32], EPG), ALU.mult).then_inc(sem["dve_step"], 1)
            dve.wait_ge(sem["dve_step"], step_no())
            tt_op(l2, o2, bc(rt[:, 32:34], EPG), ALU.mult).then_inc(sem["dve_step"], 1)
            dve.wait_ge(sem["dve_step"], step_no())
            tt_op(lev, lev, l2, ALU.add).then_inc(sem["dve_step"], 1)
            dve.wait_ge(sem["dve_step"], step_no())
            tt_op(both, o1, o2, ALU.add).then_inc(sem["dve_step"], 1)
            dve.wait_ge(sem["dve_step"], step_no())
            shp = [P, TT, NG, EPG]
            pos3 = pos.rearrange("p (a n) -> p a n", a=TT)
            gate3 = gate.rearrange("p (a n) -> p a n", a=TT)
            tt_op(gate3[:, :, 0:NE].rearrange("p a (g j) -> p a g j", g=NG), ogb, lev.unsqueeze(2).to_broadcast(shp),
                  ALU.mult).then_inc(sem["dve_step"], 1)
            dve.wait_ge(sem["dve_step"], step_no())
            tt_op(mask.rearrange("p (a g j) -> p a g j", a=TT, g=NG), ogb, both.unsqueeze(2).to_broadcast(shp),
                  ALU.mult).then_inc(sem["mask_ready"], 1)
            dve.wait_ge(sem["places_done"], 1)
            tt_op(pos3[:, :, 0:NE], M[:, 0:1024].rearrange("p (a n) -> p a n", a=TT)[:, :, 0:NE],
                  mask.rearrange("p (a n) -> p a n", a=TT), ALU.mult).then_inc(sem["dve_step"], 1)
            dve.wait_ge(sem["dve_step"], step_no())
            dve.tensor_scalar(pos3[:, :, NE:NE + 4], pos3[:, :, 0:4], -33.0, None, ALU.add)
            dve.tensor_copy(gate3[:, :, NE:NE + 4], gate3[:, :, 0:4]).then_inc(sem["dve_step"], 1)
            dve.wait_ge(sem["dve_step"], step_no())
            dve.tensor_scalar(pos3[:, :, 0:NE], pos3[:, :, 0:NE], -1.0, None, ALU.add).then_inc(sem["dve_step"], 1)
            dve.wait_ge(sem["dve_step"], step_no())
            iob = const('iota').unsqueeze(1).unsqueeze(1).to_broadcast([P, TT, 4, 32])

            def column(v, g):
                return v[:, :, bass.ds(4 * g, 4)].unsqueeze(3).to_broadcast([P, TT, 4, 32])

            def dress_tokens():
                for k in range(8, KT):
                    ins = dve.tensor_scalar(XT[:, k, :], W[:, k * P:k * P + P], gsc[:, KT + k:KT + k + 1],
                                            modc[:, 3 * KT + k:3 * KT + k + 1], ALU.mult, ALU.add)
                ins.then_inc(sem["xt_dve"], 1)

            tt_op(Gm, column(pos3, 0), iob, ALU.is_equal).then_inc(sem["dve_step"], 1)
            dve.wait_ge(sem["dve_step"], step_no())
            tt_op(Gg, Gm, column(gate3, 0), ALU.mult).then_inc(sem["g_ready"], 1)
            dve.tensor_reduce(rt[:, 34:35], M[:, 1024:1024 + NE], AX, ALU.max).then_inc(sem["dve_step"], 1)
            dve.wait_ge(sem["dve_step"], step_no())
            dve.tensor_scalar(cnt_i[:], rt[:, 34:35], 31.0, None, ALU.add).then_inc(sem["dve_step"], 1)
            dve.wait_ge(sem["dve_step"], step_no())
            dve.tensor_scalar(cnt_i[:], cnt_i[:], 5, None, ALU.logical_shift_right).then_inc(sem["rounds_ready"], 1)
            dve.wait_ge(sem["gathered"], 2)
            dress_tokens()

            def add_scattered(n):
                for tt in range(TT):
                    dve.wait_ge(sem["scattered"], 2 * n + tt + 1)
                    dve.wait_ge(sem["y_added"], 2 * n + tt + 1)
                    tt_op(yacc[:, tt, :], W[:], yacc[:, tt, :], ALU.add).then_inc(sem["y_added"], 1)

            rounds = load_rounds(dve)
            LINKS = 1 + 4
            with dve.Fori(0, rounds) as r:
                with dve.Fori(0, NE // 4) as g:
                    it = 8 * r + g
                    count = [0]

                    def loop_step_no():
                        count[0] += 1
                        return LINKS * it + count[0]

                    for q in range(4):
                        dve.wait_ge(sem["e_ready"], 4 * it + q + 1)
                        dve.scalar_tensor_tensor(aa, ee, 1.0, M[:, 0:128], ALU.add, ALU.mult).then_inc(
                            sem["dve_loop_step"], 1)
                        dve.wait_ge(sem["dve_loop_step"], loop_step_no())
                        dve.scalar_tensor_tensor(hh, M[:, 512:640], 0.5, aa, ALU.mult, ALU.mult).then_inc(
                            sem["hh_ready"], 1)
                        if q == 0:
                            add_scattered(it)
                            dve.wait_ge(sem["g_turned"], it + 1)
                            tt_op(Gm, column(pos3, g + 1), iob, ALU.is_equal).then_inc(sem["dve_loop_step"], 1)
                            dve.wait_ge(sem["dve_loop_step"], loop_step_no())
                            tt_op(Gg, Gm, column(gate3, g + 1), ALU.mult).then_inc(sem["g_ready"], 1)
                        elif q == 3:
                            dve.wait_ge(sem["gathered"], 2 * it + 4)
                            dress_tokens()
                    assert count[0] == LINKS
                dve.tensor_scalar(pos, pos, -32.0, None, ALU.add).then_inc(sem["round_shifted"], 1)
                dve.wait_ge(sem["round_shifted"], r + 1)
            add_scattered(8 * rounds)
            for tt in range(TT):
                tt_op(yacc[:, tt, :], yacc[:, tt, :], g2b[:], ALU.mult).then_inc(sem["dve_step"], 1)
                dve.wait_ge(sem["dve_step"], step_no())
                tt_op(yacc[:, tt, :], yacc[:, tt, :], x1[:, tt, :], ALU.add).then_inc(sem["out_ready"], 1)


INPUTS = ('x', 'c', 'norm1_g', 'norm2_g', 'ada_w', 'ada_b', 'w_in', 'mlstm_gate_b', 'mlstm_conv_w', 'mlstm_out_g',
          'moba_qk_g', 'ret_out_g', 'nsa_q_g', 'nsa_k_g', 'nsa_cmp_pos', 'nsa_cmp_w1', 'nsa_cmp_w2', 'w_out',
          'router_g_w', 'router_g_b', 'router_e_w', 'router_e_b', 'exp_w1', 'exp_w3', 'exp_w2')


def kernel(**inputs):
    import concourse.bacc as bacc
    from concourse.bass_utils import run_bass_kernel_spmd

    nc = bacc.Bacc("TRN2", target_bir_lowering=False, num_devices=1)
    arrays = {f"in_{n}": np.ascontiguousarray(inputs[n]) for n in INPUTS}
    arrays["in_consts"] = constants()
    aps = {n[3:]: nc.dram_tensor(n, v.shape, F32, kind="ExternalInput").ap() for n, v in arrays.items()}
    out = nc.dram_tensor("out", (1, T, D), F32, kind="ExternalOutput").ap()
    build_program(nc, aps, out)
    return run_bass_kernel_spmd(nc, [arrays], core_ids=[0]).results[0]["out"]
```

```python
from contextlib import ExitStack

import numpy as np

import concourse.bass as bass
from concourse import mybir

F32 = mybir.dt.float32
I32 = mybir.dt.int32
ALU = mybir.AluOpType
ACT = mybir.ActivationFunctionType
AX = mybir.AxisListType.X

P = 128
D = 2048
T = 256
TT = T // P
KT = D // P
H = 4
DH = 128
GW = H * DH
NE = 32
NG = 4
EPG = NE // NG
DE = 512
N_CMP = T // 16 - 1
CMP_LEN = 32
EPS = 1e-6
NEG = -1e30
QSCALE = float(DH) ** -0.5

LAYOUT = (('m_q', GW), ('m_k', GW), ('m_v', GW), ('m_o', GW), ('m_i', H), ('m_f', H),
          ('b_q', GW), ('b_k', GW), ('b_v', GW), ('r_q', GW), ('r_k', GW), ('r_v', GW), ('r_g', GW),
          ('n_q', GW), ('n_kc', GW), ('n_vc', GW), ('n_ks', GW), ('n_vs', GW), ('n_kw', GW), ('n_vw', GW),
          ('n_g', 3 * H))
COL = {}
_o = 0
for _n, _w in LAYOUT:
    COL[_n] = _o
    _o += _w
NX = 2 * H + 3 * H

CONST = {}
_o = 0
for _n, _w in (('ident', P), ('tri', P), ('ones', P), ('sel4', P), ('iota', 32),
               ('cmp_bias', TT * H * N_CMP), ('cmp_ok', TT * H * N_CMP), ('alibi', 8 * T),
               ('decay', H * T), ('negmask', T)):
    CONST[_n] = (_o, _w)
    _o += _w
NCONST = _o
N_FIRST = CONST['alibi'][0]
N_EARLY = CONST['decay'][0]

ADA_FIRST = [4, 0, 5, 1, 6, 2, 7, 3]
ADA_LATER = [16, 12, 17, 13, 18, 14, 19, 15, 8, 9, 10, 11, 20, 21, 22, 23]
ADA = ADA_FIRST + ADA_LATER
ORDER = [('chunk', 'n_kc'), ('extras', 0), ('ada', 8),
         ('chunk', 'n_vc'), ('gates', 0),
         ('chunk', 'n_q'), ('cmp_hid', 0), ('norm', 'n_q'), ('ada', 9),
         ('chunk', 'n_ks'), ('cmp_out', 0), ('turn', 'n_q'), ('norm', 'n_ks'), ('ada', 10),
         ('chunk', 'n_vs'), ('cmp_kT', 0), ('cmp_scores', 0), ('turn', 'n_ks'), ('ada', 11),
         ('chunk', 'n_kw'), ('cmp_pT', 0), ('cmp_pv', 0), ('scores', 'slc'), ('norm', 'n_kw'), ('ada', 12),
         ('chunk', 'n_vw'), ('turn', 'n_kw'), ('turn_p', 'slc'), ('ada', 13),
         ('chunk', 'm_q'), ('pv', 'slc'), ('ada', 14), ('conv', 'm_q'),
         ('chunk', 'm_k'), ('scores', 'win'), ('ada', 15), ('conv', 'm_k'),
         ('chunk', 'm_v'), ('turn_p', 'win'), ('pv', 'win'), ('ada', 16),
         ('chunk', 'm_o'), ('ada', 17),
         ('chunk', 'b_v'), ('m_decay', 0), ('ada', 18),
         ('chunk', 'r_v'), ('turn_y', 'n'), ('m_scores', 0), ('ada', 19),
         ('chunk', 'b_q'), ('m_pv', 0), ('norm', 'b_q'), ('ada', 20),
         ('chunk', 'b_k'), ('turn', 'b_q'), ('turn_y', 'm'), ('norm', 'b_k'), ('ada', 21),
         ('chunk', 'r_q'), ('turn', 'b_k'), ('scores', 'moba'), ('ada', 22),
         ('chunk', 'r_k'), ('turn_p', 'moba'), ('ada', 23),
         ('chunk', 'r_g'), ('pv', 'moba'), ('r_scores', 0), ('turn_y', 'b'), ('r_pv', 0), ('turn_y', 'r')]


def place_sums(order):
    placed, waiting = [], []
    for step, arg in order:
        placed.append((step, arg))
        if step == 'ada':
            waiting.append(arg)
        elif step == 'chunk':
            placed += [('ada_sum', n) for n in waiting]
            waiting = []
    assert not waiting
    return placed


ORDER = place_sums(ORDER)
CHUNKS = [a for s, a in ORDER if s == 'chunk']
MIX_Y = {'m': 0, 'b': 1, 'r': 2, 'n': 3}
AFTER_ADA = {4: CHUNKS[0], 5: CHUNKS[1]}


def weight_stream():
    halves = []
    for n in range(len(ADA_FIRST)):
        halves += [('ada', n, 0), ('ada', n, 1)]
        if n in AFTER_ADA:
            halves.append(('chunk', AFTER_ADA[n], 0))
    for step, arg in ORDER:
        if step == 'chunk' and arg in AFTER_ADA.values():
            halves.append(('chunk', arg, 1))
        elif step in ('chunk', 'ada', 'cmp_hid'):
            halves += [('cmp' if step == 'cmp_hid' else step, arg, 0), ('cmp' if step == 'cmp_hid' else step, arg, 1)]
    return halves + [('wout', n, hf) for n in range(D // 512) for hf in range(2)]


STREAM = weight_stream()
RING = 4
HALF = 8 * 512
PER_GROUP = 24
EXPERT_BASE = len(STREAM)


def by_vector(item):
    return item[0] == 'ada' and item[1] >= len(ADA_FIRST)


def halves_used(i):
    v = sum(by_vector(STREAM[j]) for j in range(i))
    return i - v, v


PE_BASE = halves_used(EXPERT_BASE)[0]


SEMAPHORES = (
    "slot_full0", "slot_full1", "slot_full2", "slot_full3", "half_used", "rounds_ready", "out_ready", "stored",
    "exponent_ready", "x_ms", "x_rstd", "kc_ms", "kc_rstd", "norm_n_q_ms", "norm_n_ks_ms", "norm_n_kw_ms",
    "norm_b_q_ms", "norm_b_k_ms", "norm_n_q_rstd", "norm_n_ks_rstd", "norm_n_kw_rstd", "norm_b_q_rstd",
    "norm_b_k_rstd", "y_m_ms", "y_r_ms", "y_m_rstd", "y_r_rstd", "scores_done", "negmask_loaded",
    "decay_loaded", "r_scores_done", "router_loaded", "x_again", "x1_ms", "x1_rstd", 
    "rows_loaded", "cols_turned", "xhat_ready1", "xhat_ready2", "xT_copied1", "xT_copied2", "xT_turned1",
    "xT_turned2", "csil_ready", "ada_combined", "ada_partial", "ada_half_used", "ada_summed", "chunk_copied", "h_ready",
    "misc_loaded", "cols_ready", "extras_done", "zx_ready", "gates_turned", "gates_read", "blocks_ready",
    "hid_ready", "cmp_projected", "kc_normed", "turned_ready", "kc_turned", "kct_ready", "cmp_scores_done",
    "cmp_exp", "cmp_p_turned", "cmp_pT_ready", "cmp_pv_done", "normed", "kc_read", "vc_ready",
    "cmp_scores_read", "scores_read", "m_o_read", "yT_ready_m", "turned", "cmp_y", "o_read", "exp_done",
    "p_turned", "pT_ready", "o_done", "gate_rows_ready", "hsel_ready", "m_cols_turned", "conv_done",
    "yT_ready_n", "y_ready_b", "m_scores_done", "m_p_ready", "r_p_ready", "yT_ready_b", "m_pv_done",
    "r_pv_done", "y_ready_n", "y_ready_m", "y_ready_r", "m_cols_read", "m_args_ready", "y_turned_n",
    "y_turned_m", "y_turned_b", "y_turned_r", "yT_ready_r", "x1_ready", "router_done", "mask_ready",
    "places_done", "g_ready", "y_added", "gathered", "g_turned", "xt_act", "xt_dve", "gt_ready", "round_shifted", "hh_ready",
    "hh_turned", "hT_ready", "y_copied", "scattered", "x_loaded", "c_loaded", "c_turned", "late_loaded", "c_tanh", "x_squared", "gains_ready",
    "gate_tanh_m", "gate_tanh_r", "n_gate_tanh", "f_abs", "f_exp", "f_one", "f_ln", "gelu_arg", "gelu_tanh",
    "cmp_arg", "cmp_e", "nmax_ready", "conv_sum", "conv_tanh", "enm_ready", "m_decay_ready", "x1_squared", "shift_products", "shift_logits", "shift_read",
    "group_arg", "group_exp", "pair_arg", "pair_exp", "e_ready", "dve_step", "r_o_read",
    "dve_loop_step",
)


def constants():
    c = np.zeros((P, NCONST), np.float32)

    def put(name, a):
        o, w = CONST[name]
        c[:, o:o + w] = np.asarray(a, np.float32).reshape(P, w)
    p = np.arange(P)
    put('ident', np.eye(P))
    put('tri', p[:, None] <= p[None, :])
    put('ones', np.ones((P, P)))
    put('sel4', np.repeat((p % 32 == 0)[:, None], P, 1))
    put('iota', np.tile(np.arange(32), (P, 1)))
    slopes = 2.0 ** (-np.arange(1, 2 * H + 1, dtype=np.float64))
    dist = (P + p)[:, None] - np.arange(T)[None, :]
    put('alibi', np.stack([np.where(dist >= 0, -slopes[2 * h + st] * dist, NEG)
                           for st in range(2) for h in range(H)], 1))
    gam = np.log1p(-2.0 ** (-5.0 - np.arange(H)))
    fwd = np.arange(T)[None, :] - p[:, None]
    put('decay', np.stack([np.where(fwd >= 0, np.exp(gam[h] * np.maximum(fwd, 0)), 0.0) * QSCALE
                           for h in range(H)], 1))
    t = (np.arange(TT) * P)[None, :, None] + p[:, None, None]
    dc = t - (np.arange(N_CMP) * 16 + CMP_LEN - 1)[None, None, :]
    put('cmp_bias', np.stack([np.where(dc >= 0, -slopes[2 * h + 1] * dc, NEG) for h in range(H)], 2))
    put('cmp_ok', np.stack([dc >= 0] * H, 2))
    put('negmask', np.where(fwd >= 0, 0.0, NEG))
    return c


def build_program(nc, a, out):
    with ExitStack() as ctx:
        def sb(name, cols, dt=F32):
            return ctx.enter_context(nc.sbuf_tensor(name, [P, cols], dt))

        def psum(name, cols):
            return ctx.enter_context(nc.psum_tensor(name, [P, cols], F32))

        ring = [sb(f"ring{s}", HALF) for s in range(RING)]
        consts = sb("consts", N_EARLY)
        buf_h = sb("buf_h", TT * D)
        buf_x = sb("buf_x", TT * D)
        g1b = sb("g1b", D)
        g2b = sb("g2b", D)
        Z = sb("Z", 10 * 1024)
        pad = sb("pad", 2 * H * (T + 3))
        tmp = sb("tmp", 2048)
        yb = sb("yb", 1024)
        PA = sb("PA", 1536)
        PB = sb("PB", 1536)
        ada_s = sb("ada_s", 512)
        rows = PB[:, 0:3 * P]
        w2c = PB[:, 384:640]
        wx = PA[:, 1024:1024 + KT * NX]
        cols_a = sb("cols_a", 88)
        cols_b = sb("cols_b", 96)
        cols_c = sb("cols_c", 64)
        csil = sb("csil", KT * 32)
        small = sb("small", 512)
        rb = sb("rb", 36)
        modc = sb("modc", 4 * KT)
        gsc = sb("gsc", 2 * KT)
        hsel = PB[:, 0:H * P]
        hid = sb("hid", 120)
        kct = sb("kct", 60)
        vc = Z[:, 9216:9216 + GW]
        wr = Z[:, 8192:8192 + KT * 36]
        zx = sb("zx", TT * NX)
        sgn = sb("sgn", TT * 3 * H)
        gat = sb("gat", 3 * T)
        gb = sb("gb", 2)
        cnt_i = sb("cnt_i", 1, I32)

        W = psum("W", 2048)
        M = psum("M", 1536)
        A = psum("A", 512)

        hT = buf_h[:].rearrange("p (k t) -> p k t", k=KT)
        x1 = buf_h[:].rearrange("p (a d) -> p a d", a=TT)
        xs = buf_x[:].rearrange("p (a d) -> p a d", a=TT)
        YT = buf_x[:].rearrange("p (k t) -> p k t", k=KT)

        negmask = Z[:, 5120:5376]

        def const(name):
            o, w = CONST[name]
            return consts[:, o:o + w]
        ident, tri, ones, sel4 = const('ident'), const('tri'), const('ones'), const('sel4')
        alibi = const('alibi').rearrange("p (s h t) -> p s h t", s=2, h=H)
        decay = Z[:, 3072:4096].rearrange("p (h t) -> p h t", h=H)

        def slot(i):
            return Z[:, i * 1024:(i + 1) * 1024]
        zslot = {'n_kc': slot(0), 'n_vc': slot(1), 'n_q': slot(2), 'n_ks': slot(4), 'n_vs': slot(6),
                 'n_kw': slot(7), 'n_vw': slot(9), 'm_v': slot(2), 'm_o': slot(4), 'b_q': slot(0),
                 'b_k': slot(1), 'b_v': slot(6), 'r_q': slot(8), 'r_k': slot(2), 'r_v': slot(9), 'r_g': slot(4)}
        tslot = {'n_q': slot(3), 'n_ks': slot(5), 'n_kw': slot(8), 'b_q': slot(7), 'b_k': slot(0),
                 'm_q': slot(0), 'm_k': slot(1), 'r_q': slot(8), 'r_k': slot(2)}
        padv = pad[:].rearrange("p (w h t) -> p w h t", w=2, h=H)
        blk = [pad[:, 0:CMP_LEN * 60], tmp[:, 0:CMP_LEN * 60]]

        def heads(ap):
            return ap.rearrange("p (h t) -> p h t", h=H)

        def tth(ap):
            return ap.rearrange("p (a d) -> p a d", d=DH)

        CA_C, CA_N1, CA_N2, CA_CONV, CA_G = 0, 16, 32, 48, 80
        GAIN = {'m': CA_G, 'b_q': CA_G + 1, 'b_k': CA_G + 2, 'r': CA_G + 3, 'n_q': CA_G + 4,
                'cmp': CA_G + 5, 'n_ks': CA_G + 6, 'n_kw': CA_G + 7}

        used = [0]

        def sm(n):
            o = used[0]
            used[0] += n
            assert used[0] <= 512
            return small[:, o:o + n]
        minus_half = sm(8)
        ss, rst = sm(8), sm(8)
        ssx, rsx = sm(2), sm(2)
        ssp = sm(8)
        mx, nmx, lsum, fac = sm(8), sm(8), sm(8), sm(8)
        ssy, rsy = sm(8), sm(8)
        bcol_enm, den = sm(16), sm(8)
        bcol, enm = bcol_enm[:, 0:8], bcol_enm[:, 8:16]
        ssc, rsc = sm(1), sm(1)
        cmx, csum, cf = sm(8), sm(8), sm(8)
        cs = sm(48)
        exc = sm(24)
        lg = sm(TT * 36)
        pos = sm(TT * (NE + 4))
        gate = sm(TT * (NE + 4))
        rt = sm(40)

        sem = {name: ctx.enter_context(nc.semaphore(name)) for name in SEMAPHORES}
        slot_full = [sem[f"slot_full{s}"] for s in range(RING)]
        half_used = sem["half_used"]

        def chunk_no(name):
            return CHUNKS.index(name) + 1

        def item_done(eng, kind, arg):
            eng.wait_ge(half_used, halves_used(STREAM.index((kind, arg, 1)) + 1)[0])

        def kview(ap):
            return ap.rearrange("(k p) n -> p k n", p=P)
        ada_w, w_in, w_out = kview(a['ada_w'][0]), kview(a['w_in'][0]), kview(a['w_out'][0])
        cmp1 = a['nsa_cmp_w1'][0]

        h2T = Z[:, 0:4096].rearrange("p (k t) -> p k t", k=KT)
        yacc = Z[:, 0:4096].rearrange("p (a d) -> p a d", a=TT)
        XT = Z[:, 4096:6144].rearrange("p (k j) -> p k j", k=KT)
        ysb = Z[:, 6144:8192]
        Gm = tmp[:, 0:256].rearrange("p (a q j) -> p a q j", a=TT, q=4)
        Gg = tmp[:, 256:512].rearrange("p (a q j) -> p a q j", a=TT, q=4)
        GT = tmp[:, 512:768]
        hh, ee, aa = (tmp[:, 768 + 128 * i:896 + 128 * i] for i in range(3))
        hTs = tmp[:, 1408:1536]
        ohg, le_g, oh1, oh2, le2, tie = (PA[:, 64 * i:64 * i + 64] for i in range(6))
        expd = PA[:, 384:512]
        mask = PA[:, 512:576]
        mprod = PA[:, 576:640]
        jdesc = PA[:, 640:672]
        w12 = PA[:, 672:688]
        s36 = PA[:, 704:740]

        def load_rounds(eng):
            eng.wait_ge(sem["rounds_ready"], 1)
            return eng.value_load(cnt_i[0:1, 0:1], min_val=1, max_val=T // 32)

        block = ctx.enter_context(nc.Block())

        @block.sync
        def _(sp):
            sp.dma_start(consts[:, 0:P], a['consts'][:, 0:P]).then_inc(sem["c_loaded"], 16)
            sp.dma_start(rows[0:16, 0:P], a['c'].rearrange("o (k p) -> (o k) p", p=P)).then_inc(sem["c_loaded"], 16)
            for i in range(EXPERT_BASE):
                kind, arg, hf = STREAM[i]
                if i >= RING:
                    pe_halves, dve_halves = halves_used(i - RING + 1)
                    if by_vector(STREAM[i - RING]):
                        sp.wait_ge(sem["ada_half_used"], dve_halves)
                    else:
                        sp.wait_ge(half_used, pe_halves)
                dst = ring[i % RING][:].rearrange("p (k n) -> p k n", k=8)
                ks = slice(8 * hf, 8 * hf + 8)
                if kind == 'ada':
                    src = ada_w[:, ks, 512 * ADA[arg]:512 * ADA[arg] + 512]
                elif kind == 'chunk':
                    src = w_in[:, ks, COL[arg]:COL[arg] + GW]
                elif kind == 'cmp':
                    src = cmp1[hf].rearrange("(l p) e -> p l e", p=P)
                    dst = ring[i % RING][:].rearrange("p (l e) -> p l e", l=CMP_LEN)
                else:
                    src = w_out[:, ks, 512 * arg:512 * arg + 512]
                sp.dma_start(dst, src).then_inc(slot_full[i % RING], 16)

            def four_experts(it, g):
                for j in range(PER_GROUP):
                    q, part, hf = j // 6, j % 6 // 2, j % 2
                    i = EXPERT_BASE + j
                    sp.wait_ge(half_used, PER_GROUP * it + (PE_BASE + j - RING + 1))
                    if part < 2:
                        w = a['exp_w1' if part == 0 else 'exp_w3'][0]
                        sp.dma_start(ring[i % RING][:].rearrange("p (k n) -> p k n", k=8),
                                     w[4 * g + q].rearrange("(k p) n -> p k n", p=P)[:, 8 * hf:8 * hf + 8, :]
                                     ).then_inc(slot_full[i % RING], 16)
                    else:
                        w = a['exp_w2'][0]
                        sp.dma_start(ring[i % RING][:].rearrange("p (c n) -> p c n", c=2),
                                     w[4 * g + q].rearrange("(c p) n -> p c n", p=P)[:, 2 * hf:2 * hf + 2, :]
                                     ).then_inc(slot_full[i % RING], 16)

            four_experts(0, 0)
            rounds = load_rounds(sp)
            with sp.Fori(1, rounds * (NE // 4)) as it:
                four_experts(it, it % (NE // 4))
            for tt in range(TT):
                sp.wait_ge(sem["out_ready"], tt + 1)
                sp.dma_start(out[0, tt * P:tt * P + P, :], yacc[:, tt, :]).then_inc(sem["stored"], 16)
            sp.wait_ge(sem["stored"], 32)

        @block.gpsimd
        def _(pool):
            pool.memset(minus_half, -0.5).then_inc(sem["exponent_ready"], 1)
            pool.wait_ge(sem["exponent_ready"], 1)

            def rsqrt(v):
                return pool.tensor_tensor(v, v, minus_half[0:v.shape[0], 0:v.shape[1]], ALU.pow)

            pool.wait_ge(sem["x_ms"], 1)
            rsqrt(rsx).then_inc(sem["x_rstd"], 1)
            pool.wait_ge(sem["h_ready"], 4)
            pool.dma_start(g1b[:], a['ada_b'][0:1, 2 * D:3 * D].to_broadcast([P, D])).then_inc(sem["late_loaded"], 16)
            pool.dma_start(g2b[:], a['ada_b'][0:1, 5 * D:6 * D].to_broadcast([P, D])).then_inc(sem["late_loaded"], 16)
            pool.dma_start(consts[:, N_FIRST:N_EARLY], a['consts'][:, N_FIRST:N_EARLY]).then_inc(sem["late_loaded"], 16)
            n_att = 0
            for step, arg in ORDER:
                if step == 'cmp_out':
                    pool.wait_ge(sem["kc_ms"], 1)
                    rsqrt(rsc[0:60, :]).then_inc(sem["kc_rstd"], 1)
                elif step == 'norm':
                    pool.wait_ge(sem[f"norm_{arg}_ms"], 1)
                    rsqrt(rst).then_inc(sem[f"norm_{arg}_rstd"], 1)
                elif step in ('m_pv', 'r_pv'):
                    pool.wait_ge(sem[f"y_{step[0]}_ms"], 1)
                    rsqrt(rsy).then_inc(sem[f"y_{step[0]}_rstd"], 1)
                elif step == 'scores':
                    n_att += 1
                    if arg == 'slc':
                        pool.wait_ge(sem["scores_done"], n_att)
                        o, w = CONST['negmask']
                        pool.dma_start(negmask, a['consts'][:, o:o + w]).then_inc(sem["negmask_loaded"], 16)
                    elif arg == 'win':
                        pool.wait_ge(sem["scores_done"], n_att)
                        o, w = CONST['decay']
                        pool.dma_start(Z[:, 3072:4096], a['consts'][:, o:o + w]).then_inc(sem["decay_loaded"], 16)
                elif step == 'r_scores':
                    pool.wait_ge(sem["r_scores_done"], 1)
                    wrv = wr.rearrange("p (k n) -> p k n", k=KT)
                    pool.dma_start(wrv[:, :, 0:NG], kview(a['router_g_w'][0])).then_inc(sem["router_loaded"], 16)
                    pool.dma_start(wrv[:, :, NG:36], kview(a['router_e_w'][0])).then_inc(sem["router_loaded"], 16)
                    pool.dma_start(rb[:, 0:NG], a['router_g_b'].to_broadcast([P,
                            NG])).then_inc(sem["router_loaded"], 16)
                    pool.dma_start(rb[:, NG:36], a['router_e_b'].to_broadcast([P,
                            NE])).then_inc(sem["router_loaded"], 16)
                elif (step, arg) == ('chunk', CHUNKS[-1]):
                    item_done(pool, 'chunk', arg)
                    pool.dma_start(x1, a['x'][0].rearrange("(a p) d -> p a d", p=P)).then_inc(sem["x_again"], 16)
            pool.wait_ge(sem["x1_ms"], 1)
            rsqrt(rsx).then_inc(sem["x1_rstd"], 1)
            pool.memset(GT, 0.0).then_inc(sem["gt_ready"], 1)
            pool.wait_ge(sem["gt_ready"], 1)
            for q in range(4):
                pool.memset(ysb[32 * q:32 * q + 32, :], 0.0).then_inc(sem["y_copied"], 1)
                pool.wait_ge(sem["y_copied"], q + 1)
            pool.wait_ge(sem["router_done"], 1)
            pool.memset(Z[:, 0:4096], 0.0).then_inc(sem["y_added"], 1)

        @block.tensor
        def _(pe):
            half = [0]

            def half_arrives():
                i = half[0]
                pe.wait_ge(slot_full[i % RING], 16 * (i // RING + 1))
                return ring[i % RING]

            def half_done(ins):
                ins.then_inc(half_used, 1)
                half[0] += 1

            r3 = rows.rearrange("p (i d) -> p i d", i=3)
            pe.wait_ge(sem["c_loaded"], 32)
            pe.transpose(M[:, 0:16], r3[0:16, 0, :], ident[0:16, 0:16]).then_inc(sem["c_turned"], 1)

            def turn_rows():
                pe.wait_ge(sem["rows_loaded"], 16 * 11)
                pe.transpose(M[:, 0:88], r3[0:88, 0, :], ident[0:88, 0:88])
                pe.transpose(M[:, 512:608], r3[0:96, 1, :], ident[0:96, 0:96])
                pe.transpose(M[:, 1024:1088], r3[0:64, 2, :], ident[0:64, 0:64]).then_inc(sem["cols_turned"], 1)

            def turn_x():
                for b in range(4):
                    if b == 0:
                        pe.wait_ge(sem["xhat_ready1"], 1)
                    if b >= 2:
                        pe.wait_ge(sem["xT_copied1"], b - 1)
                    for k in range(4):
                        for tt in range(TT):
                            o = (b % 2) * 1024 + k * T + tt * P
                            ins = pe.transpose(W[:, o:o + P], xs[:, tt, (4 * b + k) * P:(4 * b + k + 1) * P], ident)
                    ins.then_inc(sem["xT_turned1"], 1)

            def ada_products(n):
                if n == 0:
                    pe.wait_ge(sem["csil_ready"], 1)
                else:
                    pe.wait_ge(sem["ada_combined"], n)
                for hf in range(2):
                    w = half_arrives()
                    for k in range(8):
                        kk = 8 * hf + k
                        j = kk % 4
                        ins = pe.matmul(A[32 * j:32 * j + 32, :], csil[:, 32 * kk:32 * kk + 32],
                                        w[:, 512 * k:512 * k + 512], start=(kk < 4), stop=(kk >= 12))
                    half_done(ins)

            def ada_combine(n):
                if n < len(ADA_FIRST):
                    pe.wait_ge(sem["ada_partial"], n + 1)
                    sel = sel4
                else:
                    pe.wait_ge(sem["ada_half_used"], 2 * (n - len(ADA_FIRST) + 1))
                    pe.wait_ge(sem["ada_combined"], n)
                    sel = ones
                if ADA[n] // 4 in (2, 5):
                    pe.matmul(A[:], sel, ada_s[:], start=True, stop=True).then_inc(sem["ada_summed"], 1)
                else:
                    for b in range(4):
                        ins = pe.matmul(A[:, b:b + 1], ada_s[:, b * P:(b + 1) * P], sel[:, 0:1], start=True, stop=True)
                    ins.then_inc(sem["ada_summed"], 1)

            def chunk_half(name, n, hf):
                o = (n % 2) * 1024
                if n < 2:
                    pe.wait_ge(sem["h_ready"], 2 + 2 * hf)
                    pe.wait_ge(sem["xT_copied1"], 4)
                elif hf == 0:
                    pe.wait_ge(sem["chunk_copied"], n - 1)
                w = half_arrives()
                if name in ('m_q', 'm_k', 'r_q', 'r_k', 'n_kc', 'n_vc'):
                    for h in range(H):
                        for k in range(8):
                            kk = 8 * hf + k
                            ins = pe.matmul(W[:, o + h * T:o + h * T + T],
                                            w[:, 512 * k + h * P:512 * k + h * P + P], hT[:, kk, :],
                                            start=(kk == 0 and h % 2 == 0), stop=(kk == KT - 1),
                                            skip_group_check=True)
                else:
                    for k in range(8):
                        for tt in range(TT):
                            kk = 8 * hf + k
                            ins = pe.matmul(W[:, o + tt * 512:o + tt * 512 + 512], hT[:, kk, tt * P:tt * P + P],
                                            w[:, 512 * k:512 * k + 512], start=(kk == 0), stop=(kk == KT - 1))
                half_done(ins)

            def turn8(src):
                for h in range(H):
                    for tt in range(TT):
                        ins = pe.transpose(M[:, h * T + tt * P:h * T + tt * P + P],
                                           src[:, tt * 512 + h * DH:tt * 512 + h * DH + DH], ident)
                return ins

            n_chunk = n_turn = n_att = 0
            for n in range(len(ADA_FIRST)):
                ada_products(n)
                if n == 0:
                    turn_rows()
                if n in AFTER_ADA:
                    chunk_half(AFTER_ADA[n], CHUNKS.index(AFTER_ADA[n]), 0)
                ada_combine(n)
                if n == 1:
                    turn_x()
            for step, arg in ORDER:
                if step == 'ada':
                    half[0] += 2
                elif step == 'ada_sum':
                    ada_combine(arg)
                elif step == 'chunk':
                    if arg not in AFTER_ADA.values():
                        chunk_half(arg, n_chunk, 0)
                    chunk_half(arg, n_chunk, 1)
                    n_chunk += 1
                elif step == 'extras':
                    pe.wait_ge(sem["misc_loaded"], 16 * 5)
                    pe.wait_ge(sem["cols_ready"], 1)
                    for tt in range(TT):
                        for k in range(KT):
                            ins = pe.matmul(M[:, tt * 512:tt * 512 + NX], hT[:, k, tt * P:tt * P + P],
                                            wx[:, k * NX:k * NX + NX], start=(k == 0), stop=(k == KT - 1))
                    ins.then_inc(sem["extras_done"], 1)
                elif step == 'gates':
                    pe.wait_ge(sem["zx_ready"], 1)
                    for f in range(2):
                        for tt in range(TT):
                            ins = pe.transpose(M[0:H, f * T + tt * P:f * T + tt * P + P],
                                               zx[:, tt * NX + H * f:tt * NX + H * f + H], ident)
                    ins.then_inc(sem["gates_turned"], 1)
                elif step == 'cmp_hid':
                    pe.wait_ge(sem["gates_read"], 1)
                    for w in range(2):
                        wt = half_arrives()
                        pe.wait_ge(sem["blocks_ready"], w + 1)
                        for l in range(CMP_LEN):
                            ins = pe.matmul(M[:, 512 * w:512 * w + 60], wt[:, l * P:l * P + P],
                                            blk[w][:, l * 60:l * 60 + 60], start=(l == 0), stop=(l == CMP_LEN - 1))
                        half_done(ins)
                elif step == 'cmp_out':
                    pe.wait_ge(sem["hid_ready"], 1)
                    pe.matmul(M[0:60, 0:DH], hid[:, 0:60], w2c[:, 0:DH], start=True, stop=True)
                    for h in range(H):
                        ins = pe.matmul(M[0:N_CMP, 512 + h * DH:512 + h * DH + DH], hid[:, 60 + 15 * h:75 + 15 * h],
                                        w2c[:, DH:2 * DH], start=True, stop=True)
                    ins.then_inc(sem["cmp_projected"], 1)
                elif step == 'cmp_kT':
                    pe.wait_ge(sem["kc_normed"], 1)
                    pe.wait_ge(sem["turned_ready"], 1)
                    pe.transpose(M[:, 0:60], tmp[0:60, 1024:1152], ident[0:60, 0:60]).then_inc(sem["kc_turned"], 1)
                elif step == 'cmp_scores':
                    pe.wait_ge(sem["kct_ready"], 1)
                    pe.wait_ge(sem["turned_ready"], 1)
                    for tt in range(TT):
                        for h in range(H):
                            o = (tt * H + h) * N_CMP
                            ins = pe.matmul(M[:, o:o + N_CMP], heads(tslot['n_q'])[:, h, tt * P:tt * P + P],
                                            kct[:, 15 * h:15 * h + 15], start=True, stop=True)
                    ins.then_inc(sem["cmp_scores_done"], 1)
                elif step == 'cmp_pT':
                    pe.wait_ge(sem["cmp_exp"], 1)
                    pe.wait_ge(sem["turned_ready"], 2)
                    for i in range(TT * H):
                        ins = pe.transpose(M[0:N_CMP, i * P:i * P + P], PA[:, i * N_CMP:(i + 1) * N_CMP], ident)
                    ins.then_inc(sem["cmp_p_turned"], 1)
                elif step == 'cmp_pv':
                    pe.wait_ge(sem["cmp_pT_ready"], 1)
                    for tt in range(TT):
                        for h in range(H):
                            ins = pe.matmul(M[:, tt * 512 + h * DH:tt * 512 + h * DH + DH],
                                            PB[0:N_CMP, (tt * H + h) * P:(tt * H + h + 1) * P],
                                            vc[0:N_CMP, h * DH:h * DH + DH], start=True, stop=True)
                    ins.then_inc(sem["cmp_pv_done"], 1)
                elif step == 'turn':
                    n_turn += 1
                    pe.wait_ge(sem["normed"], n_turn)
                    if arg == 'n_q':
                        pe.wait_ge(sem["kc_read"], 1)
                        pe.wait_ge(sem["vc_ready"], 1)
                    elif arg == 'n_ks':
                        pe.wait_ge(sem["cmp_scores_read"], 1)
                    elif arg == 'n_kw':
                        pe.wait_ge(sem["scores_read"], 1)
                    elif arg == 'b_q':
                        pe.wait_ge(sem["m_o_read"], 1)
                    else:
                        pe.wait_ge(sem["yT_ready_m"], 1)
                    turn8(zslot[arg]).then_inc(sem["turned"], 1)
                elif step == 'scores':
                    n_att += 1
                    qn, kn = {'slc': ('n_q', 'n_ks'), 'win': ('n_q', 'n_kw'), 'moba': ('b_q', 'b_k')}[arg]
                    pe.wait_ge(sem["turned_ready"], {'slc': 2, 'win': 3, 'moba': 5}[arg])
                    if arg == 'slc':
                        pe.wait_ge(sem["cmp_y"], 1)
                    elif arg == 'win':
                        pe.wait_ge(sem["o_read"], 1)
                    qT, kT = heads(tslot[qn]), heads(tslot[kn])
                    for h in range(H):
                        pe.matmul(M[:, h * T:h * T + T], qT[:, h, P:T], kT[:, h, :], start=True, stop=True)
                        ins = pe.matmul(M[:, 1024 + h * P:1024 + h * P + P], qT[:, h, 0:P], kT[:, h, 0:P],
                                        start=True, stop=True)
                    ins.then_inc(sem["scores_done"], 1)
                elif step == 'turn_p':
                    pe.wait_ge(sem["exp_done"], n_att)
                    if arg == 'slc':
                        pe.wait_ge(sem["turned_ready"], 3)
                    for h in range(H):
                        for i, o in enumerate((1024 + h * P, h * T, h * T + P)):
                            ins = pe.transpose(M[:, h * 384 + i * P:h * 384 + i * P + P], PA[:, o:o + P], ident)
                    ins.then_inc(sem["p_turned"], 1)
                elif step == 'pv':
                    v = zslot[{'slc': 'n_vs', 'win': 'n_vw', 'moba': 'b_v'}[arg]]
                    pe.wait_ge(sem["chunk_copied"], chunk_no({'slc': 'n_vs', 'win': 'n_vw', 'moba': 'b_v'}[arg]))
                    pe.wait_ge(sem["pT_ready"], n_att)
                    for h in range(H):
                        pt = PB[:, h * 384:h * 384 + 384]
                        d = slice(h * DH, h * DH + DH)
                        pe.matmul(M[:, d], pt[:, 0:P], v[:, d], start=True, stop=True)
                        o1 = M[:, 512 + h * DH:512 + h * DH + DH]
                        pe.matmul(o1, pt[:, P:2 * P], v[:, d], start=True, stop=False)
                        ins = pe.matmul(o1, pt[:, 2 * P:3 * P], v[:, 512 + h * DH:512 + h * DH + DH],
                                        start=False, stop=True)
                    ins.then_inc(sem["o_done"], 1)
                elif step == 'm_decay':
                    pe.wait_ge(sem["gate_rows_ready"], 1)
                    pe.wait_ge(sem["hsel_ready"], 1)
                    pe.wait_ge(sem["o_read"], 2)
                    for i in range(2):
                        for tt in range(TT):
                            pe.transpose(M[:, 8 * i + 4 * tt:8 * i + 4 * tt + 4],
                                         gat[0:H, i * T + tt * P:i * T + tt * P + P], ident[0:H, 0:H])
                    for h in range(H):
                        ins = pe.matmul(M[:, 512 + h * T:512 + h * T + T], hsel[0:H, h * P:h * P + P],
                                        gat[0:H, 2 * T:3 * T], start=True, stop=True)
                    ins.then_inc(sem["m_cols_turned"], 1)
                elif step in ('m_scores', 'r_scores'):
                    who = step[0]
                    if who == 'm':
                        pe.wait_ge(sem["conv_done"], 2)
                    else:
                        pe.wait_ge(sem["chunk_copied"], chunk_no('r_k'))
                    if who == 'm':
                        pe.wait_ge(sem["yT_ready_n"], 1)
                    else:
                        pe.wait_ge(sem["y_ready_b"], 1)
                    qT, kT = heads(tslot[who + '_q']), heads(tslot[who + '_k'])
                    for h in range(H):
                        pe.matmul(M[:, h * T:h * T + T], kT[:, h, 0:P], qT[:, h, :], start=True, stop=True)
                        ins = pe.matmul(M[:, 1024 + h * P:1024 + h * P + P], kT[:, h, P:T], qT[:, h, P:T],
                                        start=True, stop=True)
                    ins.then_inc(sem[f"{who}_scores_done"], 1)
                elif step in ('m_pv', 'r_pv'):
                    who = step[0]
                    v = zslot[who + '_v']
                    pe.wait_ge(sem[f"{who}_p_ready"], 1)
                    pe.wait_ge(sem["chunk_copied"], chunk_no(who + '_v'))
                    if who == 'r':
                        pe.wait_ge(sem["yT_ready_b"], 1)
                    for h in range(H):
                        d = slice(h * DH, h * DH + DH)
                        o1 = M[:, 512 + h * DH:512 + h * DH + DH]
                        p0, p01, p11 = (PB[:, h * T:h * T + P], PB[:, h * T + P:h * T + T],
                                        PB[:, 1024 + h * P:1024 + h * P + P])
                        v0, v1 = v[:, d], v[:, 512 + h * DH:512 + h * DH + DH]
                        pe.matmul(M[:, d], p0, v0, start=True, stop=True)
                        pe.matmul(o1, p01, v0, start=True, stop=False)
                        ins = pe.matmul(o1, p11, v1, start=False, stop=True)
                        if who == 'm':
                            pe.matmul(M[:, 1024 + h:1025 + h], p0, ones[:, 0:1], start=True, stop=True)
                            pe.matmul(M[:, 1028 + h:1029 + h], p01, ones[:, 0:1], start=True, stop=False)
                            ins = pe.matmul(M[:, 1028 + h:1029 + h], p11, ones[:, 0:1], start=False, stop=True)
                    ins.then_inc(sem[f"{who}_pv_done"], 1)
                elif (step, arg) == ('turn_y', 'r'):
                    pass
                elif step == 'turn_y':
                    pe.wait_ge(sem[f"y_ready_{arg}"], 1)
                    if arg == 'n':
                        pe.wait_ge(sem["m_cols_read"], 1)
                        pe.wait_ge(sem["m_args_ready"], 1)
                    elif arg == 'm':
                        pe.wait_ge(sem["turned_ready"], 4)
                    elif arg == 'b':
                        pe.wait_ge(sem["r_p_ready"], 1)
                    turn8(yb[:]).then_inc(sem[f"y_turned_{arg}"], 1)

            def turn_x1(n):
                pe.wait_ge(sem["x1_ready"], n + 1)
                if n > 0:
                    pe.wait_ge(sem["xT_copied2"], n)
                for k in range(4):
                    for tt in range(TT):
                        o = k * T + tt * P
                        ins = pe.transpose(M[:, o:o + P], x1[:, tt, (4 * n + k) * P:(4 * n + k + 1) * P], ident)
                ins.then_inc(sem["xT_turned2"], 1)

            def router_products(n):
                pe.wait_ge(sem["xT_copied2"], n + 1)
                if n == 0:
                    pe.wait_ge(sem["shift_read"], 1)
                    pe.wait_ge(sem["ada_combined"], len(ADA))
                for k in range(4 * n, 4 * n + 4):
                    for tt in range(TT):
                        ins = pe.matmul(M[:, 1024:1060] if tt == 0 else A[:, 0:36], h2T[:, k, tt * P:tt * P + P],
                                        wr[:, 36 * k:36 * k + 36], start=(k == 0), stop=(k == KT - 1))
                if n == 3:
                    ins.then_inc(sem["router_done"], 1)

            for m in 'nmb':
                pe.wait_ge(sem[f"yT_ready_{m}"], 1)
            for n in range(D // 512):
                o = (n % 2) * 1024
                if n < 2:
                    pe.wait_ge(sem["chunk_copied"], len(CHUNKS) - 1 + n)
                else:
                    pe.wait_ge(sem["x1_ready"], n - 1)
                for hf in range(2):
                    if (n, hf) == (0, 1):
                        pe.wait_ge(sem["y_ready_r"], 1)
                        turn8(yb[:]).then_inc(sem["y_turned_r"], 1)
                        pe.wait_ge(sem["yT_ready_r"], 1)
                    w = half_arrives()
                    for k in range(8):
                        for tt in range(TT):
                            kk = 8 * hf + k
                            ins = pe.matmul(W[:, o + tt * 512:o + tt * 512 + 512], YT[:, kk, tt * P:tt * P + P],
                                            w[:, 512 * k:512 * k + 512], start=(kk == 0), stop=(kk == KT - 1))
                    half_done(ins)
                if n == 0:
                    pe.wait_ge(sem["shift_products"], 1)
                    pe.matmul(M[:, 1024:1060], ones, s36, start=True, stop=True).then_inc(sem["shift_logits"], 1)
                else:
                    turn_x1(n - 1)
                    if n > 1:
                        router_products(n - 2)
            assert half[0] == EXPERT_BASE
            turn_x1(3)
            router_products(2)
            router_products(3)

            pe.wait_ge(sem["mask_ready"], 1)
            pe.matmul(M[:, 0:NE], tri, mask[:, 0:NE], start=True, stop=True)
            pe.matmul(M[:, 512:512 + NE], ones, mask[:, 0:NE], start=True, stop=False)
            pe.matmul(M[:, 512:512 + NE], tri, mask[:, NE:2 * NE], start=False, stop=True)
            pe.matmul(M[:, 1024:1024 + NE], ones, mask[:, 0:NE], start=True, stop=False)
            pe.matmul(M[:, 1024:1024 + NE], ones, mask[:, NE:2 * NE], start=False,
                    stop=True).then_inc(sem["places_done"], 1)

            def gather():
                for b in range(2):
                    for k in range(8 * b, 8 * b + 8):
                        for tt in range(TT):
                            ins = pe.matmul(W[:, k * P:k * P + P], xs[:, tt, k * P:k * P + P],
                                            tmp[:, 128 * tt:128 * tt + 128], start=(tt == 0), stop=(tt == 1))
                    ins.then_inc(sem["gathered"], 1)

            def scatter(n):
                pe.wait_ge(sem["gt_ready"], n + 1)
                pe.wait_ge(sem["y_copied"], 4 * n + 4)
                for tt in range(TT):
                    pe.wait_ge(sem["y_added"], 2 * n + tt + 1)
                    for b in range(4):
                        ins = pe.matmul(W[:, 512 * b:512 * b + 512], GT[:, tt * P:tt * P + P],
                                        ysb[:, 512 * b:512 * b + 512], start=True, stop=True)
                    ins.then_inc(sem["scattered"], 1)

            pe.wait_ge(sem["g_ready"], 1)
            pe.wait_ge(sem["xhat_ready2"], 1)
            gather()
            rounds = load_rounds(pe)
            with pe.Fori(0, rounds) as r:
                with pe.Fori(0, NE // 4) as g:
                    it = 8 * r + g
                    for q in range(4):
                        if q == 0:
                            pe.wait_ge(sem["xt_act"], it + 1)
                            pe.wait_ge(sem["xt_dve"], it + 1)
                        elif q == 3:
                            pe.wait_ge(sem["g_ready"], it + 2)
                            pe.wait_ge(sem["y_added"], 2 * it + 3)
                            gather()
                        for w13 in range(2):
                            for hf in range(2):
                                j = 6 * q + 2 * w13 + hf
                                i = EXPERT_BASE + j
                                pe.wait_ge(slot_full[i % RING], 96 * it + 16 * (i // RING + 1))
                                w = ring[i % RING]
                                for k in range(8):
                                    kk = 8 * hf + k
                                    for c in range(4):
                                        ins = pe.matmul(M[32 * c:32 * c + 32, 512 * w13:512 * w13 + 128],
                                                        XT[:, kk, 32 * q:32 * q + 32],
                                                        w[:, 512 * k + 128 * c:512 * k + 128 * c + 128],
                                                        start=(kk == 0), stop=(kk == KT - 1))
                                ins.then_inc(half_used, 1)
                        if q == 0:
                            scatter(it)
                            for tt in range(TT):
                                ins = pe.transpose(M[:, 1024 + tt * P:1024 + tt * P + P],
                                                   tmp[:, 256 + 128 * tt:384 + 128 * tt], ident)
                            ins.then_inc(sem["g_turned"], 1)
                            pe.wait_ge(sem["gt_ready"], it + 2)
                        pe.wait_ge(sem["hh_ready"], 4 * it + q + 1)
                        pe.transpose(M[:, 1024:1152], hh, ident).then_inc(sem["hh_turned"], 1)
                        pe.wait_ge(sem["hT_ready"], 4 * it + q + 1)
                        pe.wait_ge(sem["y_copied"], 4 * it + q + 4)
                        for hf in range(2):
                            i = EXPERT_BASE + 6 * q + 4 + hf
                            pe.wait_ge(slot_full[i % RING], 96 * it + 16 * (i // RING + 1))
                            w = ring[i % RING]
                            for c2 in range(2):
                                c = 2 * hf + c2
                                for m in range(4):
                                    ins = pe.matmul(A[32 * m:32 * m + 32, :], hTs[:, 32 * c:32 * c + 32],
                                                    w[:, 2048 * c2 + 512 * m:2048 * c2 + 512 * m + 512],
                                                    start=(c == 0), stop=(c == 3))
                            ins.then_inc(half_used, 1)
            pe.wait_ge(sem["xt_act"], 8 * rounds + 1)
            pe.wait_ge(sem["xt_dve"], 8 * rounds + 1)
            pe.wait_ge(sem["y_copied"], 32 * rounds + 4)
            for b in range(4):
                ins = pe.matmul(W[:, 512 * b:512 * b + 512], GT[:, 0:P], ysb[:, 512 * b:512 * b + 512],
                                start=True, stop=True)
            ins.then_inc(sem["scattered"], 1)
            for b in range(4):
                ins = pe.matmul(M[:, 512 * b:512 * b + 512] if b < 3 else A[:], GT[:, P:2 * P],
                                ysb[:, 512 * b:512 * b + 512], start=True, stop=True)
            ins.then_inc(sem["scattered"], 1)

        @block.scalar
        def _(act):
            x0 = a['x'][0].rearrange("(a p) d -> p a d", p=P)
            act.dma_start(xs, x0).then_inc(sem["x_loaded"], 16)
            act.dma_start(consts[:, P:N_FIRST], a['consts'][:, P:N_FIRST]).then_inc(sem["rows_loaded"], 16)
            r3 = rows.rearrange("p (i d) -> p i d", i=3)
            act.dma_start(r3[16:32, 0, :], a['norm1_g'].rearrange("o (k p) -> (o k) p",
                    p=P)).then_inc(sem["rows_loaded"], 16)
            act.dma_start(r3[32:48, 0, :], a['norm2_g'].rearrange("o (k p) -> (o k) p",
                    p=P)).then_inc(sem["rows_loaded"], 16)
            act.dma_start(r3[48:80, 0, :], a['mlstm_conv_w'][0].rearrange("j (b p) -> (j b) p",
                    p=P)).then_inc(sem["rows_loaded"], 16)
            act.dma_start(r3[80:81, 0, :], a['mlstm_out_g']).then_inc(sem["rows_loaded"], 16)
            act.dma_start(r3[81:83, 0, :], a['moba_qk_g'][0]).then_inc(sem["rows_loaded"], 16)
            act.dma_start(r3[83:84, 0, :], a['ret_out_g']).then_inc(sem["rows_loaded"], 16)
            act.dma_start(r3[84:85, 0, :], a['nsa_q_g']).then_inc(sem["rows_loaded"], 16)
            act.dma_start(r3[85:88, 0, :], a['nsa_k_g'][0]).then_inc(sem["rows_loaded"], 16)
            act.dma_start(r3[0:96, 1, :], a['ada_b'].rearrange("o (k p) -> (o k) p",
                    p=P)).then_inc(sem["rows_loaded"], 16)
            act.dma_start(r3[0:64, 2, :],
                    a['nsa_cmp_pos'][0].rearrange("w l d -> (w l) d")).then_inc(sem["rows_loaded"], 16)
            wxv = wx.rearrange("p (k n) -> p k n", k=KT)
            act.dma_start(wxv[:, :, 0:2 * H], w_in[:, :,
                    COL['m_i']:COL['m_i'] + 2 * H]).then_inc(sem["misc_loaded"], 16)
            act.dma_start(wxv[:, :, 2 * H:NX], w_in[:, :,
                    COL['n_g']:COL['n_g'] + 3 * H]).then_inc(sem["misc_loaded"], 16)
            for f in range(2):
                act.dma_start(gb[0:H, f:f + 1], a['mlstm_gate_b'][0, f, :].unsqueeze(1),
                              allow_slow_non_contiguous=True).then_inc(sem["misc_loaded"], 16)
            act.dma_start(w2c.rearrange("p (w d) -> p w d", w=2),
                           a['nsa_cmp_w2'][0].rearrange("w e d -> e w d")).then_inc(sem["misc_loaded"], 16)
            act.wait_ge(sem["c_turned"], 1)
            act.activation(cols_a[:, CA_C:CA_C + 16], M[:, 0:16], ACT.Copy)
            act.activation(cs[:, 0:16], M[:, 0:16], ACT.Tanh, scale=0.5).then_inc(sem["c_tanh"], 1)
            act.wait_ge(sem["x_loaded"], 16)
            act.activation(Z[:, 0:2048], xs[:, 0, :], ACT.Square, accum_out=ssx[:, 0:1])
            act.activation(Z[:, 2048:4096], xs[:, 1, :], ACT.Square, accum_out=ssx[:,
                    1:2]).then_inc(sem["x_squared"], 1)
            def ada_evacuate(n):
                item_done(act, 'ada', n)
                act.activation(ada_s[:], A[:], ACT.Copy).then_inc(sem["ada_partial"], 1)

            for n in range(len(ADA_FIRST)):
                ada_evacuate(n)
                if n == 0:
                    act.wait_ge(sem["cols_turned"], 1)
                    act.activation(cols_a[:, 16:88], M[:, 16:88], ACT.Copy)
                    act.activation(cols_b[:], M[:, 512:608], ACT.Copy)
                    act.activation(cols_c[:], M[:, 1024:1088], ACT.Copy).then_inc(sem["cols_ready"], 1)
                elif n == 1:
                    for b in range(4):
                        act.wait_ge(sem["xT_turned1"], b + 1)
                        act.activation(buf_h[:, b * 1024:(b + 1) * 1024], W[:, (b % 2) * 1024:(b % 2) * 1024 + 1024],
                                       ACT.Copy).then_inc(sem["xT_copied1"], 1)
            act.wait_ge(sem["gains_ready"], 1)
            n_turn = n_att = n_chunk = 0
            for step, arg in ORDER:
                if step == 'chunk':
                    item_done(act, 'chunk', arg)
                    if arg == 'm_v':
                        act.wait_ge(sem["turned"], 1)
                    elif arg == 'm_o':
                        act.wait_ge(sem["turned"], 2)
                    elif arg in ('b_q', 'b_k'):
                        act.wait_ge(sem["m_scores_done"], 1)
                    elif arg == 'b_v':
                        act.wait_ge(sem["o_done"], 1)
                    elif arg == 'r_q':
                        act.wait_ge(sem["scores_done"], 2)
                    elif arg == 'r_k':
                        act.wait_ge(sem["m_pv_done"], 1)
                    elif arg == 'r_v':
                        act.wait_ge(sem["o_done"], 2)
                    elif arg == 'r_g':
                        act.wait_ge(sem["y_ready_m"], 1)
                    o = (n_chunk % 2) * 1024
                    if arg in ('m_q', 'm_k'):
                        dst, src = padv[:, int(arg == 'm_k'), :, 3:T + 3], heads(W[:, o:o + 1024])
                    else:
                        dst, src = zslot[arg], W[:, o:o + 1024]
                    act.activation(dst, src, ACT.Copy).then_inc(sem["chunk_copied"], 1)
                    n_chunk += 1
                    if arg in ('m_o', 'r_g'):
                        act.wait_ge(sem["chunk_copied"], n_chunk)
                        if arg == 'm_o':
                            act.activation(zslot[arg], zslot[arg], ACT.Tanh,
                                    scale=0.5).then_inc(sem["gate_tanh_m"], 1)
                        else:
                            act.wait_ge(sem["p_turned"], 3)
                            act.activation(PA[:, 0:1024], zslot[arg], ACT.Tanh,
                                    scale=0.5).then_inc(sem["gate_tanh_r"], 1)
                elif step == 'gates':
                    act.wait_ge(sem["zx_ready"], 1)
                    act.activation(exc.rearrange("p (a n) -> p a n", a=TT),
                                   zx[:].rearrange("p (a n) -> p a n", a=TT)[:, :, 2 * H:NX],
                                   ACT.Tanh, scale=0.5).then_inc(sem["n_gate_tanh"], 1)
                    fa = PA[0:H, 2 * T:3 * T]
                    act.wait_ge(sem["f_abs"], 1)
                    act.activation(fa, fa, ACT.Exp).then_inc(sem["f_exp"], 1)
                    act.wait_ge(sem["f_one"], 1)
                    act.activation(fa, fa, ACT.Ln).then_inc(sem["f_ln"], 1)
                elif step == 'cmp_hid':
                    act.wait_ge(sem["gelu_arg"], 1)
                    act.activation(tmp[:, 0:120], tmp[:, 0:120], ACT.Tanh,
                            scale=0.7978845608028654).then_inc(sem["gelu_tanh"], 1)
                elif step == 'cmp_out':
                    act.wait_ge(sem["cmp_projected"], 1)
                    act.activation(vc[0:N_CMP], M[0:N_CMP, 512:1024], ACT.Copy).then_inc(sem["vc_ready"], 1)
                elif step == 'cmp_kT':
                    act.wait_ge(sem["kc_turned"], 1)
                    act.activation(kct[:], M[:, 0:60], ACT.Copy, scale=cols_a[:,
                            GAIN['cmp']:GAIN['cmp'] + 1]).then_inc(sem["kct_ready"], 1)
                elif step == 'cmp_scores':
                    act.wait_ge(sem["cmp_arg"], 1)
                    act.activation(PA[:, 0:120], PA[:, 0:120], ACT.Exp).then_inc(sem["cmp_e"], 1)
                elif step == 'cmp_pT':
                    act.wait_ge(sem["cmp_p_turned"], 1)
                    act.activation(PB[0:N_CMP, 0:1024], M[0:N_CMP, 0:1024], ACT.Copy).then_inc(sem["cmp_pT_ready"], 1)
                elif step == 'turn':
                    n_turn += 1
                    act.wait_ge(sem["turned"], n_turn)
                    act.activation(tslot[arg], M[:, 0:1024], ACT.Copy,
                                   scale=cols_a[:, GAIN[arg]:GAIN[arg] + 1]).then_inc(sem["turned_ready"], 1)
                elif step == 'scores':
                    n_att += 1
                    act.wait_ge(sem["nmax_ready"], n_att)
                    for h in range(H):
                        act.activation(PA[:, h * T:h * T + T], PA[:, h * T:h * T + T], ACT.Exp,
                                       bias=nmx[:, 4 + h:5 + h], accum_out=lsum[:, 4 + h:5 + h])
                        o = 1024 + h * P
                        ins = act.activation(PA[:, o:o + P], PA[:, o:o + P], ACT.Exp,
                                             bias=nmx[:, h:h + 1], accum_out=lsum[:, h:h + 1])
                    ins.then_inc(sem["exp_done"], 1)
                elif step == 'turn_p':
                    act.wait_ge(sem["p_turned"], n_att)
                    act.activation(PB[:], M[:], ACT.Copy).then_inc(sem["pT_ready"], 1)
                elif step == 'conv':
                    w = int(arg == 'm_k')
                    act.wait_ge(sem["conv_sum"], w + 1)
                    act.activation(tmp[:, 1024:2048], tslot[arg], ACT.Tanh, scale=0.5).then_inc(sem["conv_tanh"], 1)
                elif step == 'm_decay':
                    act.wait_ge(sem["m_cols_read"], 1)
                    act.activation(enm, enm, ACT.Exp).then_inc(sem["enm_ready"], 1)
                    act.wait_ge(sem["m_args_ready"], 1)
                    act.activation(PA[:], PA[:], ACT.Exp).then_inc(sem["m_decay_ready"], 1)
                elif step == 'turn_y':
                    act.wait_ge(sem[f"y_turned_{arg}"], 1)
                    g = MIX_Y[arg]
                    kw = dict(scale=cols_a[:, GAIN[arg]:GAIN[arg] + 1]) if arg in 'mr' else {}
                    act.activation(buf_x[:, g * 1024:(g + 1) * 1024], M[:, 0:1024], ACT.Copy,
                            **kw).then_inc(sem[f"yT_ready_{arg}"], 1)

            junk = Z[:, 6144:7168].rearrange("p (a d) -> p a d", a=TT)
            for n in range(D // 512):
                act.wait_ge(sem["x1_ready"], n + 1)
                if n > 0:
                    act.wait_ge(sem["x1_squared"], n)
                for tt in range(TT):
                    ins = act.activation(junk[:, tt, :], x1[:, tt, 512 * n:512 * n + 512], ACT.Square,
                                         accum_out=ssp[:, 4 * tt + n:4 * tt + n + 1])
                ins.then_inc(sem["x1_squared"], 1)
                act.wait_ge(sem["xT_turned2"], n + 1)
                for k in range(4):
                    kk = 4 * n + k
                    ins = act.activation(h2T[:, kk, :], M[:, k * T:k * T + T], ACT.Copy,
                                         scale=gsc[:, KT + kk:KT + kk + 1])
                ins.then_inc(sem["xT_copied2"], 1)
            act.wait_ge(sem["x1_rstd"], 1)
            act.activation(xs[:, 0, :], x1[:, 0, :], ACT.Copy, scale=rsx[:, 0:1])
            act.activation(xs[:, 1, :], x1[:, 1, :], ACT.Copy, scale=rsx[:, 1:2]).then_inc(sem["xhat_ready2"], 1)
            act.wait_ge(sem["group_arg"], 1)
            act.activation(rt[:, 8:16], rt[:, 8:16], ACT.Exp).then_inc(sem["group_exp"], 1)
            act.wait_ge(sem["pair_arg"], 1)
            act.activation(rt[:, 24:26], rt[:, 24:26], ACT.Exp).then_inc(sem["pair_exp"], 1)

            def dress_tokens():
                for k in range(8):
                    ins = act.activation(XT[:, k, :], W[:, k * P:k * P + P], ACT.Identity,
                                         scale=gsc[:, KT + k:KT + k + 1],
                                         bias=modc[:, 3 * KT + k:3 * KT + k + 1])
                ins.then_inc(sem["xt_act"], 1)

            act.wait_ge(sem["gathered"], 1)
            dress_tokens()
            rounds = load_rounds(act)
            with act.Fori(0, rounds) as r:
                with act.Fori(0, NE // 4) as g:
                    it = 8 * r + g
                    for q in range(4):
                        act.wait_ge(half_used, PER_GROUP * it + (PE_BASE + 6 * q + 4))
                        act.activation(ee, M[:, 0:128], ACT.Tanh, scale=0.5).then_inc(sem["e_ready"], 1)
                        if q == 0:
                            act.wait_ge(sem["g_turned"], it + 1)
                            act.activation(GT, M[:, 1024:1280], ACT.Copy).then_inc(sem["gt_ready"], 1)
                        act.wait_ge(sem["hh_turned"], 4 * it + q + 1)
                        act.activation(hTs, M[:, 1024:1152], ACT.Copy).then_inc(sem["hT_ready"], 1)
                        if q == 3:
                            act.wait_ge(sem["gathered"], 2 * it + 3)
                            dress_tokens()
                        act.wait_ge(half_used, PER_GROUP * it + (PE_BASE + 6 * q + 6))
                        for m in range(4):
                            ins = act.activation(ysb[32 * q:32 * q + 32, 512 * m:512 * m + 512],
                                                 A[32 * m:32 * m + 32, :], ACT.Copy)
                        ins.then_inc(sem["y_copied"], 1)

        @block.vector
        def _(dve):
            chain = [0]

            def step_no():
                chain[0] += 1
                return chain[0]

            def tt_op(o, x, y, op):
                return dve.tensor_tensor(o, x, y, op)

            def mean_eps(dst, src, n):
                return dve.tensor_scalar(dst, src, 1.0 / n, EPS, ALU.mult, ALU.add)

            def half_one_plus(v):
                dve.tensor_scalar(v, v, 0.5, 0.5, ALU.mult, ALU.add).then_inc(sem["dve_step"], 1)
                dve.wait_ge(sem["dve_step"], step_no())

            def bc(v, n):
                return v.unsqueeze(2).to_broadcast([v.shape[0], v.shape[1], n])

            dve.wait_ge(sem["c_tanh"], 1)
            half_one_plus(cs[:, 0:16])
            tt_op(cs[:, 16:32], cs[:, 0:16], cols_a[:, CA_C:CA_C + 16], ALU.mult).then_inc(sem["dve_step"], 1)
            dve.wait_ge(sem["dve_step"], step_no())
            dve.tensor_copy(csil[:].rearrange("p (k j) -> p k j", j=32), bc(cs[:, 16:32],
                    32)).then_inc(sem["csil_ready"], 1)
            dve.wait_ge(sem["x_squared"], 1)
            mean_eps(rsx, ssx, D).then_inc(sem["x_ms"], 1)
            dve.wait_ge(sem["x_rstd"], 1)
            dve.tensor_scalar(xs[:, 0, :], xs[:, 0, :], rsx[:, 0:1], None, ALU.mult)
            dve.tensor_scalar(xs[:, 1, :], xs[:, 1, :], rsx[:, 1:2], None, ALU.mult).then_inc(sem["xhat_ready1"], 1)

            dve.wait_ge(sem["cols_ready"], 1)
            for q in ('b_q', 'n_q'):
                g = cols_a[:, GAIN[q]:GAIN[q] + 1]
                ins = dve.tensor_scalar(g, g, QSCALE, None, ALU.mult)
            ins.then_inc(sem["gains_ready"], 1)

            def ada_finish(n):
                part, c = ADA[n] // 4, ADA[n] % 4
                dve.wait_ge(sem["ada_summed"], n + 1)
                if part in (2, 5):
                    gv = (g1b if part == 2 else g2b)[:, 512 * c:512 * c + 512]
                    dve.wait_ge(sem["late_loaded"], 48)
                    tt_op(gv, A[:], gv, ALU.add).then_inc(sem["ada_combined"], 1)
                    return
                o = {1: 0, 0: KT, 4: 2 * KT, 3: 3 * KT}[part] + 4 * c
                tt_op(modc[:, o:o + 4], A[:, 0:4], cols_b[:,
                        16 * part + 4 * c:16 * part + 4 * c + 4], ALU.add).then_inc(sem["ada_combined"], 1)
                if part in (0, 3):
                    sub = int(part == 3)
                    dve.wait_ge(sem["ada_combined"], n + 1)
                    dve.scalar_tensor_tensor(gsc[:, KT * sub + 4 * c:KT * sub + 4 * c + 4],
                                             modc[:, 2 * KT * sub + 4 * c:2 * KT * sub + 4 * c + 4], 1.0,
                                             cols_a[:, CA_N1 + 16 * sub + 4 * c:CA_N1 + 16 * sub + 4 * c + 4],
                                             ALU.add, ALU.mult).then_inc(sem["dve_step"], 1)
                    dve.wait_ge(sem["dve_step"], step_no())
                if part == 0:
                    dve.wait_ge(sem["xT_copied1"], c + 1)
                    for k in range(4 * c, 4 * c + 4):
                        ins = dve.tensor_scalar(hT[:, k, :], hT[:, k, :], gsc[:, k:k + 1],
                                                modc[:, KT + k:KT + k + 1], ALU.mult, ALU.add)
                    ins.then_inc(sem["h_ready"], 1)

            for n in range(len(ADA_FIRST)):
                ada_finish(n)

            def ada_accumulate(n):
                for hf in range(2):
                    i = STREAM.index(('ada', n, hf))
                    dve.wait_ge(slot_full[i % RING], 16 * (i // RING + 1))
                    for k in range(8):
                        w = ring[i % RING][:, 512 * k:512 * k + 512]
                        kk = 16 + 8 * hf + k
                        if kk == 16:
                            ins = dve.tensor_scalar(ada_s[:], w, cs[:, kk:kk + 1], None, ALU.mult)
                        else:
                            ins = dve.scalar_tensor_tensor(ada_s[:], w, cs[:, kk:kk + 1], ada_s[:], ALU.mult, ALU.add)
                        if k < 7:
                            ins.then_inc(sem["dve_step"], 1)
                            dve.wait_ge(sem["dve_step"], step_no())
                    ins.then_inc(sem["ada_half_used"], 1)
                    dve.wait_ge(sem["ada_half_used"], 2 * (n - len(ADA_FIRST)) + hf + 1)

            def out_norm(who, hs):
                tt_op(tmp[:, 0:1024], hs, hs, ALU.mult).then_inc(sem["dve_step"], 1)
                dve.wait_ge(sem["dve_step"], step_no())
                dve.tensor_reduce(ssy, tth(tmp[:, 0:1024]), AX, ALU.add).then_inc(sem["dve_step"], 1)
                dve.wait_ge(sem["dve_step"], step_no())
                mean_eps(rsy, ssy, DH).then_inc(sem[f"y_{who}_ms"], 1)
                dve.wait_ge(sem[f"gate_tanh_{who}"], 1)
                gv = zslot['m_o'] if who == 'm' else PA[:, 0:1024]
                half_one_plus(gv)
                if who == 'r':
                    tt_op(gv, gv, zslot['r_g'], ALU.mult).then_inc(sem["dve_step"], 1)
                    dve.wait_ge(sem["dve_step"], step_no())
                dve.wait_ge(sem[f"y_{who}_rstd"], 1)
                tt_op(tth(hs), tth(hs), bc(rsy, DH), ALU.mult).then_inc(sem["dve_step"], 1)
                dve.wait_ge(sem["dve_step"], step_no())
                tt_op(yb[:], hs, gv, ALU.mult).then_inc(sem[f"y_ready_{who}"], 1)

            sgv = sgn[:].rearrange("p (a n) -> p a n", a=TT)
            n_att = 0
            for step, arg in ORDER:
                if step == 'ada':
                    ada_accumulate(arg)
                elif step == 'ada_sum':
                    ada_finish(arg)
                elif step == 'extras':
                    dve.wait_ge(sem["extras_done"], 1)
                    dve.tensor_copy(zx[:].rearrange("p (a n) -> p a n", a=TT),
                                    M[:, 0:1024].rearrange("p (a n) -> p a n", a=TT)[:, :,
                                            0:NX]).then_inc(sem["zx_ready"], 1)
                elif step == 'gates':
                    dve.wait_ge(sem["gates_turned"], 1)
                    dve.wait_ge(sem["misc_loaded"], 16 * 5)
                    ip, fp, fa, zeros = (PA[0:H, i * T:(i + 1) * T] for i in range(4))
                    dve.memset(zeros, 0.0).then_inc(sem["dve_step"], 1)
                    dve.wait_ge(sem["dve_step"], step_no())
                    dve.tensor_scalar(ip, M[0:H, 0:T], gb[0:H, 0:1], None, ALU.add)
                    dve.tensor_scalar(fp, M[0:H, T:2 * T], gb[0:H, 1:2], None, ALU.add).then_inc(sem["gates_read"], 1)
                    dve.wait_ge(sem["gates_read"], 1)
                    dve.scalar_tensor_tensor(fa, fp, -1.0, fp, ALU.mult, ALU.min).then_inc(sem["f_abs"], 1)
                    dve.wait_ge(sem["n_gate_tanh"], 1)
                    dve.tensor_scalar(sgn[:], exc, 0.5, 0.5, ALU.mult, ALU.add).then_inc(sem["dve_step"], 1)
                    dve.wait_ge(sem["dve_step"], step_no())
                    dve.wait_ge(sem["f_exp"], 1)
                    dve.tensor_scalar(fa, fa, 1.0, None, ALU.add).then_inc(sem["f_one"], 1)
                    dve.wait_ge(sem["f_ln"], 1)
                    dve.scalar_tensor_tensor(fa, fp, 0.0, fa, ALU.min, ALU.subtract).then_inc(sem["dve_step"], 1)
                    dve.wait_ge(sem["dve_step"], step_no())
                    dve.tensor_tensor_scan(fp, fa, zeros, 0.0, ALU.add, ALU.add).then_inc(sem["dve_step"], 1)
                    dve.wait_ge(sem["dve_step"], step_no())
                    b_row = gat[0:H, 0:T]
                    tt_op(b_row, ip, fp, ALU.subtract).then_inc(sem["dve_step"], 1)
                    dve.wait_ge(sem["dve_step"], step_no())
                    dve.tensor_tensor_scan(fa, b_row, b_row, 0.0, ALU.max, ALU.max).then_inc(sem["dve_step"], 1)
                    dve.wait_ge(sem["dve_step"], step_no())
                    dve.scalar_tensor_tensor(gat[0:H, T:2 * T], fa, -1.0, fp, ALU.mult,
                            ALU.subtract).then_inc(sem["dve_step"], 1)
                    dve.wait_ge(sem["dve_step"], step_no())
                    dve.tensor_scalar(gat[0:H, T:2 * T], gat[0:H, T:2 * T], 87.0, None, ALU.min)
                    dve.tensor_scalar(gat[0:H, 2 * T:3 * T], fa, -1.0, None,
                            ALU.mult).then_inc(sem["gate_rows_ready"], 1)
                elif step == 'cmp_hid':
                    for w in range(2):
                        dve.wait_ge(sem["chunk_copied"], chunk_no(('n_kc', 'n_vc')[w]))
                        src = zslot[('n_kc', 'n_vc')[w]].rearrange("p (h n l) -> p l h n", h=H, l=16)
                        dst = blk[w].rearrange("p (l h n) -> p l h n", l=CMP_LEN, h=H)
                        for lh in range(2):
                            pe_c = cols_c[:, 32 * w + 16 * lh:32 * w + 16 * lh + 16].unsqueeze(2).unsqueeze(3)
                            ins = tt_op(dst[:, 16 * lh:16 * lh + 16], src[:, :, :, lh:lh + N_CMP],
                                        pe_c.to_broadcast([P, 16, H, N_CMP]), ALU.add)
                        ins.then_inc(sem["blocks_ready"], 1)
                    item_done(dve, 'cmp', 0)
                    dve.tensor_copy(hid[:].rearrange("p (w n) -> p w n", w=2),
                                    M[:, 0:1024].rearrange("p (w n) -> p w n", w=2)[:, :,
                                            0:60]).then_inc(sem["dve_step"], 1)
                    dve.wait_ge(sem["dve_step"], step_no())
                    u, v = tmp[:, 0:120], tmp[:, 128:248]
                    tt_op(v, hid[:], hid[:], ALU.mult).then_inc(sem["dve_step"], 1)
                    dve.wait_ge(sem["dve_step"], step_no())
                    dve.tensor_scalar(v, v, 0.044715, 1.0, ALU.mult, ALU.add).then_inc(sem["dve_step"], 1)
                    dve.wait_ge(sem["dve_step"], step_no())
                    tt_op(u, v, hid[:], ALU.mult).then_inc(sem["gelu_arg"], 1)
                    dve.wait_ge(sem["gelu_tanh"], 1)
                    half_one_plus(u)
                    tt_op(hid[:], hid[:], u, ALU.mult).then_inc(sem["hid_ready"], 1)
                    dve.wait_ge(sem["hid_ready"], 1)
                elif step == 'cmp_out':
                    kc, sq = tmp[0:60, 1024:1152], tmp[0:60, 1152:1280]
                    dve.wait_ge(sem["cmp_projected"], 1)
                    dve.tensor_copy(kc, M[0:60, 0:DH]).then_inc(sem["kc_read"], 1)
                    dve.wait_ge(sem["kc_read"], 1)
                    tt_op(sq, kc, kc, ALU.mult).then_inc(sem["dve_step"], 1)
                    dve.wait_ge(sem["dve_step"], step_no())
                    dve.tensor_reduce(ssc[0:60, :], sq, AX, ALU.add).then_inc(sem["dve_step"], 1)
                    dve.wait_ge(sem["dve_step"], step_no())
                    mean_eps(rsc[0:60, :], ssc[0:60, :], DH).then_inc(sem["kc_ms"], 1)
                    dve.wait_ge(sem["kc_rstd"], 1)
                    dve.tensor_scalar(kc, kc, rsc[0:60, :], None, ALU.mult).then_inc(sem["kc_normed"], 1)
                elif step == 'cmp_scores':
                    s = PA[:, 0:120]
                    s3 = s.rearrange("p (a n) -> p a n", n=N_CMP)
                    dve.wait_ge(sem["cmp_scores_done"], 1)
                    tt_op(s, M[:, 0:120], const('cmp_bias'), ALU.add).then_inc(sem["cmp_scores_read"], 1)
                    dve.wait_ge(sem["cmp_scores_read"], 1)
                    dve.tensor_reduce(cmx, s3, AX, ALU.max).then_inc(sem["dve_step"], 1)
                    dve.wait_ge(sem["dve_step"], step_no())
                    tt_op(s3, s3, bc(cmx, N_CMP), ALU.subtract).then_inc(sem["cmp_arg"], 1)
                    dve.wait_ge(sem["cmp_e"], 1)
                    tt_op(s, s, const('cmp_ok'), ALU.mult).then_inc(sem["cmp_exp"], 1)
                    dve.wait_ge(sem["cmp_exp"], 1)
                    dve.tensor_reduce(csum, s3, AX, ALU.add).then_inc(sem["dve_step"], 1)
                    dve.wait_ge(sem["dve_step"], step_no())
                    dve.tensor_scalar(csum, csum, 1e-30, None, ALU.max).then_inc(sem["dve_step"], 1)
                    dve.wait_ge(sem["dve_step"], step_no())
                    dve.reciprocal(cf, csum).then_inc(sem["dve_step"], 1)
                    dve.wait_ge(sem["dve_step"], step_no())
                    cf2 = cf.rearrange("p (a h) -> p a h", a=TT)
                    tt_op(cf2, cf2, sgv[:, :, 0:H], ALU.mult).then_inc(sem["dve_step"], 1)
                    dve.wait_ge(sem["dve_step"], step_no())
                elif step == 'cmp_pv':
                    dve.wait_ge(sem["cmp_pv_done"], 1)
                    tt_op(tth(yb[:]), tth(M[:, 0:1024]), bc(cf, DH), ALU.mult).then_inc(sem["cmp_y"], 1)
                elif step == 'norm':
                    z = zslot[arg]
                    dve.wait_ge(sem["chunk_copied"], chunk_no(arg))
                    tt_op(tmp[:, 0:1024], z, z, ALU.mult).then_inc(sem["dve_step"], 1)
                    dve.wait_ge(sem["dve_step"], step_no())
                    dve.tensor_reduce(ss, tth(tmp[:, 0:1024]), AX, ALU.add).then_inc(sem["dve_step"], 1)
                    dve.wait_ge(sem["dve_step"], step_no())
                    mean_eps(rst, ss, DH).then_inc(sem[f"norm_{arg}_ms"], 1)
                    dve.wait_ge(sem[f"norm_{arg}_rstd"], 1)
                    tt_op(tth(z), tth(z), bc(rst, DH), ALU.mult).then_inc(sem["normed"], 1)
                elif step == 'scores':
                    n_att += 1
                    al = alibi[:, int(arg != 'moba')]
                    dve.wait_ge(sem["late_loaded"], 48)
                    dve.wait_ge(sem["scores_done"], n_att)
                    tt_op(heads(PA[:, 0:1024]), heads(M[:, 0:1024]), al, ALU.add).then_inc(sem["dve_step"], 1)
                    dve.wait_ge(sem["dve_step"], step_no())
                    tt_op(heads(PA[:, 1024:1536]), heads(M[:, 1024:1536]), al[:, :, P:T],
                            ALU.add).then_inc(sem["scores_read"], 1)
                    dve.tensor_reduce(mx[:, 4:8], heads(PA[:, 0:1024]), AX, ALU.max).then_inc(sem["dve_step"], 1)
                    dve.wait_ge(sem["dve_step"], step_no())
                    dve.wait_ge(sem["scores_read"], n_att)
                    dve.tensor_reduce(mx[:, 0:4], heads(PA[:, 1024:1536]), AX, ALU.max).then_inc(sem["dve_step"], 1)
                    dve.wait_ge(sem["dve_step"], step_no())
                    dve.tensor_scalar(nmx, mx, -1.0, None, ALU.mult).then_inc(sem["nmax_ready"], 1)
                elif step == 'pv':
                    dve.wait_ge(sem["exp_done"], n_att)
                    dve.reciprocal(fac, lsum).then_inc(sem["dve_step"], 1)
                    dve.wait_ge(sem["dve_step"], step_no())
                    if arg != 'moba':
                        br = {'slc': 1, 'win': 2}[arg]
                        f2 = fac.rearrange("p (a h) -> p a h", a=TT)
                        tt_op(f2, f2, sgv[:, :, br * H:br * H + H], ALU.mult).then_inc(sem["dve_step"], 1)
                        dve.wait_ge(sem["dve_step"], step_no())
                    dve.wait_ge(sem["o_done"], n_att)
                    if arg == 'moba':
                        tt_op(tth(yb[:]), tth(M[:, 0:1024]), bc(fac, DH), ALU.mult).then_inc(sem["y_ready_b"], 1)
                    else:
                        tt_op(tth(tmp[:, 0:1024]), tth(M[:, 0:1024]), bc(fac, DH),
                                ALU.mult).then_inc(sem["o_read"], 1)
                        dve.wait_ge(sem["o_read"], n_att)
                        ins = tt_op(yb[:], yb[:], tmp[:, 0:1024], ALU.add)
                        if arg == 'win':
                            ins.then_inc(sem["y_ready_n"], 1)
                            dve.tensor_copy(hsel[0:H, :].rearrange("p (h t) -> p h t", h=H),
                                            bc(ident[0:H, 0:H], P)).then_inc(sem["hsel_ready"], 1)
                        else:
                            ins.then_inc(sem["dve_step"], 1)
                            dve.wait_ge(sem["dve_step"], step_no())
                elif step == 'conv':
                    w = int(arg == 'm_k')
                    acc, pd = heads(tslot[arg]), padv[:, w]
                    if w == 0:
                        item_done(dve, 'cmp', 0)
                        dve.memset(padv[:, :, :, 0:3].rearrange("p w h t -> p (w h) t"),
                                0.0).then_inc(sem["dve_step"], 1)
                        dve.wait_ge(sem["dve_step"], step_no())
                    dve.wait_ge(sem["chunk_copied"], chunk_no(arg))
                    for j in (3, 2, 1, 0):
                        for h in range(H):
                            o = CA_CONV + 8 * j + 4 * w + h
                            cw = cols_a[:, o:o + 1]
                            if j == 3:
                                ins = dve.tensor_scalar(acc[:, h], pd[:, h, 3:3 + T], cw, None, ALU.mult)
                            else:
                                ins = dve.scalar_tensor_tensor(acc[:, h], pd[:, h, j:j + T], cw, acc[:, h],
                                                               ALU.mult, ALU.add)
                            if (j, h) != (0, H - 1) and h == H - 1:
                                ins.then_inc(sem["dve_step"], 1)
                                dve.wait_ge(sem["dve_step"], step_no())
                    ins.then_inc(sem["conv_sum"], 1)
                    dve.wait_ge(sem["conv_tanh"], w + 1)
                    e = tmp[:, 1024:2048]
                    half_one_plus(e)
                    dve.scalar_tensor_tensor(tslot[arg], tslot[arg], 1.0 if w else QSCALE, e,
                                             ALU.mult, ALU.mult).then_inc(sem["conv_done"], 1)
                elif step == 'm_decay':
                    dve.wait_ge(sem["m_cols_turned"], 1)
                    dve.tensor_copy(bcol_enm, M[:, 0:16]).then_inc(sem["m_cols_read"], 1)
                    dve.wait_ge(sem["m_cols_read"], 1)
                    dve.wait_ge(sem["negmask_loaded"], 16)
                    nm = negmask
                    for h in range(H):
                        o = 512 + h * T
                        dve.scalar_tensor_tensor(PA[:, h * T:h * T + T], M[:, o:o + T], bcol[:, h:h + 1], nm,
                                                 ALU.add, ALU.add)
                        ins = dve.scalar_tensor_tensor(PA[:, 1024 + h * P:1024 + h * P + P], M[:, o + P:o + T],
                                                       bcol[:, 4 + h:5 + h], nm[:, 0:P], ALU.add, ALU.add)
                    ins.then_inc(sem["m_args_ready"], 1)
                elif step == 'm_scores':
                    dve.wait_ge(sem["m_decay_ready"], 1)
                    dve.wait_ge(sem["m_scores_done"], 1)
                    tt_op(PB[:], M[:], PA[:], ALU.mult).then_inc(sem["m_p_ready"], 1)
                elif step == 'm_pv':
                    dve.wait_ge(sem["enm_ready"], 1)
                    dve.wait_ge(sem["m_pv_done"], 1)
                    dve.tensor_copy(den, M[:, 1024:1032]).then_inc(sem["dve_step"], 1)
                    dve.wait_ge(sem["dve_step"], step_no())
                    dve.scalar_tensor_tensor(den, den, -1.0, den, ALU.mult, ALU.max).then_inc(sem["dve_step"], 1)
                    dve.wait_ge(sem["dve_step"], step_no())
                    tt_op(den, den, enm, ALU.max).then_inc(sem["dve_step"], 1)
                    dve.wait_ge(sem["dve_step"], step_no())
                    dve.reciprocal(den, den).then_inc(sem["dve_step"], 1)
                    dve.wait_ge(sem["dve_step"], step_no())
                    hs = tmp[:, 1024:2048]
                    tt_op(tth(hs), tth(M[:, 0:1024]), bc(den, DH), ALU.mult).then_inc(sem["m_o_read"], 1)
                    dve.wait_ge(sem["m_o_read"], 1)
                    out_norm('m', hs)
                elif step == 'r_scores':
                    dve.wait_ge(sem["decay_loaded"], 16)
                    dve.wait_ge(sem["r_scores_done"], 1)
                    dve.tensor_tensor(heads(PB[:, 0:1024]), heads(M[:, 0:1024]), decay, ALU.mult)
                    tt_op(heads(PB[:, 1024:1536]), heads(M[:, 1024:1536]), decay[:, :, 0:P],
                            ALU.mult).then_inc(sem["r_p_ready"], 1)
                elif step == 'r_pv':
                    dve.wait_ge(sem["r_pv_done"], 1)
                    hs = tmp[:, 1024:2048]
                    dve.tensor_copy(hs, M[:, 0:1024]).then_inc(sem["r_o_read"], 1)
                    dve.wait_ge(sem["r_o_read"], 1)
                    out_norm('r', hs)

            dve.wait_ge(sem["router_loaded"], 64)
            dve.wait_ge(sem["y_ready_r"], 1)
            tt_op(PA[:, 0:KT * 36].rearrange("p (k n) -> p k n", k=KT), wr.rearrange("p (k n) -> p k n", k=KT),
                  bc(modc[:, 3 * KT:4 * KT], 36), ALU.mult).then_inc(sem["dve_step"], 1)
            dve.wait_ge(sem["dve_step"], step_no())
            dve.tensor_reduce(s36, PA[:, 0:KT * 36].rearrange("p (k n) -> p n k", k=KT), AX,
                              ALU.add).then_inc(sem["shift_products"], 1)

            dve.wait_ge(sem["x_again"], 16)
            for n in range(D // 512):
                item_done(dve, 'wout', n)
                if n > 0:
                    dve.wait_ge(sem["x1_ready"], n)
                o = (n % 2) * 1024
                t3 = tmp[:, 0:1024].rearrange("p (a d) -> p a d", a=TT)
                tt_op(t3, W[:, o:o + 1024].rearrange("p (a d) -> p a d", a=TT),
                      g1b[:, 512 * n:512 * n + 512].unsqueeze(1).to_broadcast([P, TT, 512]),
                              ALU.mult).then_inc(sem["dve_step"], 1)
                dve.wait_ge(sem["dve_step"], step_no())
                xo = x1[:, :, 512 * n:512 * n + 512]
                tt_op(xo, xo, t3, ALU.add).then_inc(sem["x1_ready"], 1)
                if n == 0:
                    dve.wait_ge(sem["shift_logits"], 1)
                    tt_op(rb[:], M[:, 1024:1060], rb[:], ALU.add).then_inc(sem["shift_read"], 1)
            dve.wait_ge(sem["x1_squared"], 4)
            dve.tensor_reduce(ssx, ssp.rearrange("p (a n) -> p a n", a=TT), AX, ALU.add).then_inc(sem["dve_step"], 1)
            dve.wait_ge(sem["dve_step"], step_no())
            mean_eps(rsx, ssx, D).then_inc(sem["x1_ms"], 1)

            L = lg.rearrange("p (a n) -> p a n", a=TT)
            Lg, Le = L[:, :, 0:NG], L[:, :, NG:36].rearrange("p a (g j) -> p a g j", g=NG)
            dve.tensor_scalar(jdesc, const('iota'), -1.0, 32.0, ALU.mult, ALU.add)
            dve.wait_ge(sem["x1_rstd"], 1)
            dve.wait_ge(sem["router_done"], 1)
            dve.scalar_tensor_tensor(L[:, 0, :], M[:, 1024:1060], rsx[:, 0:1], rb[:], ALU.mult, ALU.add)
            dve.scalar_tensor_tensor(L[:, 1, :], A[:, 0:36], rsx[:, 1:2], rb[:], ALU.mult, ALU.add).then_inc(
                sem["dve_step"], 1)
            dve.wait_ge(sem["dve_step"], step_no())

            def first_maximum(dst, vals, top, n):
                t = tie[:, 0:TT * n].rearrange("p (a n) -> p a n", a=TT)
                dve.tensor_reduce(top, vals, AX, ALU.max).then_inc(sem["dve_step"], 1)
                dve.wait_ge(sem["dve_step"], step_no())
                tt_op(dst, vals, bc(top, n), ALU.is_equal).then_inc(sem["dve_step"], 1)
                dve.wait_ge(sem["dve_step"], step_no())
                tt_op(t, dst, jdesc[:, 0:n].unsqueeze(1).to_broadcast([P, TT, n]),
                        ALU.mult).then_inc(sem["dve_step"], 1)
                dve.wait_ge(sem["dve_step"], step_no())
                dve.tensor_reduce(rt[:, 38:40], t, AX, ALU.max).then_inc(sem["dve_step"], 1)
                dve.wait_ge(sem["dve_step"], step_no())
                tt_op(dst, t, bc(rt[:, 38:40], n), ALU.is_equal).then_inc(sem["dve_step"], 1)
                dve.wait_ge(sem["dve_step"], step_no())

            og = ohg[:, 0:TT * NG].rearrange("p (a n) -> p a n", a=TT)
            first_maximum(og, Lg, rt[:, 0:2], NG)
            eg = rt[:, 8:16].rearrange("p (a n) -> p a n", a=TT)
            tt_op(eg, Lg, bc(rt[:, 0:2], NG), ALU.subtract).then_inc(sem["group_arg"], 1)
            mp = mprod.rearrange("p (a g j) -> p a g j", a=TT, g=NG)
            ogb = og.unsqueeze(3).to_broadcast([P, TT, NG, EPG])
            tt_op(mp, Le, ogb, ALU.mult).then_inc(sem["dve_step"], 1)
            dve.wait_ge(sem["dve_step"], step_no())
            lev = le_g[:, 0:16].rearrange("p (a j) -> p a j", a=TT)
            dve.tensor_reduce(lev, mp.rearrange("p a g j -> p a j g"), AX, ALU.add).then_inc(sem["dve_step"], 1)
            dve.wait_ge(sem["dve_step"], step_no())
            o1, o2, l2 = (v[:, 0:16].rearrange("p (a j) -> p a j", a=TT) for v in (oh1, oh2, le2))
            first_maximum(o1, lev, rt[:, 2:4], EPG)
            dve.scalar_tensor_tensor(l2, o1, NEG, lev, ALU.mult, ALU.add).then_inc(sem["dve_step"], 1)
            dve.wait_ge(sem["dve_step"], step_no())
            first_maximum(o2, l2, rt[:, 4:6], EPG)
            tt_op(rt[:, 24:26], rt[:, 4:6], rt[:, 2:4], ALU.subtract).then_inc(sem["pair_arg"], 1)
            dve.wait_ge(sem["group_exp"], 1)
            dve.tensor_reduce(rt[:, 16:18], eg, AX, ALU.add).then_inc(sem["dve_step"], 1)
            dve.wait_ge(sem["dve_step"], step_no())
            dve.reciprocal(rt[:, 18:20], rt[:, 16:18]).then_inc(sem["dve_step"], 1)
            dve.wait_ge(sem["dve_step"], step_no())
            dve.wait_ge(sem["pair_exp"], 1)
            dve.tensor_scalar(rt[:, 26:28], rt[:, 24:26], 1.0, None, ALU.add).then_inc(sem["dve_step"], 1)
            dve.wait_ge(sem["dve_step"], step_no())
            dve.reciprocal(rt[:, 28:30], rt[:, 26:28]).then_inc(sem["dve_step"], 1)
            dve.wait_ge(sem["dve_step"], step_no())
            tt_op(rt[:, 30:32], rt[:, 28:30], rt[:, 18:20], ALU.mult).then_inc(sem["dve_step"], 1)
            dve.wait_ge(sem["dve_step"], step_no())
            tt_op(rt[:, 32:34], rt[:, 30:32], rt[:, 24:26], ALU.mult).then_inc(sem["dve_step"], 1)
            dve.wait_ge(sem["dve_step"], step_no())
            both = w12.rearrange("p (a j) -> p a j", a=TT)
            tt_op(lev, o1, bc(rt[:, 30:32], EPG), ALU.mult).then_inc(sem["dve_step"], 1)
            dve.wait_ge(sem["dve_step"], step_no())
            tt_op(l2, o2, bc(rt[:, 32:34], EPG), ALU.mult).then_inc(sem["dve_step"], 1)
            dve.wait_ge(sem["dve_step"], step_no())
            tt_op(lev, lev, l2, ALU.add).then_inc(sem["dve_step"], 1)
            dve.wait_ge(sem["dve_step"], step_no())
            tt_op(both, o1, o2, ALU.add).then_inc(sem["dve_step"], 1)
            dve.wait_ge(sem["dve_step"], step_no())
            shp = [P, TT, NG, EPG]
            pos3 = pos.rearrange("p (a n) -> p a n", a=TT)
            gate3 = gate.rearrange("p (a n) -> p a n", a=TT)
            tt_op(gate3[:, :, 0:NE].rearrange("p a (g j) -> p a g j", g=NG), ogb, lev.unsqueeze(2).to_broadcast(shp),
                  ALU.mult).then_inc(sem["dve_step"], 1)
            dve.wait_ge(sem["dve_step"], step_no())
            tt_op(mask.rearrange("p (a g j) -> p a g j", a=TT, g=NG), ogb, both.unsqueeze(2).to_broadcast(shp),
                  ALU.mult).then_inc(sem["mask_ready"], 1)
            dve.wait_ge(sem["places_done"], 1)
            tt_op(pos3[:, :, 0:NE], M[:, 0:1024].rearrange("p (a n) -> p a n", a=TT)[:, :, 0:NE],
                  mask.rearrange("p (a n) -> p a n", a=TT), ALU.mult).then_inc(sem["dve_step"], 1)
            dve.wait_ge(sem["dve_step"], step_no())
            dve.tensor_scalar(pos3[:, :, NE:NE + 4], pos3[:, :, 0:4], -33.0, None, ALU.add)
            dve.tensor_copy(gate3[:, :, NE:NE + 4], gate3[:, :, 0:4]).then_inc(sem["dve_step"], 1)
            dve.wait_ge(sem["dve_step"], step_no())
            dve.tensor_scalar(pos3[:, :, 0:NE], pos3[:, :, 0:NE], -1.0, None, ALU.add).then_inc(sem["dve_step"], 1)
            dve.wait_ge(sem["dve_step"], step_no())
            iob = const('iota').unsqueeze(1).unsqueeze(1).to_broadcast([P, TT, 4, 32])

            def column(v, g):
                return v[:, :, bass.ds(4 * g, 4)].unsqueeze(3).to_broadcast([P, TT, 4, 32])

            def dress_tokens():
                for k in range(8, KT):
                    ins = dve.tensor_scalar(XT[:, k, :], W[:, k * P:k * P + P], gsc[:, KT + k:KT + k + 1],
                                            modc[:, 3 * KT + k:3 * KT + k + 1], ALU.mult, ALU.add)
                ins.then_inc(sem["xt_dve"], 1)

            tt_op(Gm, column(pos3, 0), iob, ALU.is_equal).then_inc(sem["dve_step"], 1)
            dve.wait_ge(sem["dve_step"], step_no())
            tt_op(Gg, Gm, column(gate3, 0), ALU.mult).then_inc(sem["g_ready"], 1)
            dve.tensor_reduce(rt[:, 34:35], M[:, 1024:1024 + NE], AX, ALU.max).then_inc(sem["dve_step"], 1)
            dve.wait_ge(sem["dve_step"], step_no())
            dve.tensor_scalar(cnt_i[:], rt[:, 34:35], 31.0, None, ALU.add).then_inc(sem["dve_step"], 1)
            dve.wait_ge(sem["dve_step"], step_no())
            dve.tensor_scalar(cnt_i[:], cnt_i[:], 5, None, ALU.logical_shift_right).then_inc(sem["rounds_ready"], 1)
            dve.wait_ge(sem["gathered"], 2)
            dress_tokens()

            def add_scattered(n):
                for tt in range(TT):
                    dve.wait_ge(sem["scattered"], 2 * n + tt + 1)
                    dve.wait_ge(sem["y_added"], 2 * n + tt + 1)
                    tt_op(yacc[:, tt, :], W[:], yacc[:, tt, :], ALU.add).then_inc(sem["y_added"], 1)

            rounds = load_rounds(dve)
            LINKS = 1 + 4
            with dve.Fori(0, rounds) as r:
                with dve.Fori(0, NE // 4) as g:
                    it = 8 * r + g
                    count = [0]

                    def loop_step_no():
                        count[0] += 1
                        return LINKS * it + count[0]

                    for q in range(4):
                        dve.wait_ge(sem["e_ready"], 4 * it + q + 1)
                        dve.scalar_tensor_tensor(aa, ee, 1.0, M[:, 0:128], ALU.add, ALU.mult).then_inc(
                            sem["dve_loop_step"], 1)
                        dve.wait_ge(sem["dve_loop_step"], loop_step_no())
                        dve.scalar_tensor_tensor(hh, M[:, 512:640], 0.5, aa, ALU.mult, ALU.mult).then_inc(
                            sem["hh_ready"], 1)
                        if q == 0:
                            add_scattered(it)
                            dve.wait_ge(sem["g_turned"], it + 1)
                            tt_op(Gm, column(pos3, g + 1), iob, ALU.is_equal).then_inc(sem["dve_loop_step"], 1)
                            dve.wait_ge(sem["dve_loop_step"], loop_step_no())
                            tt_op(Gg, Gm, column(gate3, g + 1), ALU.mult).then_inc(sem["g_ready"], 1)
                        elif q == 3:
                            dve.wait_ge(sem["gathered"], 2 * it + 4)
                            dress_tokens()
                    assert count[0] == LINKS
                dve.tensor_scalar(pos, pos, -32.0, None, ALU.add).then_inc(sem["round_shifted"], 1)
                dve.wait_ge(sem["round_shifted"], r + 1)
            for tt in range(TT):
                tt_op(yacc[:, tt, :], yacc[:, tt, :], g2b[:], ALU.mult).then_inc(sem["dve_step"], 1)
                dve.wait_ge(sem["dve_step"], step_no())
                tt_op(yacc[:, tt, :], yacc[:, tt, :], x1[:, tt, :], ALU.add).then_inc(sem["dve_step"], 1)
                dve.wait_ge(sem["dve_step"], step_no())
            dve.wait_ge(sem["scattered"], 16 * rounds + 1)
            tt_op(xs[:, 0, :], W[:], g2b[:], ALU.mult).then_inc(sem["dve_step"], 1)
            dve.wait_ge(sem["dve_step"], step_no())
            tt_op(yacc[:, 0, :], yacc[:, 0, :], xs[:, 0, :], ALU.add).then_inc(sem["out_ready"], 1)
            dve.wait_ge(sem["scattered"], 16 * rounds + 2)
            tt_op(xs[:, 1, 0:1536], M[:], g2b[:, 0:1536], ALU.mult)
            tt_op(xs[:, 1, 1536:D], A[:], g2b[:, 1536:D], ALU.mult).then_inc(sem["dve_step"], 1)
            dve.wait_ge(sem["dve_step"], step_no())
            tt_op(yacc[:, 1, :], yacc[:, 1, :], xs[:, 1, :], ALU.add).then_inc(sem["out_ready"], 1)


INPUTS = ('x', 'c', 'norm1_g', 'norm2_g', 'ada_w', 'ada_b', 'w_in', 'mlstm_gate_b', 'mlstm_conv_w', 'mlstm_out_g',
          'moba_qk_g', 'ret_out_g', 'nsa_q_g', 'nsa_k_g', 'nsa_cmp_pos', 'nsa_cmp_w1', 'nsa_cmp_w2', 'w_out',
          'router_g_w', 'router_g_b', 'router_e_w', 'router_e_b', 'exp_w1', 'exp_w3', 'exp_w2')


def kernel(**inputs):
    import concourse.bacc as bacc
    from concourse.bass_utils import run_bass_kernel_spmd

    nc = bacc.Bacc("TRN2", target_bir_lowering=False, num_devices=1)
    arrays = {f"in_{n}": np.ascontiguousarray(inputs[n]) for n in INPUTS}
    arrays["in_consts"] = constants()
    aps = {n[3:]: nc.dram_tensor(n, v.shape, F32, kind="ExternalInput").ap() for n, v in arrays.items()}
    out = nc.dram_tensor("out", (1, T, D), F32, kind="ExternalOutput").ap()
    build_program(nc, aps, out)
    return run_bass_kernel_spmd(nc, [arrays], core_ids=[0]).results[0]["out"]
```
